# Optimizing a Trainium2 kernel written in Bass

```python
import math
import jax, jax.numpy as jnp
from jax import lax
import numpy as np

D_MODEL = 1024
BATCH = 1
SEQ = 512
DEPTH = 2
DEC_BATCH = 8
DEC_SEQ = 8
PAST_LEN = 256
PAGE_SIZE = 128

D_MIX = D_MODEL
D_A = D_MIX // 2
H_A = 8
DH_A = D_A // H_A
CHUNK = 128
D_B = D_MIX - D_A
H_B = 4
DV = D_B // H_B
DK = DV // 2
D_QK = H_B * 2 * DK
D_IN = 2 * D_A + 2 * D_QK + D_B
Q_BLOCK = 128
ATTN_SCALE = DK ** -0.5
NEG_INF = -1e30
N_GROUPS = 4
E_PER = 4
N_EXP = N_GROUPS * E_PER
TOP_K = 2
D_E = 256
EPS = 1e-6

kernel_name = "hymba_chunkmlp_diffattn_hmoe_step"

def rmsnorm(x, g):
    xf = x.astype(jnp.float32)
    y = xf * lax.rsqrt(jnp.mean(xf * xf, axis=-1, keepdims=True) + EPS)
    return y.astype(x.dtype) * g

def in_proj(x, g1, w_in, av_g, qn_g, kn_g):
    b, t, _ = x.shape
    z = rmsnorm(x, g1) @ w_in
    a = jax.nn.gelu(z[..., :2 * D_A])
    u = a[..., :D_A]
    va = rmsnorm(a[..., D_A:], av_g)
    q = z[..., 2 * D_A:2 * D_A + D_QK].reshape(b, t, H_B, 2, DK)
    k = z[..., 2 * D_A + D_QK:2 * D_A + 2 * D_QK].reshape(b, t, H_B, 2, DK)
    vb = z[..., 2 * D_A + 2 * D_QK:].reshape(b, t, H_B, DV)
    return u, va, rmsnorm(q, qn_g), rmsnorm(k, kn_g), vb

def masked_ws(ws):
    tril = jnp.tril(jnp.ones((CHUNK, CHUNK), dtype=bool))
    return jnp.where(tril[None], ws, jnp.zeros_like(ws))

def chunk_mix_prompt(va, ws_m, bs):
    b, t, _ = va.shape
    vc = va.reshape(b, t // CHUNK, CHUNK, H_A, DH_A)
    s = jnp.einsum('hts,bcshd->bcthd', ws_m, vc) + bs.T[None, None, :, :, None]
    return s.reshape(b, t, D_A)

def chunk_mix_sample(va, ws_m, bs):
    b, n, _ = va.shape
    vs = va.reshape(b, n, H_A, DH_A)
    s = jnp.einsum('hts,bshd->bthd', ws_m[:, :n, :n], vs) + bs[:, :n].T[None, :, :, None]
    return s.reshape(b, n, D_A)

def diff_lambda(lq1, lk1, lq2, lk2, lam_init):
    f = jnp.float32
    return (jnp.exp(jnp.sum(lq1.astype(f) * lk1.astype(f))) -
            jnp.exp(jnp.sum(lq2.astype(f) * lk2.astype(f))) + lam_init)

def diff_core(q, k, v, mask, lam):
    s = jnp.einsum('bqhmd,bkhmd->bhmqk', q, k).astype(jnp.float32) * ATTN_SCALE
    s = jnp.where(mask[None, None, None], s, NEG_INF)
    p = jax.nn.softmax(s, axis=-1)
    a = p[:, :, 0] - lam * p[:, :, 1]
    return jnp.einsum('bhqk,bkhd->bqhd', a.astype(v.dtype), v)

def attn_prompt(q, k, v, lam):
    b, t = q.shape[:2]
    kpos = jnp.arange(t)

    def blk(i):
        qs = lax.dynamic_slice_in_dim(q, i * Q_BLOCK, Q_BLOCK, axis=1)
        qpos = i * Q_BLOCK + jnp.arange(Q_BLOCK)
        return diff_core(qs, k, v, kpos[None, :] <= qpos[:, None], lam)

    o = lax.map(blk, jnp.arange(t // Q_BLOCK))
    return jnp.moveaxis(o, 0, 1).reshape(b, t, H_B, DV)

def attn_sample(q, k_new, v_new, k_past, v_past, lam):
    n = q.shape[1]
    past = k_past.shape[1]
    k_all = jnp.concatenate([k_past, k_new], axis=1)
    v_all = jnp.concatenate([v_past, v_new], axis=1)
    mask = jnp.concatenate([jnp.ones((n, past), dtype=bool),
                            jnp.tril(jnp.ones((n, n), dtype=bool))], axis=1)
    return diff_core(q, k_all, v_all, mask, lam)

def merge_out(u, s_a, o_b, on_g, lam_init, w_out):
    b, t, _ = u.shape
    a_out = u * s_a
    b_out = (rmsnorm(o_b, on_g) * (1.0 - lam_init)).reshape(b, t, D_B)
    return jnp.concatenate([a_out, b_out], axis=-1) @ w_out

def hier_moe(x, g2, r_g, r_e, w_gate, w_up, w_down):
    b, t, d = x.shape
    h = rmsnorm(x, g2).reshape(b * t, d)
    pg = jax.nn.softmax((h @ r_g).astype(jnp.float32), axis=-1)
    gi = jnp.argmax(pg, axis=-1)
    gw = jnp.max(pg, axis=-1)
    le = (h @ r_e).astype(jnp.float32).reshape(-1, N_GROUPS, E_PER)
    le_sel = jnp.take_along_axis(le, gi[:, None, None], axis=1)[:, 0]
    tw, ti = lax.top_k(jax.nn.softmax(le_sel, axis=-1), TOP_K)
    tw = tw / jnp.sum(tw, axis=-1, keepdims=True)
    eidx = gi[:, None] * E_PER + ti
    gates = jnp.sum(jax.nn.one_hot(eidx, N_EXP, dtype=jnp.float32) * (gw[:, None] * tw)[..., None], axis=1)
    hg = jnp.einsum('nd,edf->nef', h, w_gate)
    hu = jnp.einsum('nd,edf->nef', h, w_up)
    a = jax.nn.silu(hg) * hu * gates.astype(h.dtype)[..., None]
    return jnp.einsum('nef,efd->nd', a, w_down).reshape(b, t, d)

def setup_inputs(seed: int = 0) -> dict:
    key = jax.random.key(seed)
    ks = jax.random.split(key, 26)
    n_pages = PAST_LEN // PAGE_SIZE
    n_used = DEC_BATCH * n_pages
    n_pool = n_used + n_used // 4
    f = jnp.float32
    nrm = lambda k, shape, s: jax.random.normal(k, shape, f) * s
    gain = lambda k, shape: 1.0 + 0.02 * jax.random.normal(k, shape, f)
    page_table = jax.random.permutation(ks[4], n_pool)[:n_used].reshape(DEC_BATCH, n_pages).astype(jnp.int32)
    return {
        "x_prompt": nrm(ks[0], (BATCH, SEQ, D_MODEL), 1.0),
        "x_sample": nrm(ks[1], (DEC_BATCH, DEC_SEQ, D_MODEL), 1.0),
        "cache_k": nrm(ks[2], (DEPTH, n_pool, PAGE_SIZE, H_B, 2 * DK), 1.0),
        "cache_v": nrm(ks[3], (DEPTH, n_pool, PAGE_SIZE, H_B, DV), 1.0),
        "page_table": page_table,
        "norm1_g": gain(ks[5], (DEPTH, D_MODEL)),
        "w_in": nrm(ks[6], (DEPTH, D_MODEL, D_IN), D_MODEL ** -0.5),
        "a_vnorm_g": gain(ks[7], (DEPTH, D_A)),
        "a_ws": nrm(ks[8], (DEPTH, H_A, CHUNK, CHUNK), CHUNK ** -0.5),
        "a_bs": 1.0 + nrm(ks[9], (DEPTH, H_A, CHUNK), 0.02),
        "qn_g": gain(ks[10], (DEPTH, DK)),
        "kn_g": gain(ks[11], (DEPTH, DK)),
        "lam_q1": nrm(ks[12], (DEPTH, DK), 0.1),
        "lam_k1": nrm(ks[13], (DEPTH, DK), 0.1),
        "lam_q2": nrm(ks[14], (DEPTH, DK), 0.1),
        "lam_k2": nrm(ks[15], (DEPTH, DK), 0.1),
        "b_onorm_g": gain(ks[16], (DEPTH, DV)),
        "w_out": nrm(ks[17], (DEPTH, D_MIX, D_MODEL), D_MIX ** -0.5),
        "norm2_g": gain(ks[18], (DEPTH, D_MODEL)),
        "router_g": nrm(ks[19], (DEPTH, D_MODEL, N_GROUPS), D_MODEL ** -0.5),
        "router_e": nrm(ks[20], (DEPTH, D_MODEL, N_EXP), D_MODEL ** -0.5),
        "w_gate": nrm(ks[21], (DEPTH, N_EXP, D_MODEL, D_E), D_MODEL ** -0.5),
        "w_up": nrm(ks[22], (DEPTH, N_EXP, D_MODEL, D_E), D_MODEL ** -0.5),
        "w_down": nrm(ks[23], (DEPTH, N_EXP, D_E, D_MODEL), D_E ** -0.5),
    }

def reference(x_prompt, x_sample, cache_k, cache_v, page_table, norm1_g, w_in, a_vnorm_g, a_ws, a_bs,
              qn_g, kn_g, lam_q1, lam_k1, lam_q2, lam_k2, b_onorm_g, w_out, norm2_g,
              router_g, router_e, w_gate, w_up, w_down):
    xp, xs = x_prompt, x_sample
    db, n_new = xs.shape[:2]
    past_len = page_table.shape[1] * cache_k.shape[2]
    kp_rows, vp_rows, ks_rows, vs_rows, cv_rows = [], [], [], [], []
    for l in range(DEPTH):
        lam_init = 0.8 - 0.6 * math.exp(-0.3 * l)
        lam = diff_lambda(lam_q1[l], lam_k1[l], lam_q2[l], lam_k2[l], lam_init)
        ws_m = masked_ws(a_ws[l])
        u, va, q, k, vb = in_proj(xp, norm1_g[l], w_in[l], a_vnorm_g[l], qn_g[l], kn_g[l])
        s_a = chunk_mix_prompt(va, ws_m, a_bs[l])
        o_b = attn_prompt(q, k, vb, lam)
        xp = xp + merge_out(u, s_a, o_b, b_onorm_g[l], lam_init, w_out[l])
        xp = xp + hier_moe(xp, norm2_g[l], router_g[l], router_e[l], w_gate[l], w_up[l], w_down[l])
        kp_rows.append(k.reshape(k.shape[0], k.shape[1], H_B, 2 * DK))
        vp_rows.append(vb)
        u, va, q, k, vb = in_proj(xs, norm1_g[l], w_in[l], a_vnorm_g[l], qn_g[l], kn_g[l])
        s_a = chunk_mix_sample(va, ws_m, a_bs[l])
        k_past = cache_k[l][page_table].reshape(db, past_len, H_B, 2, DK)
        v_past = cache_v[l][page_table].reshape(db, past_len, H_B, DV)
        o_b = attn_sample(q, k, vb, k_past, v_past, lam)
        xs = xs + merge_out(u, s_a, o_b, b_onorm_g[l], lam_init, w_out[l])
        xs = xs + hier_moe(xs, norm2_g[l], router_g[l], router_e[l], w_gate[l], w_up[l], w_down[l])
        ks_rows.append(k.reshape(db, n_new, H_B, 2 * DK))
        vs_rows.append(vb)
        cv_rows.append(va)
    k_prompt = jnp.stack(kp_rows)
    v_prompt = jnp.stack(vp_rows)
    k_sample = jnp.stack(ks_rows)
    v_sample = jnp.stack(vs_rows)
    chunk_v_sample = jnp.stack(cv_rows)
    return (xp, xs, k_prompt, v_prompt, k_sample, v_sample, chunk_v_sample)


_drawn_inputs = setup_inputs


def setup_inputs(seed=0):
    import zlib

    import numpy as np

    out = dict(_drawn_inputs(seed))
    spreads = {}
    factors = {'a_vnorm_g': 8.108, 'a_bs': 9.624, 'b_onorm_g': 2.966, 'norm2_g': 4.162}
    for name, (base, spread) in spreads.items():
        noise = np.random.default_rng([zlib.crc32(name.encode()), seed]).standard_normal(out[name].shape)
        drawn = base * np.exp(spread * noise) if base else spread * noise
        out[name] = __import__('jax').numpy.asarray(drawn.astype(out[name].dtype))
    for name, factor in factors.items():
        out[name] = (out[name] * factor).astype(out[name].dtype)
    return out
```

```python
import math
from contextlib import ExitStack, contextmanager

import numpy as np
import concourse.bass as bass
from concourse import mybir

ALU = mybir.AluOpType
ACT = mybir.ActivationFunctionType
AX = mybir.AxisListType
F32 = mybir.dt.float32
BF16 = mybir.dt.bfloat16

P = 128
L = 2
D = 1024
KD = D // P
NT = 5
TP = 4
TOK = NT * P
NB, NS = 8, 8
NROW = NB * NS
H = 4
DK, DV = 64, 128
HA, DHA = 8, 64
PAGES = 2
NPOOL = 20
E, G, EG = 16, 4, 4
DE = 256
EPS = 1e-6
SCALE = DK ** -0.5
W = 512
HALF = KD // 2
PIECE = HALF * W
RING = 6
N_IN = 10
N_OUT = 4
N_DENSE = N_IN + N_OUT
PER_EXPERT = 3
PER_LAYER = N_DENSE + E * PER_EXPERT
UNROLL = 4
CREDIT = 8

_PAR = [("g1", KD), ("g2", KD), ("qn", 1), ("on", 1), ("keep", 1), ("init", 1), ("kn", DK), ("av", W),
        ("lam", 4 * DK), ("bs", 4 * P), ("router", KD * 20)]
PAR = {}
_at = 0
for _n, _w in _PAR:
    PAR[_n] = slice(_at, _at + _w)
    _at += _w
NPAR = _at
C_ID, C_CAUSAL, C_BATCH, C_SPREAD, C_FIRST = (slice(i * P, (i + 1) * P) for i in range(5))
NC32 = 5 * P
C_MAP0, C_MAP1 = slice(4 * P + 16, 4 * P + 17), slice(4 * P + 17, 4 * P + 18)
B_ID, B_CAUSAL = slice(0, P), slice(P, 2 * P)
B_SAMPLE = slice(2 * P, 2 * P + NB * NROW)
NC16 = 2 * P + NB * NROW


class Count:

    loops = []
    every = []

    def __init__(self, sem, name, totals, start=0, answers=None):
        self.sem, self.name, self.totals = sem, name, totals
        self.local, self.where = start, totals.setdefault(("where", name), {})
        self.answers, self.begin = answers, start
        Count.every.append(self)

    def step(self, loop):
        if self.answers:
            return self.answers.step(loop)
        return self.totals.get((self.name, loop), 0)

    def inc(self, *label, by=1):
        self.local += by
        self.where[label] = (self.local, tuple(n for n, _, _ in Count.loops))
        return self.sem, by

    def value(self, local, names):
        active = {n: i for n, i, _ in Count.loops}
        out = local
        for n in names:
            if self.step(n):
                out = (active[n] if n in active else TURNS[n] - 1) * self.step(n) + out
        return out

    def at(self, *label):
        local, names = (self.answers or self).where.get(label, (1, ()))
        return self.sem, self.value(local + (self.begin if self.answers else 0), names)

    def now(self, more=0):
        return self.value(self.local + more, [n for n, _, _ in Count.loops])

    def start(self, initial):
        return self.sem, self.value(initial, ["layer"])


TURNS = {"layer": L, "expert": E // UNROLL}


@contextmanager
def turns(eng, name):
    before = {c: c.local for c in Count.every}
    with eng.Fori(0, TURNS[name]) as i:
        Count.loops.append((name, i, TURNS[name]))
        yield i
        Count.loops.pop()
    for c in Count.every:
        if c in before and c.local != before[c]:
            c.totals[(c.name, name)] = c.local - before[c]
            c.local = before[c] + TURNS[name] * (c.local - before[c])


def program(nc, totals, d):
    Count.loops, Count.every = [], []
    with ExitStack() as ctx:
        def sb(name, shape, dt=F32):
            return ctx.enter_context(nc.sbuf_tensor(name, shape, dt))

        def count(name, start=0, answers=None):
            return Count(ctx.enter_context(nc.semaphore(name)), name, totals, start, answers)

        x = sb("x", [P, NT, D])
        ring = sb("ring", [P, RING, PIECE])
        hT_cols = sb("hT", [P, KD * TOK])
        hT = hT_cols[:, :].rearrange("p (k t) -> p k t", k=KD)
        e_sb = hT_cols[:, 0:2048].rearrange("p (b m k) -> p b m k", b=2, m=2)
        a_sb = hT_cols[:, 2048:3072].rearrange("p (b k) -> p b k", b=2)
        aT = hT_cols[:, 3072:4096].rearrange("p (b j k) -> p b j k", b=2, j=4)
        es = hT_cols[:, 4096:4096 + 640].rearrange("p (b k) -> p b k", b=2)
        aTs = hT_cols[:, 4736:4736 + 384].rearrange("p (b j k) -> p b j k", b=2, j=3)
        cat_cols = sb("cat", [P, KD * TOK])
        catT = cat_cols[:, :].rearrange("p (k t) -> p k t", k=KD)
        qz = cat_cols[:, 4 * TOK:8 * TOK].rearrange("p (t n) -> p t n", t=NT)
        hn = sb("hn", [P, 2, D])
        qS = hn[:, :, :].rearrange("p a (b h r) -> p (a b) h r", b=4, h=H)
        kva = sb("kva", [P, NT, W])
        v = sb("v", [P, NT, W])
        qT = sb("qT", [P, H, TOK])
        kT = sb("kT", [P, H, TOK])
        par = sb("par", [P, NPAR])
        ws = sb("ws", [P, HA, P])
        wsS = sb("wsS", [P, HA, P])
        kc = sb("kc", [P, 2, H, PAGES * P])
        vc = sb("vc", [P, 2, PAGES, W])
        sqj = sb("sqj", [P, 2, W])
        tmp = sb("tmp", [P, W])
        o_sb = sb("o_sb", [P, 2, W])
        oT = sb("oT", [P, H, P])
        c32 = sb("c32", [P, NC32])
        c16 = sb("c16", [P, NC16], BF16)
        st = sb("st", [P, 512])
        lg = sb("lg", [P, NT, 20])
        gates = sb("gates", [P, NT, E])
        gcur = sb("gcur", [P, NT, UNROLL])
        cmpA = cat_cols[:, 0:NT * E * EG].rearrange("p (n j) -> p n j", j=EG)
        cmpB = cat_cols[:, 512:512 + NT * E * EG].rearrange("p (n j) -> p n j", j=EG)
        sil = cat_cols[:, 1024:1536].rearrange("p (b f) -> p b f", b=2)
        act_sb = cat_cols[:, 1536:2048].rearrange("p (b f) -> p b f", b=2)
        actT = cat_cols[:, 2048:2560].rearrange("p (b f t) -> p b f t", b=2, f=2)
        half = sb("half", [P, 64])
        pages = sb("pages", [1, NB * PAGES], mybir.dt.int32)
        ps = ctx.enter_context(nc.psum_tensor("ps", [P, 8, 512], F32))

        stat = {}
        used = 0
        for name, w in [("ss", NT), ("rs", NT), ("ssk", 8 * NT), ("rsk", 8 * NT), ("ssa", NT), ("rsa", NT),
                        ("sso", 4 * NT), ("rso", 4 * NT), ("mx", 8), ("nb", 8), ("sm", 16), ("co", 8), ("r0", 8),
                        ("mxs", 4), ("nbs", 4), ("sms", 4), ("lam", 4), ("gm", 5), ("gs", 5), ("gw", 5),
                        ("rank", 20), ("goh", 20), ("em", 20), ("es", 20), ("sel", 80), ("ex", 80), ("ms", 8), ("rowf", 1)]:
            stat[name] = st[:, used:used + w]
            used += w
        assert used <= 512

        ident, identb = c32[:, C_ID], c16[:, B_ID]

        FIRST = {"S0": 0, "T0": 2, "T1": 3, "S1": 4, "O": 6}
        full = {u: count(f"full_{u}") for u in FIRST}
        read = {u: count(f"read_{u}", 1, full[u]) for u in FIRST}

        def bank(u, k=0):
            return ps[:, FIRST[u] + k, :]

        landed = [count(f"landed_{s}") for s in range(RING)]
        piece_used = count("piece_used", CREDIT)
        x_in, c_in = count("x_in"), count("c_in")
        par_in, ws_in = count("par_in"), count("ws_in")
        kv_in = [count(f"kv_in{b}") for b in range(2)]
        kv_used = count("kv_used", 2)
        pages_in = count("pages_in")
        k_stored, va_stored, v_stored, stored = count("k_stored"), count("va_stored"), count("v_stored"), count("stored")
        act_s, dve_s, pool_s = count("act_s"), count("dve_s"), count("pool_s")
        dve_c, pool_c = count("dve_c"), count("pool_c")
        pool_passed = ctx.enter_context(nc.semaphore("pool_passed"))
        par_free = count("par_free", 1)

        x_in_ready = (x_in.sem, 16 * NT)

        block = ctx.enter_context(nc.Block())

        SLOT = [i % RING for i in range(PER_LAYER)]

        @block.sync
        def _(sp):
            for c in [*read.values(), piece_used, kv_used, par_free]:
                sp.sem_inc(c.sem, c.begin)
            for t in range(TP):
                sp.dma_start(x[:, t, :], d["xp"][t * P:(t + 1) * P, :]).then_inc(*x_in.inc(by=16))
            sp.dma_start(x[0:NROW, TP, :], d["xs"]).then_inc(*x_in.inc(by=16))
            sp.dma_start(c32[:, :], d["c32"]).then_inc(*c_in.inc(by=16))
            sp.dma_start(cat_cols[:, 0:NC16], d["c16"]).then_inc(*c_in.inc(by=16))
            with turns(sp, "layer") as l:
                for i in range(N_DENSE):
                    back = (i - RING if i >= RING else i - 1 if i < PER_LAYER % RING else i - 7)
                    sp.wait_ge(piece_used.sem, l * PER_LAYER + (back + (1 if i >= RING else 0) + CREDIT))
                    sp.dma_start(ring[:, SLOT[i], :], d["w"][bass.DynSlice(l * PER_LAYER + i, 1), :, :].rearrange("a p n -> (a p) n")
                                 ).then_inc(*landed[SLOT[i]].inc("w", i, by=16))
                with turns(sp, "expert") as q:
                    for j in range(UNROLL * PER_EXPERT):
                        i = N_DENSE + j
                        piece = l * PER_LAYER + q * (UNROLL * PER_EXPERT)
                        sp.wait_ge(piece_used.sem, piece + (i - RING + 1 + CREDIT))
                        sp.dma_start(ring[:, SLOT[i], :], d["w"][bass.DynSlice(piece + i, 1), :, :].rearrange("a p n -> (a p) n")
                                     ).then_inc(*landed[SLOT[i]].inc("w", i, by=16))
            sp.wait_ge(*read["O"].at("down", UNROLL * NT - 1))
            for t in range(TP):
                sp.dma_start(d["yp"][t * P:(t + 1) * P, :], x[:, t, :]).then_inc(*stored.inc(by=16))
            sp.dma_start(d["ys"], x[0:NROW, TP, :]).then_inc(*stored.inc(by=16))
            sp.wait_ge(stored.sem, stored.now())
            sp.wait_ge(*v_stored.at("v"))
            sp.wait_ge(*va_stored.at("va"))
            sp.wait_ge(*k_stored.at("k"))

        @block.gpsimd
        def _(pool):
            nc.gpsimd.memset(half[:, :], -0.5).then_inc(*pool_c.inc())
            pool.dma_start(pages[:, :], d["pages"]).then_inc(*pages_in.inc(by=16))
            pool.wait_ge(pages_in.sem, 16)

            def wait(sem, value):
                pool.wait_ge(sem, value)
                pool.sem_inc(pool_passed, 1)

            def rsqrt(dst, src, n, size, label):
                if Count.loops:
                    wait(pool_c.sem, pool_c.now())
                nc.gpsimd.tensor_scalar(stat["ms"][:, 0:n], src, 1.0 / size, EPS, ALU.mult, ALU.add).then_inc(*pool_c.inc())
                wait(pool_c.sem, pool_c.now())
                nc.gpsimd.tensor_tensor(dst, stat["ms"][:, 0:n], half[:, 0:n], ALU.pow).then_inc(*pool_c.inc(*label))

            def kv_load(b, l):
                wait(kv_used.sem, kv_used_value(b))
                for g in range(PAGES):
                    page = pool.value_load(pages[0:1, b * PAGES + g:b * PAGES + g + 1], min_val=0, max_val=NPOOL - 1)
                    row = bass.DynSlice(l * NPOOL + page, 1)
                    pool.dma_start(kc[:, b % 2, :, g * P:(g + 1) * P], d["ck"][row, :, :, :].rearrange("a p h t -> (a p) h t")
                                   ).then_inc(*kv_in[b % 2].inc("kv", b, by=16))
                    pool.dma_start(vc[:, b % 2, g, :], d["cv"][row, :, :].rearrange("a p n -> (a p) n")
                                   ).then_inc(*kv_in[b % 2].inc("kv", b, by=16))

            def kv_used_value(b):
                return Count.loops[0][1] * NB + (b + 1) if b < 2 else Count.loops[0][1] * NB + (b - 2 + 1 + 2)

            with turns(pool, "layer") as l:
                wait(*par_free.start(1))
                pool.dma_start(par[:, :], d["par"][bass.DynSlice(l, 1), :, :].rearrange("a p n -> (a p) n")).then_inc(*par_in.inc("par", by=16))
                pool.dma_start(ws[:, :, :], d["ws"][bass.DynSlice(l, 1), :, :, :].rearrange("a p h t -> (a p) h t")).then_inc(*ws_in.inc("ws", by=16))
                kv_load(0, l)
                kv_load(1, l)
                for t in range(NT):
                    wait(*act_s.at("ss1", t))
                    rsqrt(stat["rs"][:, t:t + 1], stat["ss"][:, t:t + 1], 1, D, ("rs1", t))
                for t in range(NT):
                    wait(*dve_s.at("ssk", t))
                    rsqrt(stat["rsk"][:, 8 * t:8 * t + 8], stat["ssk"][:, 8 * t:8 * t + 8], 8, DK, ("rsk", t))
                wait(*dve_s.at("k", NT - 1))
                pool.dma_start(d["kp"][bass.DynSlice(l, 1), :, :, :].rearrange("a t p n -> (a p) t n"), kva[:, 0:TP, :]).then_inc(*k_stored.inc(by=16))
                pool.dma_start(d["ks"][bass.DynSlice(l, 1), :, :].rearrange("a p n -> (a p) n"), kva[0:NROW, TP, :]).then_inc(*k_stored.inc("k", by=16))
                for t in (TP - 1, TP):
                    wait(*read[f"S{t % 2}"].at("z", "v", t))
                pool.dma_start(d["vp"][bass.DynSlice(l, 1), :, :, :].rearrange("a t p n -> (a p) t n"), v[:, 0:TP, :]).then_inc(*v_stored.inc(by=16))
                pool.dma_start(d["vs"][bass.DynSlice(l, 1), :, :].rearrange("a p n -> (a p) n"), v[0:NROW, TP, :]).then_inc(*v_stored.inc("v", by=16))
                for t in range(NT):
                    wait(*dve_s.at("ssq", t))
                    rsqrt(stat["rsk"][:, 8 * t:8 * t + 8], stat["ssk"][:, 8 * t:8 * t + 8], 8, DK, ("rsq", t))
                for t in range(NT):
                    wait(*act_s.at("ssa", t))
                    rsqrt(stat["rsa"][:, t:t + 1], stat["ssa"][:, t:t + 1], 1, W, ("rsa", t))
                wait(*dve_s.at("va", NT - 1))
                pool.dma_start(d["cvs"][bass.DynSlice(l, 1), :, :].rearrange("a p n -> (a p) n"), kva[0:NROW, TP, :]).then_inc(*va_stored.inc("va", by=16))
                for t in range(NT):
                    if t == TP:
                        for b in range(2, NB):
                            kv_load(b, l)
                    wait(*dve_s.at("sso", t))
                    rsqrt(stat["rso"][:, 4 * t:4 * t + 4], stat["sso"][:, 4 * t:4 * t + 4], 4, DV, ("rso", t))
                for t in range(NT):
                    wait(*act_s.at("ss2", t))
                    rsqrt(stat["rs"][:, t:t + 1], stat["ss"][:, t:t + 1], 1, D, ("rs2", t))

        ATT = [(i, h) for i in range(TP) for h in range(H)]

        @block.tensor
        def _(pe):
            pending = []

            def mm(out, lhsT, rhs, start=True, stop=True, inc=None, tr=False, loose=False):
                if tr:
                    ins = pe.transpose(out, lhsT, rhs)
                else:
                    ins = pe.matmul(out, lhsT, rhs, start=start, stop=stop, skip_group_check=loose)
                if inc:
                    ins.then_inc(*inc)
                elif pending:
                    c, label = pending.pop(0)
                    ins.then_inc(*c.inc(*label))

            def claim(u):
                pe.wait_ge(read[u].sem, full[u].now(1))

            def turn_rows(stage, t, ready):
                pe.wait_ge(*ready)
                for hf in range(2):
                    u = f"T{hf}"
                    claim(u)
                    for j in range(HALF):
                        k = hf * HALF + j
                        mm(bank(u)[:, j * P:(j + 1) * P], hn[:, t % 2, k * P:(k + 1) * P], ident, tr=True,
                           inc=full[u].inc(stage, t, hf) if j == HALF - 1 else None)

            pe.wait_ge(c_in.sem, 32)
            pe.wait_ge(dve_s.sem, 1)
            with turns(pe, "layer"):
                for t in range(NT):
                    turn_rows("h1", t, dve_s.at("hn1", t))

                def arrived(i):
                    pe.wait_ge(*landed[SLOT[i]].at("w", i))

                def rows(name, c):
                    for t in range(NT):
                        u = f"S{t % 2}"
                        claim(u)
                        if c == 0:
                            for hf in range(2):
                                pe.wait_ge(*read[f"T{hf}"].at("h1", t, hf))
                        for k in range(KD):
                            if t == 0 and k % HALF == 0:
                                arrived(2 * c + k // HALF)
                            mm(bank(u), hT[:, k, t * P:(t + 1) * P], ring[:, SLOT[2 * c + k // HALF], (k % HALF) * W:(k % HALF + 1) * W],
                               start=(k == 0), stop=(k == KD - 1),
                               inc=full[u].inc("z", name, t) if k == KD - 1 else None)
                            if t == NT - 1 and k % HALF == HALF - 1:
                                pending.append((piece_used, ()))

                def turn_heads(name, src, ready):
                    for t in range(NT):
                        pe.wait_ge(*ready(t))
                        u = f"T{t % 2}"
                        claim(u)
                        for h in range(H):
                            mm(bank(u)[:, h * P:(h + 1) * P], src[:, t, h * P:(h + 1) * P], ident, tr=True,
                               inc=full[u].inc(name, t) if h == H - 1 else None)

                rows("k", 0)
                rows("v", 1)
                rows("q", 2)
                turn_heads("kT", kva, lambda t: dve_s.at("k", t))
                rows("va", 3)
                turn_heads("qT", qz, lambda t: dve_s.at("q", t))
                for m in range(4):
                    for part, (a, b) in enumerate([(0, W), (W, TOK)]):
                        u = f"S{part}"
                        claim(u)
                        for k in range(KD):
                            if m == 0 and part == 0 and k % HALF == 0:
                                arrived(8 + k // HALF)
                            mm(bank(u)[:, 0:b - a], ring[:, SLOT[8 + k // HALF], (k % HALF) * W + m * P:(k % HALF) * W + (m + 1) * P],
                               hT[:, k, a:b], start=(k == 0), stop=(k == KD - 1),
                               inc=full[u].inc("u", m, part) if k == KD - 1 else None)
                            if m == 3 and part == 1 and k % HALF == HALF - 1:
                                pending.append((piece_used, ()))
                pe.wait_ge(*dve_s.at("ws"))
                claim("O")
                mm(bank("O")[:, 0:HA * NS].rearrange("p (h t) -> p h t", h=HA), c32[0:NS, C_SPREAD], ws[0:NS, :, 0:NS], inc=full["O"].inc("wsS"))
                for t in range(NT):
                    u = f"S{t % 2}"
                    claim(u)
                    pe.wait_ge(*dve_s.at("va", t))
                    if t == TP:
                        pe.wait_ge(*read["O"].at("wsS"))
                    for h in range(HA):
                        r = (h % 2) * DHA
                        mm(bank(u)[r:r + DHA, (h // 2) * P:(h // 2 + 1) * P], kva[:, t, h * DHA:(h + 1) * DHA],
                           (wsS if t == TP else ws)[:, h, :], inc=full[u].inc("mix", t) if h == HA - 1 else None)

                def scores(n):
                    i, h = ATT[n]
                    u = f"S{n % 2}"
                    claim(u)
                    if n == 0:
                        for t in (TP - 1, TP):
                            pe.wait_ge(*read[f"T{t % 2}"].at("qT", t))
                    for m in range(2):
                        mm(bank(u, m)[:, 0:(i + 1) * P], qT[m * DK:(m + 1) * DK, h, i * P:(i + 1) * P],
                           kT[m * DK:(m + 1) * DK, h, 0:(i + 1) * P])
                        mm(bank(u, m)[:, i * P:(i + 1) * P], identb, c16[:, B_CAUSAL], start=False, loose=True,
                           inc=full[u].inc("s", n) if m == 1 else None)

                def turn_probs(n):
                    i, h = ATT[n]
                    pe.wait_ge(*dve_s.at("a", n))
                    u = f"T{n % 2}"
                    claim(u)
                    for j in range(i + 1):
                        mm(bank(u)[:, j * P:(j + 1) * P], a_sb[:, n % 2, j * P:(j + 1) * P], ident, tr=True,
                           inc=full[u].inc("aT", n) if j == i else None)

                def weigh(n):
                    i, h = ATT[n]
                    if h == 0:
                        claim("O")
                    pe.wait_ge(*read[f"T{n % 2}"].at("aT", n))
                    for j in range(i + 1):
                        mm(bank("O")[:, h * DV:(h + 1) * DV], aT[:, n % 2, j, :], v[:, j, h * DV:(h + 1) * DV],
                           start=(j == 0), stop=(j == i), inc=full["O"].inc("o", i) if (h == H - 1 and j == i) else None)

                def turn_out(t):
                    pe.wait_ge(*dve_s.at("o", t))
                    u = f"T{t % 2}"
                    claim(u)
                    for h in range(H):
                        mm(bank(u)[:, h * P:(h + 1) * P], o_sb[:, t % 2, h * P:(h + 1) * P], ident, tr=True,
                           inc=full[u].inc("oT", t) if h == H - 1 else None)

                for n in range(len(ATT) + 2):
                    if n < len(ATT):
                        scores(n)
                    if 1 <= n <= len(ATT):
                        turn_probs(n - 1)
                    if n >= 2:
                        weigh(n - 2)
                    if n >= 8 and n % 4 == 0:
                        turn_out(n // 4 - 2)

                def sample_scores(g):
                    u = f"S{g % 2}"
                    claim(u)
                    for b in (2 * g, 2 * g + 1):
                        r = (b % 2) * 64
                        pe.wait_ge(*kv_in[b % 2].at("kv", b))
                        for h in range(H):
                            mm(bank(u)[r:r + 64, 0:PAGES * P], qS[:, b, h, :], kc[:, b % 2, h, :], start=(h == 0), stop=(h == H - 1))
                        for h in range(H):
                            mm(bank(u)[r:r + 64, PAGES * P:PAGES * P + 64], qS[:, b, h, :], kT[:, h, TP * P:TP * P + 64], start=(h == 0), stop=False)
                        mm(bank(u)[r:r + 64, PAGES * P:PAGES * P + 64], identb[0:64, 0:64],
                           c16[0:64, B_SAMPLE][:, b * 64:(b + 1) * 64], start=False, inc=full[u].inc("ss", g) if b % 2 else None)

                def sample_weigh(g):
                    u = f"T{g % 2}"
                    pe.wait_ge(*dve_s.at("ps", g))
                    claim(u)
                    for j in range(PAGES):
                        mm(bank(u)[:, j * P:(j + 1) * P], es[:, g % 2, j * P:(j + 1) * P], ident, tr=True)
                    mm(bank(u)[0:64, PAGES * P:(PAGES + 1) * P], es[:, g % 2, PAGES * P:PAGES * P + 64], ident, tr=True, inc=full[u].inc("pT", g))
                    if g == 0:
                        claim("O")
                    pe.wait_ge(*read[u].at("pT", g))
                    for b in (2 * g, 2 * g + 1):
                        for h in range(H):
                            c = (b % 2) * 32 + h * NS
                            out = bank("O")[:, h * 64 + b * NS:h * 64 + (b + 1) * NS]
                            for j in range(PAGES):
                                mm(out, vc[:, b % 2, j, h * DV:(h + 1) * DV], aTs[:, g % 2, j, c:c + NS], start=(j == 0), stop=False)
                            last = b == NB - 1 and h == H - 1
                            mm(out, v[0:64, TP, h * DV:(h + 1) * DV], aTs[0:64, g % 2, PAGES, c:c + NS], start=False,
                               inc=full["O"].inc("soT") if last else kv_used.inc() if h == H - 1 else None)
                    if g == 3:
                        pending.append((kv_used, ()))

                pe.wait_ge(*dve_s.at("qS"))
                for g in range(4):
                    sample_scores(g)
                    sample_weigh(g)
                    if g == 0:
                        turn_out(3)
                claim("O")
                pe.wait_ge(*read["O"].at("soT"))
                for h in range(H):
                    mm(bank("O")[:, h * P:(h + 1) * P], oT[:, h, :], ident, tr=True, inc=full["O"].inc("o", TP) if h == H - 1 else None)
                turn_out(TP)

                for n in range(2):
                    for t in range(NT):
                        u = f"S{(n * NT + t) % 2}"
                        claim(u)
                        if n == 0:
                            pe.wait_ge(*dve_s.at("mix", t))
                            pe.wait_ge(*read[f"T{t % 2}"].at("oT", t))
                        for k in range(KD):
                            i = N_IN + 2 * n + k // HALF
                            if t == 0 and k % HALF == 0:
                                arrived(i)
                            mm(bank(u), catT[:, k, t * P:(t + 1) * P], ring[:, SLOT[i], (k % HALF) * W:(k % HALF + 1) * W],
                               start=(k == 0), stop=(k == KD - 1), inc=full[u].inc("y", n, t) if k == KD - 1 else None)
                            if t == NT - 1 and k % HALF == HALF - 1:
                                pending.append((piece_used, ()))

                for t in range(NT):
                    turn_rows("h2", t, dve_s.at("hn2", t))
                claim("O")
                for t in range(NT):
                    for hf in range(2):
                        pe.wait_ge(*read[f"T{hf}"].at("h2", t, hf))
                    for k in range(KD):
                        mm(bank("O")[:, t * 20:(t + 1) * 20], hT[:, k, t * P:(t + 1) * P], par[:, PAR["router"]][:, k * 20:(k + 1) * 20],
                           start=(k == 0), stop=(k == KD - 1), inc=full["O"].inc("logits") if (t == NT - 1 and k == KD - 1) else None)

                with turns(pe, "expert"):
                    UNITS = [(e, t) for e in range(UNROLL) for t in range(NT)]

                    def up(n, hf):
                        e, t = UNITS[n]
                        u = f"S{n % 2}"
                        if hf == 0:
                            claim(u)
                        i = N_DENSE + e * PER_EXPERT + hf
                        if t == 0:
                            arrived(i)
                        for j in range(HALF):
                            k = hf * HALF + j
                            mm(bank(u), hT[:, k, t * P:(t + 1) * P], ring[:, SLOT[i], j * W:(j + 1) * W], start=(k == 0), stop=(k == KD - 1),
                               inc=full[u].inc("gu", n) if k == KD - 1 else None)
                        if t == NT - 1:
                            pending.append((piece_used, ()))

                    def turn_act(n):
                        pe.wait_ge(*read[f"S{n % 2}"].at("gu", n))
                        u = f"T{n % 2}"
                        claim(u)
                        for f in range(2):
                            mm(bank(u)[:, f * P:(f + 1) * P], act_sb[:, n % 2, f * P:(f + 1) * P], ident, tr=True,
                               inc=full[u].inc("actT", n) if f else None)

                    def down(n):
                        e, t = UNITS[n]
                        claim("O")
                        pe.wait_ge(*read[f"T{n % 2}"].at("actT", n))
                        i = N_DENSE + e * PER_EXPERT + 2
                        if t == 0:
                            arrived(i)
                        for c in range(2):
                            for f in range(2):
                                mm(bank("O", c), actT[:, n % 2, f, :], ring[:, SLOT[i], f * D + c * W:f * D + (c + 1) * W], start=(f == 0), stop=(f == 1),
                                   inc=full["O"].inc("down", n) if (c and f) else None)
                        if t == NT - 1:
                            pending.append((piece_used, ()))

                    up(0, 0)
                    up(0, 1)
                    for n in range(len(UNITS)):
                        if n + 1 < len(UNITS):
                            up(n + 1, 0)
                        turn_act(n)
                        if n + 1 < len(UNITS):
                            up(n + 1, 1)
                        down(n)
                    claim("T0")
                    mm(bank("T0")[:, 0:P], ident, ident, tr=True)

        @block.scalar
        def _(act):
            def square_rows(stage, ready):
                for t in range(NT):
                    act.wait_ge(*ready(t))
                    if t:
                        act.wait_ge(*act_s.at(stage, t - 1))
                    nc.scalar.activation(sqbig, x[:, t, :], ACT.Square, accum_out=stat["ss"][:, t:t + 1]).then_inc(*act_s.inc(stage, t))

            sqbig = sqj[:, :, :].rearrange("p a n -> p (a n)")

            act.wait_ge(dve_s.sem, 1)
            with turns(act, "layer"):
                act.wait_ge(*read["O"].start(1))
                square_rows("ss1", lambda t: x_in_ready)
                act.wait_ge(*par_in.at("par"))

                def evacuate(name, dst):
                    for t in range(NT):
                        u = f"S{t % 2}"
                        act.wait_ge(*full[u].at("z", name, t))
                        if name == "va" and t == 0:
                            act.wait_ge(*k_stored.at("k"))
                        if name == "va":
                            act.wait_ge(*full[f"T{t % 2}"].at("kT", t))
                            nc.scalar.activation(dst[:, t, :], bank(u), ACT.Gelu_apprx_tanh).then_inc(*read[u].inc("z", name, t))
                            act.wait_ge(*read[u].at("z", name, t))
                            if t >= 2:
                                act.wait_ge(*act_s.at("ssa", t - 2))
                            nc.scalar.activation(sqj[:, t % 2, :], dst[:, t, :], ACT.Square, accum_out=stat["ssa"][:, t:t + 1]).then_inc(*act_s.inc("ssa", t))
                            continue
                        if name in "kq":
                            if t >= 2:
                                act.wait_ge(*dve_s.at("ss" + name, t - 2))
                            elif name == "q":
                                act.wait_ge(*dve_s.at("ssk", NT - 1))
                            if name == "k" and t < 2:
                                act.wait_ge(*act_s.at("ss1", NT - 1))
                            nc.scalar.activation(sqj[:, t % 2, :], bank(u), ACT.Square).then_inc(*act_s.inc("sq", name, t))
                            nc.scalar.copy(dst[:, t, :], bank(u)).then_inc(*read[u].inc("z", name, t))
                        else:
                            nc.scalar.copy(dst[:, t, :], bank(u)).then_inc(*read[u].inc("z", name, t))

                evacuate("k", kva)
                evacuate("v", v)
                evacuate("q", qz)
                for t in range(NT):
                    act.wait_ge(*full[f"T{t % 2}"].at("kT", t))
                    nc.scalar.copy(kT[:, :, t * P:(t + 1) * P], bank(f"T{t % 2}").rearrange("p (h t) -> p h t", h=H)).then_inc(*read[f"T{t % 2}"].inc("kT", t))
                act.wait_ge(*dve_s.at("ssq", NT - 1))
                evacuate("va", kva)
                for t in range(NT):
                    act.wait_ge(*full[f"T{t % 2}"].at("qT", t))
                    nc.scalar.mul(qT[:, :, t * P:(t + 1) * P], bank(f"T{t % 2}").rearrange("p (h t) -> p h t", h=H), par[:, PAR["qn"]]).then_inc(*read[f"T{t % 2}"].inc("qT", t))
                for m in range(4):
                    for part, (a, b) in enumerate([(0, W), (W, TOK)]):
                        u = f"S{part}"
                        act.wait_ge(*full[u].at("u", m, part))
                        nc.scalar.activation(catT[:, m, a:b], bank(u)[:, 0:b - a], ACT.Gelu_apprx_tanh).then_inc(*read[u].inc("u", m, part))
                act.wait_ge(*dve_s.at("lamdot"))
                nc.scalar.activation(stat["lam"][:, 0:2], stat["lam"][:, 0:2], ACT.Exp).then_inc(*act_s.inc("lamexp"))

                def probs(n):
                    i, h = ATT[n]
                    act.wait_ge(*dve_s.at("nb", n))
                    if n >= 2:
                        act.wait_ge(*dve_s.at("a", n - 2))
                    for m in range(2):
                        c = 2 * (n % 4) + m
                        ins = nc.scalar.activation(e_sb[:, n % 2, m, 0:(i + 1) * P], bank(f"S{n % 2}", m)[:, 0:(i + 1) * P], ACT.Exp,
                                                   bias=stat["nb"][:, c:c + 1], scale=SCALE,
                                                   accum_out=stat["sm"][:, c:c + 1])
                    ins.then_inc(*read[f"S{n % 2}"].inc("s", n))

                def probs_turned(n):
                    i, h = ATT[n]
                    u = f"T{n % 2}"
                    act.wait_ge(*full[u].at("aT", n))
                    nc.scalar.copy(aT[:, n % 2, 0:i + 1, :], bank(u)[:, 0:(i + 1) * P].rearrange("p (j q) -> p j q", q=P)).then_inc(*read[u].inc("aT", n))

                for n in range(len(ATT) + 1):
                    if n < len(ATT):
                        probs(n)
                    if n >= 1:
                        probs_turned(n - 1)
                for g in range(4):
                    u = f"S{g % 2}"
                    act.wait_ge(*dve_s.at("nbs", g))
                    nc.scalar.activation(es[:, g % 2, :], bank(u)[:, 0:320], ACT.Exp, bias=stat["nbs"][:, g:g + 1], scale=SCALE,
                                         accum_out=stat["sms"][:, g:g + 1]).then_inc(*read[u].inc("ss", g))
                act.wait_ge(*full["O"].at("soT"))
                nc.scalar.copy(oT[:, :, 0:64], bank("O")[:, 0:256].rearrange("p (h t) -> p h t", h=H)).then_inc(*read["O"].inc("soT"))

                square_rows("ss2", lambda t: read[f"S{(NT + t) % 2}"].at("y", 1, t))
                act.wait_ge(*dve_s.at("lgsub"))
                nc.scalar.activation(lg[:, :, :], lg[:, :, :], ACT.Exp).then_inc(*act_s.inc("lgexp"))
                with turns(act, "expert"):
                    for n in range(UNROLL * NT):
                        u = f"S{n % 2}"
                        act.wait_ge(*full[u].at("gu", n))
                        if n >= 2:
                            act.wait_ge(*read[f"S{n % 2}"].at("gu", n - 2))
                        nc.scalar.activation(sil[:, n % 2, :], bank(u)[:, 0:DE], ACT.Silu).then_inc(*act_s.inc("sil", n))
                        act.wait_ge(*full[f"T{n % 2}"].at("actT", n))
                        nc.scalar.copy(actT[:, n % 2, :, :], bank(f"T{n % 2}")[:, 0:2 * P].rearrange("p (f t) -> p f t", f=2)).then_inc(*read[f"T{n % 2}"].inc("actT", n))

        @block.vector
        def _(dve):
            vec = nc.vector

            def link(ins):
                ins.then_inc(*dve_c.inc())
                dve.wait_ge(dve_c.sem, dve_c.now())

            vec.memset(x[NROW:P, TP, :], 0.0)
            vec.memset(oT[:, :, :], 0.0)
            dve.wait_ge(c_in.sem, 32)
            vec.tensor_copy(c16[:, :], cat_cols[:, 0:NC16]).then_inc(*dve_s.inc("init"))
            dve.wait_ge(*x_in_ready)

            def norm_rows(stage, stage_r, gain, square):
                def scaled(t):
                    dve.wait_ge(*pool_c.at(stage_r, t))
                    vec.tensor_scalar(hn[:, t % 2, :], x[:, t, :], stat["rs"][:, t:t + 1], None, ALU.mult).then_inc(*dve_s.inc("hn" + stage[1], t))

                def turned(t):
                    for hf in range(2):
                        dve.wait_ge(*full[f"T{hf}"].at(stage, t, hf))
                        g = par[:, PAR[gain]][:, hf * HALF:(hf + 1) * HALF].unsqueeze(2).to_broadcast([P, HALF, P])
                        vec.tensor_tensor(hT[:, hf * HALF:(hf + 1) * HALF, t * P:(t + 1) * P],
                                          bank(f"T{hf}").rearrange("p (j t) -> p j t", j=HALF), g, ALU.mult).then_inc(*read[f"T{hf}"].inc(stage, t, hf))

                for t in range(NT + 1):
                    if t < NT:
                        scaled(t)
                    if t >= 1:
                        turned(t - 1)

            def groups(ap, n, w):
                return ap.rearrange("p (n w) -> p n w", n=n)

            def wide(ap, n, w):
                return ap.unsqueeze(2).to_broadcast([P, n, w])

            def across(ap, n, w):
                return ap.unsqueeze(1).to_broadcast([P, n, w])

            with turns(dve, "layer"):
                dve.wait_ge(*par_in.at("par"))
                norm_rows("h1", "rs1", "g1", "ss1")
                dve.wait_ge(*ws_in.at("ws"))
                vec.tensor_tensor(ws[:, :, :], ws[:, :, :], across(c32[:, C_CAUSAL], HA, P), ALU.mult).then_inc(*dve_s.inc("ws"))
                lam = par[:, PAR["lam"]]
                for i in range(2):
                    link(vec.tensor_tensor(tmp[:, i * DK:(i + 1) * DK], lam[:, 2 * i * DK:(2 * i + 1) * DK], lam[:, (2 * i + 1) * DK:(2 * i + 2) * DK], ALU.mult))
                vec.tensor_reduce(stat["lam"][:, 0:2], groups(tmp[:, 0:2 * DK], 2, DK), AX.X, ALU.add).then_inc(*dve_s.inc("lamdot"))
                link(vec.memset(qS[:, :, :, :], 0.0))

                def sums(name, t):
                    dve.wait_ge(*act_s.at("sq", name, t))
                    if name == "q":
                        dve.wait_ge(dve_c.sem, dve_c.now())
                    vec.tensor_reduce(stat["ssk"][:, 8 * t:8 * t + 8], groups(sqj[:, t % 2, :], 8, DK), AX.X, ALU.add).then_inc(*dve_s.inc("ss" + name, t))

                for t in range(NT):
                    sums("k", t)
                for t in range(NT):
                    dve.wait_ge(*pool_c.at("rsk", t))
                    dve.wait_ge(*read[f"S{t % 2}"].at("z", "k", t))
                    z = groups(kva[:, t, :], 8, DK)
                    link(vec.tensor_tensor(z, z, wide(stat["rsk"][:, 8 * t:8 * t + 8], 8, DK), ALU.mult))
                    vec.tensor_tensor(z, z, across(par[:, PAR["kn"]], 8, DK), ALU.mult).then_inc(*dve_s.inc("k", t))
                for t in range(NT):
                    sums("q", t)
                for t in range(NT):
                    dve.wait_ge(*pool_c.at("rsq", t))
                    dve.wait_ge(*read[f"S{t % 2}"].at("z", "q", t))
                    z = groups(qz[:, t, :], 8, DK)
                    vec.tensor_tensor(z, z, wide(stat["rsk"][:, 8 * t:8 * t + 8], 8, DK), ALU.mult).then_inc(*dve_s.inc("q", t))
                for t in range(NT):
                    dve.wait_ge(*pool_c.at("rsa", t))
                    vec.scalar_tensor_tensor(kva[:, t, :], kva[:, t, :], stat["rsa"][:, t:t + 1], par[:, PAR["av"]],
                                             ALU.mult, ALU.mult).then_inc(*dve_s.inc("va", t))
                dve.wait_ge(*read["T0"].at("qT", TP))
                for h in range(H):
                    for m in range(2):
                        r = slice(m * DK, (m + 1) * DK)
                        c = h * 16 + m * NS
                        ins = vec.tensor_copy(qS[r, :, h, c:c + NS], qT[r, h, TP * P:TP * P + NROW].rearrange("p (b t) -> p b t", b=NB))
                ins.then_inc(*dve_s.inc("qS"))
                dve.wait_ge(*act_s.at("lamexp"))
                link(vec.tensor_tensor(stat["lam"][:, 2:3], stat["lam"][:, 1:2], stat["lam"][:, 0:1], ALU.subtract))
                link(vec.tensor_tensor(stat["lam"][:, 3:4], stat["lam"][:, 2:3], par[:, PAR["init"]], ALU.subtract))
                neglam = stat["lam"][:, 3:4]
                link(vec.scalar_tensor_tensor(stat["rowf"], c32[:, C_MAP1], neglam, c32[:, C_MAP0], ALU.mult, ALU.add))
                dve.wait_ge(*full["O"].at("wsS"))
                vec.tensor_tensor(wsS[:, :, :].rearrange("p h (b t) -> p h b t", t=NS),
                                  bank("O")[:, 0:HA * NS].rearrange("p (h t) -> p h t", h=HA).unsqueeze(2).to_broadcast([P, HA, 16, NS]),
                                  c32[:, C_BATCH].rearrange("p (b t) -> p b t", t=NS).unsqueeze(1).to_broadcast([P, HA, 16, NS]),
                                  ALU.mult).then_inc(*read["O"].inc("wsS"))
                for t in range(NT):
                    u = f"S{t % 2}"
                    dve.wait_ge(*full[u].at("mix", t))
                    if t == 0:
                        dve.wait_ge(*read["S0"].at("u", 3, 0))
                        dve.wait_ge(*read["S1"].at("u", 3, 1))
                    bs = par[:, PAR["bs"]].rearrange("p (c t) -> p c t", c=4)
                    s, o = bank(u), tmp[:, :]
                    if t < TP:
                        s, o = (a.rearrange("p (c t) -> p c t", c=4) for a in (s, o))
                    else:
                        s, o = (a.rearrange("p (c b t) -> p c b t", c=4, t=NS) for a in (s, o))
                        bs = bs[:, :, 0:NS].unsqueeze(2).to_broadcast([P, 4, 16, NS])
                    if t:
                        dve.wait_ge(*dve_s.at("mix", t - 1))
                    vec.tensor_tensor(o, s, bs, ALU.add).then_inc(*read[u].inc("mix", t))
                    dve.wait_ge(*read[u].at("mix", t))
                    vec.tensor_tensor(catT[:, 0:4, t * P:(t + 1) * P], tmp[:, :].rearrange("p (c t) -> p c t", c=4),
                                      catT[:, 0:4, t * P:(t + 1) * P], ALU.mult).then_inc(*dve_s.inc("mix", t))

                def biggest(n):
                    i, h = ATT[n]
                    c = 2 * (n % 4)
                    dve.wait_ge(*full[f"S{n % 2}"].at("s", n))
                    b0 = FIRST[f"S{n % 2}"]
                    link(vec.tensor_reduce(stat["mx"][:, c:c + 2], ps[:, b0:b0 + 2, 0:(i + 1) * P], AX.X, ALU.max))
                    vec.tensor_scalar(stat["nb"][:, c:c + 2], stat["mx"][:, c:c + 2], -SCALE, None, ALU.mult).then_inc(*dve_s.inc("nb", n))

                def combine(n):
                    i, h = ATT[n]
                    c = 2 * (n % 4)
                    dve.wait_ge(*read[f"S{n % 2}"].at("s", n))
                    link(vec.reciprocal(stat["co"][:, 0:2], stat["sm"][:, c:c + 2]))
                    r0 = stat["r0"][:, 4 * (i % 2) + h:4 * (i % 2) + h + 1]
                    vec.tensor_copy(r0, stat["co"][:, 0:1])
                    link(vec.scalar_tensor_tensor(stat["co"][:, 2:3], stat["co"][:, 1:2], neglam, stat["sm"][:, c:c + 1], ALU.mult, ALU.mult))
                    if n >= 2:
                        dve.wait_ge(*full[f"T{n % 2}"].at("aT", n - 2))
                    vec.scalar_tensor_tensor(a_sb[:, n % 2, 0:(i + 1) * P], e_sb[:, n % 2, 1, 0:(i + 1) * P], stat["co"][:, 2:3],
                                             e_sb[:, n % 2, 0, 0:(i + 1) * P], ALU.mult, ALU.add).then_inc(*dve_s.inc("a", n))

                def head_norm(t):
                    dve.wait_ge(*full["O"].at("o", t))
                    o = o_sb[:, t % 2, :]
                    if t < TP:
                        dve.wait_ge(dve_c.sem, dve_c.now())
                        ins = vec.tensor_tensor(groups(o, H, DV), groups(bank("O"), H, DV), wide(stat["r0"][:, 4 * (t % 2):4 * (t % 2) + 4], H, DV), ALU.mult)
                    else:
                        ins = vec.tensor_copy(o, bank("O"))
                    ins.then_inc(*read["O"].inc("o", t))
                    dve.wait_ge(*read["O"].at("o", t))
                    link(vec.tensor_tensor(tmp[:, :], o, o, ALU.mult))
                    vec.tensor_reduce(stat["sso"][:, 4 * t:4 * t + 4], groups(tmp[:, :], H, DV), AX.X, ALU.add).then_inc(*dve_s.inc("sso", t))

                def head_scale(t):
                    o = groups(o_sb[:, t % 2, :], H, DV)
                    dve.wait_ge(*pool_c.at("rso", t))
                    vec.tensor_tensor(o, o, wide(stat["rso"][:, 4 * t:4 * t + 4], H, DV), ALU.mult).then_inc(*dve_s.inc("o", t))

                def head_turned(t):
                    u = f"T{t % 2}"
                    dve.wait_ge(*full[u].at("oT", t))
                    vec.tensor_scalar(catT[:, 4:8, t * P:(t + 1) * P], groups(bank(u), H, P), par[:, PAR["on"]], par[:, PAR["keep"]],
                                      ALU.mult, ALU.mult).then_inc(*read[u].inc("oT", t))

                for n in range(len(ATT) + 1):
                    if n < len(ATT):
                        biggest(n)
                    if n >= 1:
                        combine(n - 1)
                    if n >= 6 and n % 4 == 2:
                        head_norm(n // 4 - 1)
                    if n >= 7 and n % 4 == 3:
                        head_scale(n // 4 - 1)
                    if n >= 9 and n % 4 == 1:
                        head_turned(n // 4 - 2)
                head_turned(2)
                for g in range(4):
                    u = f"S{g % 2}"
                    dve.wait_ge(*full[u].at("ss", g))
                    link(vec.tensor_reduce(stat["mxs"][:, g:g + 1], bank(u)[:, 0:320], AX.X, ALU.max))
                    vec.tensor_scalar(stat["nbs"][:, g:g + 1], stat["mxs"][:, g:g + 1], -SCALE, None, ALU.mult).then_inc(*dve_s.inc("nbs", g))
                    if g == 0:
                        head_norm(3)
                        head_scale(3)
                    dve.wait_ge(*read[u].at("ss", g))
                    link(vec.reciprocal(stat["mxs"][:, g:g + 1], stat["sms"][:, g:g + 1]))
                    vec.tensor_scalar(es[:, g % 2, :], es[:, g % 2, :], stat["mxs"][:, g:g + 1], stat["rowf"], ALU.mult, ALU.mult).then_inc(*dve_s.inc("ps", g))
                    u = f"T{g % 2}"
                    dve.wait_ge(*full[u].at("pT", g))
                    for rows, a, b in ((P, 0, PAGES), (64, PAGES, PAGES + 1)):
                        pt = bank(u)[0:rows, a * P:b * P].rearrange("p (j r m t) -> p j r m t", j=b - a, m=2, t=NS)
                        for j in range(b - a):
                            ins = vec.tensor_reduce(aTs[0:rows, g % 2, a + j, :].rearrange("p (r t) -> p r t", t=NS),
                                                    pt[:, j, :, :, :].rearrange("p r m t -> p r t m"), AX.X, ALU.add)
                            if j == b - a - 1 and a == PAGES:
                                ins.then_inc(*read[u].inc("pT", g))
                            else:
                                link(ins)
                    if g == 0:
                        head_turned(3)
                head_norm(TP)
                head_scale(TP)
                head_turned(TP)

                for n in range(2):
                    for t in range(NT):
                        u = f"S{(n * NT + t) % 2}"
                        dve.wait_ge(*full[u].at("y", n, t))
                        cols = x[:, t, n * W:(n + 1) * W]
                        vec.tensor_tensor(cols, cols, bank(u), ALU.add).then_inc(*read[u].inc("y", n, t))
                norm_rows("h2", "rs2", "g2", "ss2")

                dve.wait_ge(*full["O"].at("logits"))
                vec.tensor_copy(lg[:, :, :], bank("O")[:, 0:NT * 20].rearrange("p (t n) -> p t n", t=NT)).then_inc(*read["O"].inc("logits"))
                dve.wait_ge(*read["O"].at("logits"))
                lgg, lge = lg[:, :, 0:G], lg[:, :, G:20].rearrange("p t (g j) -> p t g j", g=G)

                def rank(out, cols, n):
                    A, B = cmpA[:, 0:n * EG, :], cmpB[:, 0:n * EG, :]
                    A4, B4 = (a.rearrange("p (n j) i -> p n j i", j=EG) for a in (A, B))
                    vi = cols.unsqueeze(2).to_broadcast([P, n, EG, EG])
                    vj = cols.unsqueeze(3).to_broadcast([P, n, EG, EG])
                    vec.tensor_tensor(A4, vi, vj, ALU.is_gt)
                    link(vec.tensor_tensor(B4, vi, vj, ALU.is_equal))
                    first = c32[:, C_FIRST][:, 0:EG * EG].rearrange("p (j i) -> p j i", j=EG).unsqueeze(1).to_broadcast([P, n, EG, EG])
                    link(vec.tensor_tensor(B4, B4, first, ALU.mult))
                    link(vec.tensor_tensor(A, A, B, ALU.add))
                    link(vec.tensor_reduce(out, A, AX.X, ALU.add))

                vec.tensor_copy(stat["goh"].rearrange("p (t g) -> p t g", t=NT), lgg).then_inc(*par_free.inc())
                dve.wait_ge(par_free.sem, par_free.now())
                rank(stat["rank"], stat["goh"].rearrange("p (t g) -> p t g", t=NT), NT)
                link(vec.tensor_scalar(stat["goh"], stat["rank"], 0.5, None, ALU.is_lt))
                link(vec.tensor_copy(stat["ex"].rearrange("p (t n) -> p t n", t=NT), lg[:, :, G:20]))
                ex = stat["ex"].rearrange("p (n j) -> p n j", j=EG)
                rank(stat["sel"], ex, NT * G)
                link(vec.tensor_scalar(stat["sel"], stat["sel"], 1.5, None, ALU.is_lt))
                link(vec.tensor_reduce(stat["gm"], lgg, AX.X, ALU.max))
                link(vec.tensor_tensor(lgg, lgg, wide(stat["gm"], NT, G), ALU.subtract))
                link(vec.tensor_reduce(stat["em"], ex, AX.X, ALU.max))
                link(vec.tensor_tensor(ex, ex, wide(stat["em"], NT * G, EG), ALU.subtract))
                vec.tensor_copy(lg[:, :, G:20], stat["ex"].rearrange("p (t n) -> p t n", t=NT)).then_inc(*dve_s.inc("lgsub"))
                dve.wait_ge(*act_s.at("lgexp"))
                link(vec.tensor_reduce(stat["gs"], lgg, AX.X, ALU.add))
                link(vec.reciprocal(stat["gw"], stat["gs"]))
                link(vec.tensor_copy(stat["ex"].rearrange("p (t n) -> p t n", t=NT), lg[:, :, G:20]))
                link(vec.tensor_tensor(stat["ex"], stat["ex"], stat["sel"], ALU.mult))
                link(vec.tensor_reduce(stat["es"], ex, AX.X, ALU.add))
                link(vec.reciprocal(stat["em"], stat["es"]))
                link(vec.tensor_tensor(stat["em"], stat["em"], stat["goh"], ALU.mult))
                em = stat["em"].rearrange("p (t g) -> p t g", t=NT)
                link(vec.tensor_tensor(em, em, wide(stat["gw"], NT, G), ALU.mult))
                vec.tensor_tensor(gates[:, :, :].rearrange("p t (g j) -> p (t g) j", g=G), ex, wide(stat["em"], NT * G, EG),
                                  ALU.mult).then_inc(*dve_s.inc("gates"))

                with turns(dve, "expert") as q:
                    dve.wait_ge(*dve_s.at("gates"))
                    link(vec.tensor_copy(gcur[:, :, :], gates[:, :, bass.DynSlice(q * UNROLL, UNROLL)]))
                    UNITS = [(e, t) for e in range(UNROLL) for t in range(NT)]

                    def gated(n):
                        e, t = UNITS[n]
                        dve.wait_ge(*act_s.at("sil", n))
                        if n >= 2:
                            dve.wait_ge(*full[f"T{n % 2}"].at("actT", n - 2))
                        vec.scalar_tensor_tensor(act_sb[:, n % 2, :], sil[:, n % 2, :], gcur[:, t, e:e + 1], bank(f"S{n % 2}")[:, DE:2 * DE],
                                                 ALU.mult, ALU.mult).then_inc(*read[f"S{n % 2}"].inc("gu", n))

                    def added(n):
                        e, t = UNITS[n]
                        dve.wait_ge(*full["O"].at("down", n))
                        ins = vec.tensor_tensor(x[:, t, :], x[:, t, :], ps[:, 6:8, :].rearrange("p a n -> p (a n)"), ALU.add)
                        ins.then_inc(*read["O"].inc("down", n))

                    for n in range(len(UNITS) + 1):
                        if n < len(UNITS):
                            gated(n)
                        if n >= 1:
                            added(n - 1)

        return totals


_SHAPES = [("yp", (4 * P, D)), ("ys", (NROW, D)), ("kp", (L, TP, P, W)), ("vp", (L, TP, P, W)), ("ks", (L, NROW, W)),
           ("vs", (L, NROW, W)), ("cvs", (L, NROW, W))]


def layout(a):
    f = np.float32

    def blocks(w):
        k, n = w.shape
        return w.reshape(k // (HALF * P), HALF, P, n // W, W).transpose(3, 0, 2, 1, 4).reshape(-1, P, PIECE)

    w_in, w_out = a["w_in"], a["w_out"]
    w = np.empty((L * PER_LAYER, P, PIECE), f)
    for l in range(L):
        parts = w[l * PER_LAYER:(l + 1) * PER_LAYER]
        cols = blocks(w_in[l])
        for i, c in enumerate((3, 4, 2, 1, 0)):
            parts[2 * i:2 * i + 2] = cols[2 * c:2 * c + 2]
        parts[N_IN:N_DENSE] = blocks(w_out[l])
        for e in range(E):
            at = N_DENSE + PER_EXPERT * e
            parts[at:at + 2] = blocks(np.concatenate([a["w_gate"][l, e], a["w_up"][l, e]], axis=1))
            parts[at + 2] = a["w_down"][l, e].reshape(2, P, D).transpose(1, 0, 2).reshape(P, 2 * D)
    par = np.zeros((L, P, NPAR), f)

    def put(name, value):
        par[:, :, PAR[name]] = value
    put("g1", a["norm1_g"].reshape(L, KD, P).transpose(0, 2, 1))
    put("g2", a["norm2_g"].reshape(L, KD, P).transpose(0, 2, 1))
    put("qn", np.concatenate([a["qn_g"], a["qn_g"]], axis=1)[:, :, None])
    put("on", a["b_onorm_g"][:, :, None])
    for l in range(L):
        init = 0.8 - 0.6 * math.exp(-0.3 * l)
        par[l, :, PAR["init"]] = init
        par[l, :, PAR["keep"]] = 1.0 - init
    put("kn", a["kn_g"][:, None, :])
    put("av", a["a_vnorm_g"][:, None, :])
    put("lam", np.concatenate([a["lam_q1"], a["lam_k1"], a["lam_q2"], a["lam_k2"]], axis=1)[:, None, :])
    bs = a["a_bs"].reshape(L, 4, 2, P).transpose(0, 2, 1, 3).reshape(L, 2, 4 * P)
    put("bs", np.repeat(bs, DHA, axis=1))
    router = np.concatenate([a["router_g"], a["router_e"]], axis=2)
    put("router", router.reshape(L, KD, P, 20).transpose(0, 2, 1, 3).reshape(L, P, KD * 20))
    c32 = np.zeros((P, NC32), f)
    r = np.arange(P)
    c32[:, C_ID] = np.eye(P)
    c32[:, C_CAUSAL] = r[:, None] <= r[None, :]
    c32[:, C_BATCH] = r[:, None] // NS == r[None, :] // NS
    c32[0:NS, C_SPREAD] = r[0:NS, None] == r[None, :] % NS
    j, i = np.divmod(np.arange(EG * EG), EG)
    c32[:, C_FIRST.start:C_FIRST.start + EG * EG] = i < j
    c32[:, C_MAP0] = (r[:, None] // NS) % 2 == 0
    c32[:, C_MAP1] = (r[:, None] // NS) % 2 == 1
    c16 = np.zeros((P, NC16), f)
    c16[:, B_ID] = np.eye(P)
    c16[:, B_CAUSAL] = np.where(r[None, :] <= r[:, None], 0.0, -1e30)
    row, key = np.arange(64), np.arange(64)
    for b in range(NB):
        ok = (key[None, :] // NS == b) & (key[None, :] % NS <= row[:, None] % NS)
        c16[0:64, B_SAMPLE.start + b * 64:B_SAMPLE.start + (b + 1) * 64] = np.where(ok, 0.0, -1e30)
    return {
        "xp": a["x_prompt"].reshape(4 * P, D), "xs": a["x_sample"].reshape(NROW, D),
        "w": w, "par": par, "ws": a["a_ws"].transpose(0, 3, 1, 2),
        "ck": a["cache_k"].transpose(0, 1, 4, 3, 2).reshape(L * NPOOL, P, H, P),
        "cv": a["cache_v"].reshape(L * NPOOL, P, W),
        "pages": a["page_table"].reshape(1, -1).astype(np.int32), "c32": c32, "c16": c16,
    }


def build(nc, arrays, totals):
    d = {n: nc.dram_tensor(f"in_{n}", v.shape, mybir.dt.from_np(v.dtype), kind="ExternalInput").ap() for n, v in arrays.items()}
    for n, shape in _SHAPES:
        d[n] = nc.dram_tensor(f"out_{n}", shape, F32, kind="ExternalOutput").ap()
    program(nc, totals, d)


def kernel(**inputs):
    import concourse.bacc as bacc
    from concourse.bass_utils import run_bass_kernel_spmd
    arrays = {n: np.ascontiguousarray(v) for n, v in layout({n: np.asarray(v) for n, v in inputs.items()}).items()}
    totals = {}
    for _ in range(2):
        nc = bacc.Bacc("TRN2", target_bir_lowering=False, num_devices=1)
        build(nc, arrays, totals)
    r = run_bass_kernel_spmd(nc, [{f"in_{n}": v for n, v in arrays.items()}], core_ids=[0]).results[0]
    o = {n: r[f"out_{n}"] for n, _ in _SHAPES}
    return (o["yp"].reshape(1, 4 * P, D), o["ys"].reshape(NB, NS, D), o["kp"].reshape(L, 1, 4 * P, H, 2 * DK),
            o["vp"].reshape(L, 1, 4 * P, H, DV), o["ks"].reshape(L, NB, NS, H, 2 * DK), o["vs"].reshape(L, NB, NS, H, DV),
            o["cvs"].reshape(L, NB, NS, HA * DHA))
```

```python
import math
from contextlib import ExitStack, contextmanager

import numpy as np
import concourse.bass as bass
from concourse import mybir

ALU = mybir.AluOpType
ACT = mybir.ActivationFunctionType
AX = mybir.AxisListType
F32 = mybir.dt.float32
BF16 = mybir.dt.bfloat16

P = 128
L = 2
D = 1024
KD = D // P
NT = 5
TP = 4
TOK = NT * P
NB, NS = 8, 8
NROW = NB * NS
H = 4
DK, DV = 64, 128
HA, DHA = 8, 64
PAGES = 2
NPOOL = 20
E, G, EG = 16, 4, 4
DE = 256
EPS = 1e-6
SCALE = DK ** -0.5
W = 512
HALF = KD // 2
PIECE = HALF * W
RING = 6
N_IN = 10
N_OUT = 4
N_DENSE = N_IN + N_OUT
PER_EXPERT = 3
W_LAYER = N_DENSE + E * PER_EXPERT
EXTRA = 2 * (TP * P + NROW) // P - 1
EXTRA += EXTRA % 2
PER_LAYER = W_LAYER + EXTRA * PER_EXPERT
SKIP = 65536.0
CREDIT = 8

_PAR = [("g1", KD), ("g2", KD), ("qn", 1), ("on", 1), ("keep", 1), ("init", 1), ("kn", DK), ("av", W),
        ("lam", 4 * DK), ("bs", 4 * P), ("router", KD * 20)]
PAR = {}
_at = 0
for _n, _w in _PAR:
    PAR[_n] = slice(_at, _at + _w)
    _at += _w
NPAR = _at
C_ID, C_CAUSAL, C_BATCH, C_SPREAD, C_FIRST = (slice(i * P, (i + 1) * P) for i in range(5))
NC32 = 8 * P + NT * 4 + 24
C_TRI = slice(5 * P, 7 * P)
C_IOTA = slice(7 * P, 8 * P)
C_ROWS = slice(8 * P, 8 * P + NT * 4)
C_SLOTS = slice(8 * P + NT * 4, 8 * P + NT * 4 + 24)
C_MAP0, C_MAP1 = slice(4 * P + 16, 4 * P + 17), slice(4 * P + 17, 4 * P + 18)
B_ID, B_CAUSAL = slice(0, P), slice(P, 2 * P)
B_SAMPLE = slice(2 * P, 2 * P + NB * NROW)
B_ONES, B_BEFORE = (slice(2 * P + NB * NROW + i * P, 2 * P + NB * NROW + (i + 1) * P) for i in range(2))
NC16 = 4 * P + NB * NROW


class Count:

    loops = []
    every = []

    def __init__(self, sem, name, totals, start=0, answers=None):
        self.sem, self.name, self.totals = sem, name, totals
        self.local, self.where = start, totals.setdefault(("where", name), {})
        self.answers, self.begin = answers, start
        Count.every.append(self)

    def step(self, loop):
        if self.answers:
            return self.answers.step(loop)
        return self.totals.get((self.name, loop), 0)

    def inc(self, *label, by=1):
        self.local += by
        self.where[label] = (self.local, tuple(n for n, _, _ in Count.loops))
        return self.sem, by

    def value(self, local, names):
        active = {n: i for n, i, _ in Count.loops}
        out = local
        for n in names:
            if self.step(n):
                out = (active[n] if n in active else TURNS[n] - 1) * self.step(n) + out
        return out

    def at(self, *label, less=0):
        local, names = (self.answers or self).where.get(label, (1 + less, ()))
        return self.sem, self.value(local - less + (self.begin if self.answers else 0), names)

    def now(self, more=0):
        return self.value(self.local + more, [n for n, _, _ in Count.loops])


TURNS = {"layer": L, "extra": EXTRA // 2}


def only_if(eng, cond, body, arrivals=(), uncounted=()):
    before = {c: c.local for c in Count.every}
    with eng.If(cond):
        body()
    after = {c: c.local for c in Count.every}
    with eng.Else():
        for c in before:
            c.local = before[c]
        if not arrivals:
            eng.drain()
        for c in before:
            if after[c] != before[c] and c not in uncounted:
                if c in arrivals:
                    eng.wait_ge(c.sem, c.now())
                eng.sem_inc(c.sem, after[c] - before[c])
                c.local = after[c]
    eng.nop()


@contextmanager
def turns(eng, name):
    before = {c: c.local for c in Count.every}
    with eng.Fori(0, TURNS[name]) as i:
        Count.loops.append((name, i, TURNS[name]))
        yield i
        Count.loops.pop()
    for c in Count.every:
        if c in before and c.local != before[c]:
            c.totals[(c.name, name)] = c.local - before[c]
            c.local = before[c] + TURNS[name] * (c.local - before[c])


def program(nc, totals, d):
    Count.loops, Count.every = [], []
    with ExitStack() as ctx:
        def sb(name, shape, dt=F32):
            return ctx.enter_context(nc.sbuf_tensor(name, shape, dt))

        def count(name, start=0, answers=None):
            return Count(ctx.enter_context(nc.semaphore(name)), name, totals, start, answers)

        h_rows = nc.dram_tensor("h_rows", [TOK, D], F32).ap()
        y_rows = nc.dram_tensor("y_rows", [2 * TOK, D], F32).ap()
        x = sb("x", [P, NT, D])
        ring = sb("ring", [P, RING, PIECE])
        hT_cols = sb("hT", [P, KD * TOK])
        hT = hT_cols[:, :].rearrange("p (k t) -> p k t", k=KD)
        e_sb = hT_cols[:, 0:2048].rearrange("p (b m k) -> p b m k", b=2, m=2)
        a_sb = hT_cols[:, 2048:3072].rearrange("p (b k) -> p b k", b=2)
        aT = hT_cols[:, 3072:4096].rearrange("p (b j k) -> p b j k", b=2, j=4)
        es = hT_cols[:, 4096:4096 + 640].rearrange("p (b k) -> p b k", b=2)
        aTs = hT_cols[:, 4736:4736 + 384].rearrange("p (b j k) -> p b j k", b=2, j=3)
        cat_cols = sb("cat", [P, KD * TOK])
        catT = cat_cols[:, :].rearrange("p (k t) -> p k t", k=KD)
        qz = cat_cols[:, 4 * TOK:8 * TOK].rearrange("p (t n) -> p t n", t=NT)
        hn = sb("hn", [P, 2, D])
        qS = hn[:, :, :].rearrange("p a (b h r) -> p (a b) h r", b=4, h=H)
        kva = sb("kva", [P, NT, W])
        v = sb("v", [P, NT, W])
        qk = sb("qk", [P, 2 * H * TOK])
        qT, kT = (qk[:, i * H * TOK:(i + 1) * H * TOK].rearrange("p (h t) -> p h t", h=H) for i in range(2))
        hn2 = qk[:, :].rearrange("p (t n) -> p t n", t=NT)
        par = sb("par", [P, NPAR])
        ws = sb("ws", [P, HA, P])
        wsS = hT_cols[:, 0:HA * P].rearrange("p (h t) -> p h t", h=HA)
        kc = sb("kc", [P, 2, H, PAGES * P])
        vc = sb("vc", [P, 2, PAGES, W])
        sqj = sb("sqj", [P, 2, W])
        tmp = sb("tmp", [P, W])
        o_sb = sb("o_sb", [P, 2, W])
        oT = sb("oT", [P, H, P])
        c32 = sb("c32", [P, NC32])
        c16 = sb("c16", [P, NC16], BF16)
        st = sb("st", [P, 640])
        lg = sb("lg", [P, NT, 20])
        cmpA = cat_cols[:, 0:NT * E * EG].rearrange("p (n j) -> p n j", j=EG)
        cmpB = cat_cols[:, 512:512 + NT * E * EG].rearrange("p (n j) -> p n j", j=EG)
        sil = cat_cols[:, 1024:1536].rearrange("p (b f) -> p b f", b=2)
        act_sb = cat_cols[:, 1536:2048].rearrange("p (b f) -> p b f", b=2)
        actT = cat_cols[:, 2048:2560].rearrange("p (b f t) -> p b f t", b=2, f=2)
        onehot = cat_cols[:, 2560:3840].bitcast(BF16).rearrange("p (b t s) -> p b t s", b=4, t=NT)
        hs = hT_cols[:, 0:2 * D].rearrange("p (b n) -> p b n", b=2)
        hsT = hT_cols[:, 2 * D:4 * D].rearrange("p (b k t) -> p b k t", b=2, k=KD)
        both = hT_cols[:, 0:4 * D].rearrange("p (b a n) -> p b a n", b=2, a=2)
        y_sb = hn
        rows_of = sb("rows_of", [P, NT, E, 4], BF16)
        rows_ofx = sb("rows_ofx", [P, EXTRA, NT, 4], BF16)
        M = sb("M", [P, NT * E], BF16)
        placed = cat_cols[:, 3840:4240].rearrange("p (i n) -> p i n", i=5)
        gates = cat_cols[:, 4240:4320].rearrange("p (t e) -> p t e", t=NT)
        igat = sb("igat", [P, E + EXTRA], mybir.dt.uint32)
        isca = sb("isca", [P, E + EXTRA], mybir.dt.uint32)
        icur = sb("icur", [P, 2, 2], mybir.dt.uint32)
        flags = sb("flags", [P, 16], mybir.dt.int32)
        half = sb("half", [P, 64])
        pages = sb("pages", [1, NB * PAGES], mybir.dt.int32)
        ps = ctx.enter_context(nc.psum_tensor("ps", [P, 8, 512], F32))

        stat = {}
        used = 0
        for name, w in [("ss", NT), ("rs", NT), ("ssk", 8 * NT), ("rsk", 8 * NT), ("ssa", NT), ("rsa", NT),
                        ("sso", 4 * NT), ("rso", 4 * NT), ("mx", 8), ("nb", 8), ("sm", 16), ("co", 8), ("r0", 8),
                        ("mxs", 4), ("nbs", 4), ("sms", 4), ("lam", 4), ("gm", 5), ("gs", 5), ("gw", 5),
                        ("rank", 20), ("goh", 20), ("em", 20), ("es", 20), ("sel", 80), ("ex", 80), ("ms", 8), ("rowf", 1), ("gAB", 10), ("cnt", 16), ("nov", 16), ("ovb", 16), ("vt", 5)]:
            stat[name] = st[:, used:used + w]
            used += w
        assert used <= 640

        ident, identb = c32[:, C_ID], c16[:, B_ID]

        FIRST = {"S0": 0, "J": 1, "T0": 2, "T1": 3, "S1": 4, "I": 5, "O": 6}
        full = {u: count(f"full_{u}") for u in FIRST}
        read = {u: count(f"read_{u}", 1, full[u]) for u in FIRST}

        def bank(u, k=0):
            return ps[:, FIRST[u] + k, :]

        landed = [count(f"landed_{s}") for s in range(RING)]
        piece_used = count("piece_used", CREDIT)
        x_in, c_in = count("x_in"), count("c_in")
        par_in, ws_in = count("par_in"), count("ws_in")
        kv_in = [count(f"kv_in{b}") for b in range(2)]
        kv_used = count("kv_used", 2)
        pages_in = count("pages_in")
        k_stored, va_stored, v_stored, stored = count("k_stored"), count("va_stored"), count("v_stored"), count("stored")
        act_s, dve_s, pool_s = count("act_s"), count("dve_s"), count("pool_s")
        dve_c, pool_c = count("dve_c"), count("pool_c")
        pool_passed = ctx.enter_context(nc.semaphore("pool_passed"))
        x_ready = count("x_ready", NT)
        h_stored = count("h_stored")
        hs_in = [count(f"hs_in{b}") for b in range(2)]
        hs_used = [count(f"hs_used{b}", 1) for b in range(2)]
        y_out = [count(f"y_out{b}") for b in range(2)]
        hs_inx = [count(f"hs_inx{b}") for b in range(2)]
        y_outx = [count(f"y_outx{b}") for b in range(2)]
        y_in = [count(f"y_in{b}") for b in range(2)]
        passed = {e: ctx.enter_context(nc.semaphore(f"passed_{e}")) for e in ("sp", "act", "dve", "pe")}

        x_in_ready = (x_in.sem, 16 * NT)

        block = ctx.enter_context(nc.Block())

        GROUPS = [range(0, 2), range(2, 4), range(4, 8), range(8, 12), range(12, 16)]
        GROUPS += [range(E + 4 * i, E + 4 * i + 4) for i in range(EXTRA // 4)]

        UP_AT = [N_DENSE + max(3 * n - 1, 0) for n in range(E)]
        DOWN_AT = [min(N_DENSE + 3 * n + 4, W_LAYER - 1) for n in range(E)]
        PIECE_AT = list(range(W_LAYER))
        for n in range(E):
            PIECE_AT[UP_AT[n]], PIECE_AT[UP_AT[n] + 1], PIECE_AT[DOWN_AT[n]] = (N_DENSE + PER_EXPERT * n + j for j in range(3))
        assert sorted(PIECE_AT) == list(range(W_LAYER))

        SLOT = [i % RING for i in range(PER_LAYER)]

        def extra_slots(eng, name):
            eng.wait_ge(*dve_s.at("flags"))
            eng.sem_inc(passed[name], 1)
            return eng.value_load(flags[0:1, 0:1], min_val=0, max_val=EXTRA)

        @block.sync
        def _(sp):
            for c in [*read.values(), piece_used, kv_used, x_ready, *hs_used]:
                sp.sem_inc(c.sem, c.begin)
            for t in range(TP):
                sp.dma_start(x[:, t, :], d["xp"][t * P:(t + 1) * P, :]).then_inc(*x_in.inc(by=16))
            sp.dma_start(x[0:NROW, TP, :], d["xs"]).then_inc(*x_in.inc(by=16))
            sp.dma_start(c32[:, :], d["c32"]).then_inc(*c_in.inc(by=16))
            sp.dma_start(cat_cols[:, 0:NC16], d["c16"]).then_inc(*c_in.inc(by=16))
            with turns(sp, "layer") as l:
                for i in range(W_LAYER):
                    back = (i - RING if i >= RING else i - 1 if i < PER_LAYER % RING else i - 7)
                    sp.wait_ge(piece_used.sem, l * PER_LAYER + (back + (1 if i >= RING else 0) + CREDIT))
                    sp.dma_start(ring[:, SLOT[i], :], d["w"][bass.DynSlice(l * W_LAYER + PIECE_AT[i], 1), :, :].rearrange("a p n -> (a p) n")
                                 ).then_inc(*landed[SLOT[i]].inc("w", i, by=16))
                n_extra = extra_slots(sp, "sp")
                with turns(sp, "extra") as q:
                    for b in range(2):
                        def load():
                            e = sp.value_load(flags[0:1, bass.DynSlice(q * 2 + (1 + b), 1)], min_val=0, max_val=E - 1)
                            for j in range(PER_EXPERT):
                                i = W_LAYER + b * PER_EXPERT + j
                                sp.wait_ge(piece_used.sem, l * PER_LAYER + q * (2 * PER_EXPERT) + (i - RING + 1 + CREDIT))
                                sp.dma_start(ring[:, SLOT[i], :],
                                             d["w"][bass.DynSlice(l * W_LAYER + e * PER_EXPERT + (N_DENSE + j), 1), :, :].rearrange("a p n -> (a p) n")
                                             ).then_inc(*landed[SLOT[i]].inc("w", i, by=16))
                        only_if(sp, n_extra > q * 2 + b, load, arrivals=landed)
            sp.wait_ge(x_ready.sem, (L + 1) * NT)
            for t in range(TP):
                sp.dma_start(d["yp"][t * P:(t + 1) * P, :], x[:, t, :]).then_inc(*stored.inc(by=16))
            sp.dma_start(d["ys"], x[0:NROW, TP, :]).then_inc(*stored.inc(by=16))
            sp.wait_ge(stored.sem, stored.now())
            sp.wait_ge(*v_stored.at("v"))
            sp.wait_ge(*va_stored.at("va"))
            sp.wait_ge(*k_stored.at("k"))

        @block.gpsimd
        def _(pool):
            nc.gpsimd.memset(half[:, :], -0.5).then_inc(*pool_c.inc())
            pool.dma_start(pages[:, :], d["pages"]).then_inc(*pages_in.inc(by=16))
            pool.wait_ge(pages_in.sem, 16)

            def wait(sem, value):
                pool.wait_ge(sem, value)
                pool.sem_inc(pool_passed, 1)

            def rsqrt(dst, src, n, size, label):
                if Count.loops:
                    wait(pool_c.sem, pool_c.now())
                nc.gpsimd.tensor_scalar(stat["ms"][:, 0:n], src, 1.0 / size, EPS, ALU.mult, ALU.add).then_inc(*pool_c.inc())
                wait(pool_c.sem, pool_c.now())
                nc.gpsimd.tensor_tensor(dst, stat["ms"][:, 0:n], half[:, 0:n], ALU.pow).then_inc(*pool_c.inc(*label))

            def kv_load(b, l):
                wait(kv_used.sem, kv_used_value(b))
                for g in range(PAGES):
                    page = pool.value_load(pages[0:1, b * PAGES + g:b * PAGES + g + 1], min_val=0, max_val=NPOOL - 1)
                    row = bass.DynSlice(l * NPOOL + page, 1)
                    pool.dma_start(kc[:, b % 2, :, g * P:(g + 1) * P], d["ck"][row, :, :, :].rearrange("a p h t -> (a p) h t")
                                   ).then_inc(*kv_in[b % 2].inc("kv", b, by=16))
                    pool.dma_start(vc[:, b % 2, g, :], d["cv"][row, :, :].rearrange("a p n -> (a p) n")
                                   ).then_inc(*kv_in[b % 2].inc("kv", b, by=16))

            def kv_used_value(b):
                return Count.loops[0][1] * NB + (b + 1) if b < 2 else Count.loops[0][1] * NB + (b - 2 + 1 + 2)

            with turns(pool, "layer") as l:
                wait(x_ready.sem, l * NT + 1)
                pool.dma_start(par[:, :], d["par"][bass.DynSlice(l, 1), :, :].rearrange("a p n -> (a p) n")).then_inc(*par_in.inc("par", by=16))
                pool.dma_start(ws[:, :, :], d["ws"][bass.DynSlice(l, 1), :, :, :].rearrange("a p h t -> (a p) h t")).then_inc(*ws_in.inc("ws", by=16))
                kv_load(0, l)
                kv_load(1, l)
                for t in range(NT):
                    wait(*act_s.at("ss1", t))
                    rsqrt(stat["rs"][:, t:t + 1], stat["ss"][:, t:t + 1], 1, D, ("rs1", t))
                for t in range(NT):
                    wait(*dve_s.at("ssk", t))
                    rsqrt(stat["rsk"][:, 8 * t:8 * t + 8], stat["ssk"][:, 8 * t:8 * t + 8], 8, DK, ("rsk", t))
                wait(*dve_s.at("k", NT - 1))
                pool.dma_start(d["kp"][bass.DynSlice(l, 1), :, :, :].rearrange("a t p n -> (a p) t n"), kva[:, 0:TP, :]).then_inc(*k_stored.inc(by=16))
                pool.dma_start(d["ks"][bass.DynSlice(l, 1), :, :].rearrange("a p n -> (a p) n"), kva[0:NROW, TP, :]).then_inc(*k_stored.inc("k", by=16))
                for t in (TP - 1, TP):
                    wait(*read[f"S{t % 2}"].at("z", "v", t))
                pool.dma_start(d["vp"][bass.DynSlice(l, 1), :, :, :].rearrange("a t p n -> (a p) t n"), v[:, 0:TP, :]).then_inc(*v_stored.inc(by=16))
                pool.dma_start(d["vs"][bass.DynSlice(l, 1), :, :].rearrange("a p n -> (a p) n"), v[0:NROW, TP, :]).then_inc(*v_stored.inc("v", by=16))
                for t in range(NT):
                    wait(*dve_s.at("ssq", t))
                    rsqrt(stat["rsk"][:, 8 * t:8 * t + 8], stat["ssk"][:, 8 * t:8 * t + 8], 8, DK, ("rsq", t))
                for t in range(NT):
                    wait(*act_s.at("ssa", t))
                    rsqrt(stat["rsa"][:, t:t + 1], stat["ssa"][:, t:t + 1], 1, W, ("rsa", t))
                wait(*dve_s.at("va", NT - 1))
                pool.dma_start(d["cvs"][bass.DynSlice(l, 1), :, :].rearrange("a p n -> (a p) n"), kva[0:NROW, TP, :]).then_inc(*va_stored.inc("va", by=16))
                for t in range(NT):
                    if t == TP:
                        for b in range(2, NB):
                            kv_load(b, l)
                    wait(*dve_s.at("sso", t))
                    rsqrt(stat["rso"][:, 4 * t:4 * t + 4], stat["sso"][:, 4 * t:4 * t + 4], 4, DV, ("rso", t))
                for t in range(NT):
                    wait(*act_s.at("ss2", t))
                    rsqrt(stat["rs"][:, t:t + 1], stat["ss"][:, t:t + 1], 1, D, ("rs2", t))

                def gather(b, index, key, landed):
                    wait(*hs_used[b].at("tr", *key, less=1))
                    pool.indirect_dma_start(hs[:, b, :], None, h_rows, bass.IndirectOffsetOnAxis(index, 0),
                                            bounds_check=TOK - 1, oob_is_err=False).then_inc(*landed.inc("hs", *key, by=16))

                def scatter(b, index, key, landed):
                    wait(*read["O"].at("down", *key))
                    pool.indirect_dma_start(y_rows, bass.IndirectOffsetOnAxis(index, 0), y_sb[:, b, :], None,
                                            bounds_check=2 * TOK - 1, oob_is_err=False).then_inc(*landed.inc("y", *key, by=16))

                wait(*h_stored.at("h", NT - 1))
                for n in range(E):
                    for m in ([0, 1] if n == 0 else []) + ([n + 2] if n + 2 < E else []):
                        wait(*dve_s.at("idx", min(g for g, es in enumerate(GROUPS) if m in es)))
                        gather(m % 2, igat[:, m:m + 1], ("m", m), hs_in[m % 2])
                    scatter(n % 2, isca[:, n:n + 1], ("m", n), y_out[n % 2])
                wait(*dve_s.at("flags"))
                wait(*dve_s.at("idx", len(GROUPS) - 1))
                n_extra = pool.value_load(flags[0:1, 0:1], min_val=0, max_val=EXTRA)
                with turns(pool, "extra") as q:
                    for b in range(2):
                        def move():
                            at = bass.DynSlice(q * 2 + (E + b), 1)
                            nc.gpsimd.tensor_copy(icur[:, b, 0:1], igat[:, at]).then_inc(*pool_c.inc())
                            nc.gpsimd.tensor_copy(icur[:, b, 1:2], isca[:, at]).then_inc(*pool_c.inc())
                            wait(pool_c.sem, pool_c.now())
                            gather(b, icur[:, b, 0:1], ("x", b), hs_inx[b])
                            scatter(b, icur[:, b, 1:2], ("x", b), y_outx[b])
                        only_if(pool, n_extra > q * 2 + b, move, uncounted=[*hs_inx, *y_outx])

        ATT = [(i, h) for i in range(TP) for h in range(H)]

        @block.tensor
        def _(pe):
            pending = []

            def mm(out, lhsT, rhs, start=True, stop=True, inc=None, tr=False, loose=False):
                if tr:
                    ins = pe.transpose(out, lhsT, rhs)
                else:
                    ins = pe.matmul(out, lhsT, rhs, start=start, stop=stop, skip_group_check=loose)
                if inc:
                    ins.then_inc(*inc)
                elif pending:
                    c, label = pending.pop(0)
                    ins.then_inc(*c.inc(*label))

            def claim(u):
                pe.wait_ge(read[u].sem, full[u].now(1))

            def turn_rows(stage, t, ready):
                rows = hn2[:, t, :] if stage == "h2" else hn[:, t % 2, :]
                pe.wait_ge(*ready)
                for hf in range(2):
                    u = f"T{hf}"
                    claim(u)
                    for j in range(HALF):
                        k = hf * HALF + j
                        mm(bank(u)[:, j * P:(j + 1) * P], rows[:, k * P:(k + 1) * P], ident, tr=True,
                           inc=full[u].inc(stage, t, hf) if j == HALF - 1 else None)

            gathered = [pe.alloc_register(f"gathered{b}") for b in range(2)]
            for reg in gathered:
                pe.reg_mov(reg, 0)
            pe.wait_ge(c_in.sem, 32)
            pe.wait_ge(dve_s.sem, 1)
            with turns(pe, "layer"):
                for t in range(NT):
                    turn_rows("h1", t, dve_s.at("hn1", t))

                def arrived(i):
                    pe.wait_ge(*landed[SLOT[i]].at("w", i))

                def rows(name, c):
                    for t in range(NT):
                        u = f"S{t % 2}"
                        claim(u)
                        if c == 0:
                            for hf in range(2):
                                pe.wait_ge(*read[f"T{hf}"].at("h1", t, hf))
                        for k in range(KD):
                            if t == 0 and k % HALF == 0:
                                arrived(2 * c + k // HALF)
                            mm(bank(u), hT[:, k, t * P:(t + 1) * P], ring[:, SLOT[2 * c + k // HALF], (k % HALF) * W:(k % HALF + 1) * W],
                               start=(k == 0), stop=(k == KD - 1),
                               inc=full[u].inc("z", name, t) if k == KD - 1 else None)
                            if t == NT - 1 and k % HALF == HALF - 1:
                                pending.append((piece_used, ()))

                def turn_heads(name, src, ready):
                    for t in range(NT):
                        pe.wait_ge(*ready(t))
                        u = f"T{t % 2}"
                        claim(u)
                        for h in range(H):
                            mm(bank(u)[:, h * P:(h + 1) * P], src[:, t, h * P:(h + 1) * P], ident, tr=True,
                               inc=full[u].inc(name, t) if h == H - 1 else None)

                rows("k", 0)
                rows("v", 1)
                rows("q", 2)
                turn_heads("kT", kva, lambda t: dve_s.at("k", t))
                rows("va", 3)
                turn_heads("qT", qz, lambda t: dve_s.at("q", t))
                for m in range(4):
                    for part, (a, b) in enumerate([(0, W), (W, TOK)]):
                        u = f"S{part}"
                        claim(u)
                        for k in range(KD):
                            if m == 0 and part == 0 and k % HALF == 0:
                                arrived(8 + k // HALF)
                            mm(bank(u)[:, 0:b - a], ring[:, SLOT[8 + k // HALF], (k % HALF) * W + m * P:(k % HALF) * W + (m + 1) * P],
                               hT[:, k, a:b], start=(k == 0), stop=(k == KD - 1),
                               inc=full[u].inc("u", m, part) if k == KD - 1 else None)
                            if m == 3 and part == 1 and k % HALF == HALF - 1:
                                pending.append((piece_used, ()))
                pe.wait_ge(*dve_s.at("ws"))
                claim("O")
                mm(bank("O")[:, 0:HA * NS].rearrange("p (h t) -> p h t", h=HA), c32[0:NS, C_SPREAD], ws[0:NS, :, 0:NS], inc=full["O"].inc("wsS"))
                for t in range(NT):
                    u = f"S{t % 2}"
                    claim(u)
                    pe.wait_ge(*dve_s.at("va", t))
                    if t == TP:
                        pe.wait_ge(*read["O"].at("wsS"))
                    for h in range(HA):
                        r = (h % 2) * DHA
                        mm(bank(u)[r:r + DHA, (h // 2) * P:(h // 2 + 1) * P], kva[:, t, h * DHA:(h + 1) * DHA],
                           (wsS if t == TP else ws)[:, h, :], inc=full[u].inc("mix", t) if h == HA - 1 else None)

                def scores(n):
                    i, h = ATT[n]
                    u = f"S{n % 2}"
                    claim(u)
                    if n == 0:
                        for t in (TP - 1, TP):
                            pe.wait_ge(*read[f"T{t % 2}"].at("qT", t))
                    for m in range(2):
                        mm(bank(u, m)[:, 0:(i + 1) * P], qT[m * DK:(m + 1) * DK, h, i * P:(i + 1) * P],
                           kT[m * DK:(m + 1) * DK, h, 0:(i + 1) * P])
                        mm(bank(u, m)[:, i * P:(i + 1) * P], identb, c16[:, B_CAUSAL], start=False, loose=True,
                           inc=full[u].inc("s", n) if m == 1 else None)

                def turn_probs(n):
                    i, h = ATT[n]
                    pe.wait_ge(*dve_s.at("a", n))
                    u = f"T{n % 2}"
                    claim(u)
                    for j in range(i + 1):
                        mm(bank(u)[:, j * P:(j + 1) * P], a_sb[:, n % 2, j * P:(j + 1) * P], ident, tr=True,
                           inc=full[u].inc("aT", n) if j == i else None)

                def weigh(n):
                    i, h = ATT[n]
                    if h == 0:
                        claim("O")
                    pe.wait_ge(*read[f"T{n % 2}"].at("aT", n))
                    for j in range(i + 1):
                        mm(bank("O")[:, h * DV:(h + 1) * DV], aT[:, n % 2, j, :], v[:, j, h * DV:(h + 1) * DV],
                           start=(j == 0), stop=(j == i), inc=full["O"].inc("o", i) if (h == H - 1 and j == i) else None)

                def turn_out(t):
                    pe.wait_ge(*dve_s.at("o", t))
                    u = f"T{t % 2}"
                    claim(u)
                    for h in range(H):
                        mm(bank(u)[:, h * P:(h + 1) * P], o_sb[:, t % 2, h * P:(h + 1) * P], ident, tr=True,
                           inc=full[u].inc("oT", t) if h == H - 1 else None)

                for n in range(len(ATT) + 2):
                    if n < len(ATT):
                        scores(n)
                    if 1 <= n <= len(ATT):
                        turn_probs(n - 1)
                    if n >= 2:
                        weigh(n - 2)
                    if n >= 8 and n % 4 == 0:
                        turn_out(n // 4 - 2)

                def sample_scores(g):
                    u = f"S{g % 2}"
                    claim(u)
                    for b in (2 * g, 2 * g + 1):
                        r = (b % 2) * 64
                        pe.wait_ge(*kv_in[b % 2].at("kv", b))
                        for h in range(H):
                            mm(bank(u)[r:r + 64, 0:PAGES * P], qS[:, b, h, :], kc[:, b % 2, h, :], start=(h == 0), stop=(h == H - 1))
                        for h in range(H):
                            mm(bank(u)[r:r + 64, PAGES * P:PAGES * P + 64], qS[:, b, h, :], kT[:, h, TP * P:TP * P + 64], start=(h == 0), stop=False)
                        mm(bank(u)[r:r + 64, PAGES * P:PAGES * P + 64], identb[0:64, 0:64],
                           c16[0:64, B_SAMPLE][:, b * 64:(b + 1) * 64], start=False, inc=full[u].inc("ss", g) if b % 2 else None)

                def sample_weigh(g):
                    u = f"T{g % 2}"
                    pe.wait_ge(*dve_s.at("ps", g))
                    claim(u)
                    for j in range(PAGES):
                        mm(bank(u)[:, j * P:(j + 1) * P], es[:, g % 2, j * P:(j + 1) * P], ident, tr=True)
                    mm(bank(u)[0:64, PAGES * P:(PAGES + 1) * P], es[:, g % 2, PAGES * P:PAGES * P + 64], ident, tr=True, inc=full[u].inc("pT", g))
                    if g == 0:
                        claim("O")
                    pe.wait_ge(*read[u].at("pT", g))
                    for b in (2 * g, 2 * g + 1):
                        for h in range(H):
                            c = (b % 2) * 32 + h * NS
                            out = bank("O")[:, h * 64 + b * NS:h * 64 + (b + 1) * NS]
                            for j in range(PAGES):
                                mm(out, vc[:, b % 2, j, h * DV:(h + 1) * DV], aTs[:, g % 2, j, c:c + NS], start=(j == 0), stop=False)
                            last = b == NB - 1 and h == H - 1
                            mm(out, v[0:64, TP, h * DV:(h + 1) * DV], aTs[0:64, g % 2, PAGES, c:c + NS], start=False,
                               inc=full["O"].inc("soT") if last else kv_used.inc() if h == H - 1 else None)
                    if g == 3:
                        pending.append((kv_used, ()))

                pe.wait_ge(*dve_s.at("qS"))
                for g in range(4):
                    sample_scores(g)
                    sample_weigh(g)
                    if g == 0:
                        turn_out(3)
                claim("O")
                pe.wait_ge(*read["O"].at("soT"))
                for h in range(H):
                    mm(bank("O")[:, h * P:(h + 1) * P], oT[:, h, :], ident, tr=True, inc=full["O"].inc("o", TP) if h == H - 1 else None)
                turn_out(TP)

                for n in range(2):
                    for t in range(NT):
                        u = f"S{(n * NT + t) % 2}"
                        claim(u)
                        if n == 0:
                            pe.wait_ge(*dve_s.at("mix", t))
                            pe.wait_ge(*read[f"T{t % 2}"].at("oT", t))
                        for k in range(KD):
                            i = N_IN + 2 * n + k // HALF
                            if t == 0 and k % HALF == 0:
                                arrived(i)
                            mm(bank(u), catT[:, k, t * P:(t + 1) * P], ring[:, SLOT[i], (k % HALF) * W:(k % HALF + 1) * W],
                               start=(k == 0), stop=(k == KD - 1), inc=full[u].inc("y", n, t) if k == KD - 1 else None)
                            if t == NT - 1 and k % HALF == HALF - 1:
                                pending.append((piece_used, ()))

                for t in range(NT):
                    turn_rows("h2", t, dve_s.at("hn2", t))
                claim("O")
                for t in range(NT):
                    for hf in range(2):
                        pe.wait_ge(*read[f"T{hf}"].at("h2", t, hf))
                    for k in range(KD):
                        mm(bank("O")[:, t * 20:(t + 1) * 20], hT[:, k, t * P:(t + 1) * P], par[:, PAR["router"]][:, k * 20:(k + 1) * 20],
                           start=(k == 0), stop=(k == KD - 1), inc=full["O"].inc("logits") if (t == NT - 1 and k == KD - 1) else None)

                pe.wait_ge(*dve_s.at("M"))
                claim("I")
                for t in range(NT + 1):
                    for j in range(min(t + 1, NT)):
                        mm(bank("I")[:, t * E:(t + 1) * E], c16[:, B_BEFORE if j == t else B_ONES], M[:, j * E:(j + 1) * E],
                           start=(j == 0), stop=(j == min(t, NT - 1)), inc=full["I"].inc("ranks") if (t == NT and j == NT - 1) else None)

                def index_rows(g):
                    pe.wait_ge(*dve_s.at("onehot", g))
                    claim("I")
                    for n, s in enumerate(GROUPS[g]):
                        for t in range(NT):
                            mm(bank("I")[:, n * 4:n * 4 + 4], onehot[:, s % 4, t, :], rows_of[:, t, s, :] if s < E else rows_ofx[:, s - E, t, :],
                               start=(t == 0), stop=(t == NT - 1), inc=full["I"].inc("idx", g) if (n == len(GROUPS[g]) - 1 and t == NT - 1) else None)

                def turn_in(b, key, arrival):
                    pe.wait_ge(*arrival)
                    for hf in range(2):
                        u = f"T{hf}"
                        claim(u)
                        for j in range(HALF):
                            k = hf * HALF + j
                            mm(bank(u)[:, j * P:(j + 1) * P], hs[:, b, k * P:(k + 1) * P], ident, tr=True,
                               inc=full[u].inc("tr", *key, hf) if j == HALF - 1 else None)
                    pending.append((hs_used[b], ("tr", *key)))

                def up(b, key, hf, i):
                    u = f"S{b}"
                    if hf == 0:
                        claim(u)
                    pe.wait_ge(*read[f"T{hf}"].at("tr", *key, hf))
                    arrived(i + hf)
                    for j in range(HALF):
                        k = hf * HALF + j
                        mm(bank(u), hsT[:, b, k, :], ring[:, SLOT[i + hf], j * W:(j + 1) * W], start=(k == 0), stop=(k == KD - 1),
                           inc=full[u].inc("gu", *key) if k == KD - 1 else None)
                    pending.append((piece_used, ()))

                def turn_act(b, key):
                    pe.wait_ge(*read[f"S{b}"].at("gu", *key))
                    claim("J")
                    for f in range(2):
                        mm(bank("J")[:, f * P:(f + 1) * P], act_sb[:, b, f * P:(f + 1) * P], ident, tr=True,
                           inc=full["J"].inc("actT", *key) if f else None)

                def down(b, key, i):
                    claim("O")
                    pe.wait_ge(*read["J"].at("actT", *key))
                    arrived(i)
                    for c in range(2):
                        for f in range(2):
                            mm(bank("O", c), actT[:, b, f, :], ring[:, SLOT[i], f * D + c * W:f * D + (c + 1) * W], start=(f == 0), stop=(f == 1),
                               inc=full["O"].inc("down", *key) if (c and f) else None)
                    pending.append((piece_used, ()))

                def flush():
                    claim("T0")
                    while pending:
                        mm(bank("T0")[:, 0:P], ident, ident, tr=True)

                for g in range(3):
                    index_rows(g)
                turn_in(0, ("m", 0), hs_in[0].at("hs", "m", 0))
                for n in range(E + 1):
                    b = n % 2
                    if n < E:
                        up(b, ("m", n), 0, UP_AT[n])
                    if n >= 1:
                        turn_act(1 - b, ("m", n - 1))
                    if n < E:
                        up(b, ("m", n), 1, UP_AT[n])
                    if n < 2:
                        index_rows(n + 3)
                    if n in (4, 6):
                        index_rows(n // 2 + 3)
                    if n + 1 < E:
                        turn_in(1 - b, ("m", n + 1), hs_in[1 - b].at("hs", "m", n + 1))
                    if n >= 1:
                        down(1 - b, ("m", n - 1), DOWN_AT[n - 1])
                flush()
                n_extra = extra_slots(pe, "pe")
                with turns(pe, "extra") as q:
                    for b in range(2):
                        def slot():
                            i = W_LAYER + b * PER_EXPERT
                            pe.reg_add(gathered[b], gathered[b], 16)
                            turn_in(b, ("x", b), (hs_inx[b].sem, pe.snap(gathered[b])))
                            up(b, ("x", b), 0, i)
                            up(b, ("x", b), 1, i)
                            turn_act(b, ("x", b))
                            down(b, ("x", b), i + 2)
                            flush()
                        only_if(pe, n_extra > q * 2 + b, slot)

        @block.scalar
        def _(act):
            def square_rows(stage, ready):
                for t in range(NT):
                    act.wait_ge(*ready(t))
                    if t:
                        act.wait_ge(*act_s.at(stage, t - 1))
                    nc.scalar.activation(sqbig, x[:, t, :], ACT.Square, accum_out=stat["ss"][:, t:t + 1]).then_inc(*act_s.inc(stage, t))
                    if stage == "ss2" and t:
                        store_rows(t - 1)
                if stage == "ss2":
                    store_rows(NT - 1)

            def store_rows(t):
                act.wait_ge(*dve_s.at("hn2", t))
                act.dma_start(h_rows[t * P:(t + 1) * P, :], hn2[:, t, :]).then_inc(*h_stored.inc("h", t, by=16))

            sqbig = sqj[:, :, :].rearrange("p a n -> p (a n)")

            act.wait_ge(dve_s.sem, 1)
            scattered = [act.alloc_register(f"scattered{b}") for b in range(2)]
            for reg in scattered:
                act.reg_mov(reg, 0)
            with turns(act, "layer") as l:
                act.wait_ge(*x_in_ready)
                square_rows("ss1", lambda t: (x_ready.sem, l * NT + (t + 1)))
                act.wait_ge(*par_in.at("par"))

                def evacuate(name, dst):
                    for t in range(NT):
                        u = f"S{t % 2}"
                        act.wait_ge(*full[u].at("z", name, t))
                        if name == "va" and t == 0:
                            act.wait_ge(*k_stored.at("k"))
                        if name == "va":
                            act.wait_ge(*full[f"T{t % 2}"].at("kT", t))
                            nc.scalar.activation(dst[:, t, :], bank(u), ACT.Gelu_apprx_tanh).then_inc(*read[u].inc("z", name, t))
                            act.wait_ge(*read[u].at("z", name, t))
                            if t >= 2:
                                act.wait_ge(*act_s.at("ssa", t - 2))
                            nc.scalar.activation(sqj[:, t % 2, :], dst[:, t, :], ACT.Square, accum_out=stat["ssa"][:, t:t + 1]).then_inc(*act_s.inc("ssa", t))
                            continue
                        if name in "kq":
                            if t >= 2:
                                act.wait_ge(*dve_s.at("ss" + name, t - 2))
                            elif name == "q":
                                act.wait_ge(*dve_s.at("ssk", NT - 1))
                            if name == "k" and t < 2:
                                act.wait_ge(*act_s.at("ss1", NT - 1))
                            nc.scalar.activation(sqj[:, t % 2, :], bank(u), ACT.Square).then_inc(*act_s.inc("sq", name, t))
                            nc.scalar.copy(dst[:, t, :], bank(u)).then_inc(*read[u].inc("z", name, t))
                        else:
                            nc.scalar.copy(dst[:, t, :], bank(u)).then_inc(*read[u].inc("z", name, t))

                evacuate("k", kva)
                evacuate("v", v)
                evacuate("q", qz)
                for t in range(NT):
                    act.wait_ge(*full[f"T{t % 2}"].at("kT", t))
                    nc.scalar.copy(kT[:, :, t * P:(t + 1) * P], bank(f"T{t % 2}").rearrange("p (h t) -> p h t", h=H)).then_inc(*read[f"T{t % 2}"].inc("kT", t))
                act.wait_ge(*dve_s.at("ssq", NT - 1))
                evacuate("va", kva)
                for t in range(NT):
                    act.wait_ge(*full[f"T{t % 2}"].at("qT", t))
                    nc.scalar.mul(qT[:, :, t * P:(t + 1) * P], bank(f"T{t % 2}").rearrange("p (h t) -> p h t", h=H), par[:, PAR["qn"]]).then_inc(*read[f"T{t % 2}"].inc("qT", t))
                for m in range(4):
                    for part, (a, b) in enumerate([(0, W), (W, TOK)]):
                        u = f"S{part}"
                        act.wait_ge(*full[u].at("u", m, part))
                        nc.scalar.activation(catT[:, m, a:b], bank(u)[:, 0:b - a], ACT.Gelu_apprx_tanh).then_inc(*read[u].inc("u", m, part))
                act.wait_ge(*dve_s.at("lamdot"))
                nc.scalar.activation(stat["lam"][:, 0:2], stat["lam"][:, 0:2], ACT.Exp).then_inc(*act_s.inc("lamexp"))

                def probs(n):
                    i, h = ATT[n]
                    act.wait_ge(*dve_s.at("nb", n))
                    if n >= 2:
                        act.wait_ge(*dve_s.at("a", n - 2))
                    for m in range(2):
                        c = 2 * (n % 4) + m
                        ins = nc.scalar.activation(e_sb[:, n % 2, m, 0:(i + 1) * P], bank(f"S{n % 2}", m)[:, 0:(i + 1) * P], ACT.Exp,
                                                   bias=stat["nb"][:, c:c + 1], scale=SCALE,
                                                   accum_out=stat["sm"][:, c:c + 1])
                    ins.then_inc(*read[f"S{n % 2}"].inc("s", n))

                def probs_turned(n):
                    i, h = ATT[n]
                    u = f"T{n % 2}"
                    act.wait_ge(*full[u].at("aT", n))
                    nc.scalar.copy(aT[:, n % 2, 0:i + 1, :], bank(u)[:, 0:(i + 1) * P].rearrange("p (j q) -> p j q", q=P)).then_inc(*read[u].inc("aT", n))

                for n in range(len(ATT) + 1):
                    if n < len(ATT):
                        probs(n)
                    if n >= 1:
                        probs_turned(n - 1)
                for g in range(4):
                    u = f"S{g % 2}"
                    act.wait_ge(*dve_s.at("nbs", g))
                    nc.scalar.activation(es[:, g % 2, :], bank(u)[:, 0:320], ACT.Exp, bias=stat["nbs"][:, g:g + 1], scale=SCALE,
                                         accum_out=stat["sms"][:, g:g + 1]).then_inc(*read[u].inc("ss", g))
                act.wait_ge(*full["O"].at("soT"))
                nc.scalar.copy(oT[:, :, 0:64], bank("O")[:, 0:256].rearrange("p (h t) -> p h t", h=H)).then_inc(*read["O"].inc("soT"))

                square_rows("ss2", lambda t: read[f"S{(NT + t) % 2}"].at("y", 1, t))
                act.wait_ge(*dve_s.at("lgsub"))
                nc.scalar.activation(lg[:, :, :], lg[:, :, :], ACT.Exp).then_inc(*act_s.inc("lgexp"))
                def silu(b, key):
                    act.wait_ge(*full[f"S{b}"].at("gu", *key))
                    nc.scalar.activation(sil[:, b, :], bank(f"S{b}")[:, 0:DE], ACT.Silu).then_inc(*act_s.inc("sil", *key))

                def act_turned(b, key):
                    act.wait_ge(*full["J"].at("actT", *key))
                    nc.scalar.copy(actT[:, b, :, :], bank("J")[:, 0:2 * P].rearrange("p (f t) -> p f t", f=2)).then_inc(*read["J"].inc("actT", *key))

                def result(b, key, reused):
                    act.wait_ge(*full["O"].at("down", *key))
                    if reused:
                        act.wait_ge(*y_out[b].at("y", "m", E - 2 + b if key[0] == "x" else key[1] - 2))
                    nc.scalar.copy(y_sb[:, b, :], ps[:, 6:8, :].rearrange("p a n -> p (a n)")).then_inc(*read["O"].inc("down", *key))

                for n in range(E + 1):
                    if n >= 1:
                        act_turned((n - 1) % 2, ("m", n - 1))
                    if n < E:
                        silu(n % 2, ("m", n))
                    if n >= 1:
                        result((n - 1) % 2, ("m", n - 1), n >= 3)
                n_extra = extra_slots(act, "act")
                with turns(act, "extra") as q:
                    for b in range(2):
                        def slot():
                            silu(b, ("x", b))
                            act_turned(b, ("x", b))
                            result(b, ("x", b), True)
                            act.reg_add(scattered[b], scattered[b], 16)
                            act.wait_ge(y_outx[b].sem, act.snap(scattered[b]))
                            act.sem_inc(passed["act"], 1)
                        only_if(act, n_extra > q * 2 + b, slot)
                for t in range(NT):
                    n = NROW if t == TP else P
                    if t == 0:
                        act.wait_ge(*full["O"].at("down", "x", 1))
                        for b in range(2):
                            act.wait_ge(*y_out[b].at("y", "m", E - 2 + b))
                    if t >= 2:
                        act.wait_ge(x_ready.sem, l * NT + (NT + t - 1))
                    for a in range(2):
                        act.dma_start(both[0:n, t % 2, a, :], y_rows[a * TOK + t * P:a * TOK + t * P + n, :]).then_inc(*y_in[t % 2].inc("y", t, by=16))

        @block.vector
        def _(dve):
            vec = nc.vector

            def link(ins):
                ins.then_inc(*dve_c.inc())
                dve.wait_ge(dve_c.sem, dve_c.now())

            vec.memset(x[NROW:P, TP, :], 0.0)
            vec.memset(oT[:, :, :], 0.0)
            dve.wait_ge(c_in.sem, 32)
            vec.tensor_copy(c16[:, :], cat_cols[:, 0:NC16]).then_inc(*dve_s.inc("init"))
            rows = c32[:, C_ROWS].rearrange("p (t c) -> p t c", c=4)
            vec.tensor_copy(rows_of[:, :, :, :], rows.unsqueeze(2).to_broadcast([P, NT, E, 4]))
            vec.tensor_copy(rows_ofx[:, :, :, :], rows.unsqueeze(1).to_broadcast([P, EXTRA, NT, 4]))
            dve.wait_ge(*x_in_ready)

            def norm_rows(stage, stage_r, gain):
                def scaled(t):
                    dve.wait_ge(*pool_c.at(stage_r, t))
                    vec.tensor_scalar(hn2[:, t, :] if stage == "h2" else hn[:, t % 2, :], x[:, t, :], stat["rs"][:, t:t + 1], None, ALU.mult).then_inc(*dve_s.inc("hn" + stage[1], t))

                def turned(t):
                    for hf in range(2):
                        dve.wait_ge(*full[f"T{hf}"].at(stage, t, hf))
                        g = par[:, PAR[gain]][:, hf * HALF:(hf + 1) * HALF].unsqueeze(2).to_broadcast([P, HALF, P])
                        vec.tensor_tensor(hT[:, hf * HALF:(hf + 1) * HALF, t * P:(t + 1) * P],
                                          bank(f"T{hf}").rearrange("p (j t) -> p j t", j=HALF), g, ALU.mult).then_inc(*read[f"T{hf}"].inc(stage, t, hf))

                for t in range(NT + 1):
                    if t < NT:
                        scaled(t)
                    if t >= 1:
                        turned(t - 1)

            def groups(ap, n, w):
                return ap.rearrange("p (n w) -> p n w", n=n)

            def wide(ap, n, w):
                return ap.unsqueeze(2).to_broadcast([P, n, w])

            def across(ap, n, w):
                return ap.unsqueeze(1).to_broadcast([P, n, w])

            with turns(dve, "layer"):
                dve.wait_ge(*par_in.at("par"))
                norm_rows("h1", "rs1", "g1")
                dve.wait_ge(*ws_in.at("ws"))
                vec.tensor_tensor(ws[:, :, :], ws[:, :, :], across(c32[:, C_CAUSAL], HA, P), ALU.mult).then_inc(*dve_s.inc("ws"))
                lam = par[:, PAR["lam"]]
                for i in range(2):
                    link(vec.tensor_tensor(tmp[:, i * DK:(i + 1) * DK], lam[:, 2 * i * DK:(2 * i + 1) * DK], lam[:, (2 * i + 1) * DK:(2 * i + 2) * DK], ALU.mult))
                vec.tensor_reduce(stat["lam"][:, 0:2], groups(tmp[:, 0:2 * DK], 2, DK), AX.X, ALU.add).then_inc(*dve_s.inc("lamdot"))
                link(vec.memset(qS[:, :, :, :], 0.0))

                def sums(name, t):
                    dve.wait_ge(*act_s.at("sq", name, t))
                    if name == "q":
                        dve.wait_ge(dve_c.sem, dve_c.now())
                    vec.tensor_reduce(stat["ssk"][:, 8 * t:8 * t + 8], groups(sqj[:, t % 2, :], 8, DK), AX.X, ALU.add).then_inc(*dve_s.inc("ss" + name, t))

                for t in range(NT):
                    sums("k", t)
                for t in range(NT):
                    dve.wait_ge(*pool_c.at("rsk", t))
                    dve.wait_ge(*read[f"S{t % 2}"].at("z", "k", t))
                    z = groups(kva[:, t, :], 8, DK)
                    link(vec.tensor_tensor(z, z, wide(stat["rsk"][:, 8 * t:8 * t + 8], 8, DK), ALU.mult))
                    vec.tensor_tensor(z, z, across(par[:, PAR["kn"]], 8, DK), ALU.mult).then_inc(*dve_s.inc("k", t))
                for t in range(NT):
                    sums("q", t)
                for t in range(NT):
                    dve.wait_ge(*pool_c.at("rsq", t))
                    dve.wait_ge(*read[f"S{t % 2}"].at("z", "q", t))
                    z = groups(qz[:, t, :], 8, DK)
                    vec.tensor_tensor(z, z, wide(stat["rsk"][:, 8 * t:8 * t + 8], 8, DK), ALU.mult).then_inc(*dve_s.inc("q", t))
                for t in range(NT):
                    dve.wait_ge(*pool_c.at("rsa", t))
                    vec.scalar_tensor_tensor(kva[:, t, :], kva[:, t, :], stat["rsa"][:, t:t + 1], par[:, PAR["av"]],
                                             ALU.mult, ALU.mult).then_inc(*dve_s.inc("va", t))
                dve.wait_ge(*read["T0"].at("qT", TP))
                for h in range(H):
                    for m in range(2):
                        r = slice(m * DK, (m + 1) * DK)
                        c = h * 16 + m * NS
                        ins = vec.tensor_copy(qS[r, :, h, c:c + NS], qT[r, h, TP * P:TP * P + NROW].rearrange("p (b t) -> p b t", b=NB))
                ins.then_inc(*dve_s.inc("qS"))
                dve.wait_ge(*act_s.at("lamexp"))
                link(vec.tensor_tensor(stat["lam"][:, 2:3], stat["lam"][:, 1:2], stat["lam"][:, 0:1], ALU.subtract))
                link(vec.tensor_tensor(stat["lam"][:, 3:4], stat["lam"][:, 2:3], par[:, PAR["init"]], ALU.subtract))
                neglam = stat["lam"][:, 3:4]
                link(vec.scalar_tensor_tensor(stat["rowf"], c32[:, C_MAP1], neglam, c32[:, C_MAP0], ALU.mult, ALU.add))
                dve.wait_ge(*full["O"].at("wsS"))
                vec.tensor_tensor(wsS[:, :, :].rearrange("p h (b t) -> p h b t", t=NS),
                                  bank("O")[:, 0:HA * NS].rearrange("p (h t) -> p h t", h=HA).unsqueeze(2).to_broadcast([P, HA, 16, NS]),
                                  c32[:, C_BATCH].rearrange("p (b t) -> p b t", t=NS).unsqueeze(1).to_broadcast([P, HA, 16, NS]),
                                  ALU.mult).then_inc(*read["O"].inc("wsS"))
                for t in range(NT):
                    u = f"S{t % 2}"
                    dve.wait_ge(*full[u].at("mix", t))
                    if t == 0:
                        dve.wait_ge(*read["S0"].at("u", 3, 0))
                        dve.wait_ge(*read["S1"].at("u", 3, 1))
                    bs = par[:, PAR["bs"]].rearrange("p (c t) -> p c t", c=4)
                    s, o = bank(u), tmp[:, :]
                    if t < TP:
                        s, o = (a.rearrange("p (c t) -> p c t", c=4) for a in (s, o))
                    else:
                        s, o = (a.rearrange("p (c b t) -> p c b t", c=4, t=NS) for a in (s, o))
                        bs = bs[:, :, 0:NS].unsqueeze(2).to_broadcast([P, 4, 16, NS])
                    if t:
                        dve.wait_ge(*dve_s.at("mix", t - 1))
                    vec.tensor_tensor(o, s, bs, ALU.add).then_inc(*read[u].inc("mix", t))
                    dve.wait_ge(*read[u].at("mix", t))
                    vec.tensor_tensor(catT[:, 0:4, t * P:(t + 1) * P], tmp[:, :].rearrange("p (c t) -> p c t", c=4),
                                      catT[:, 0:4, t * P:(t + 1) * P], ALU.mult).then_inc(*dve_s.inc("mix", t))

                def biggest(n):
                    i, h = ATT[n]
                    c = 2 * (n % 4)
                    dve.wait_ge(*full[f"S{n % 2}"].at("s", n))
                    b0 = FIRST[f"S{n % 2}"]
                    link(vec.tensor_reduce(stat["mx"][:, c:c + 2], ps[:, b0:b0 + 2, 0:(i + 1) * P], AX.X, ALU.max))
                    vec.tensor_scalar(stat["nb"][:, c:c + 2], stat["mx"][:, c:c + 2], -SCALE, None, ALU.mult).then_inc(*dve_s.inc("nb", n))

                def combine(n):
                    i, h = ATT[n]
                    c = 2 * (n % 4)
                    dve.wait_ge(*read[f"S{n % 2}"].at("s", n))
                    link(vec.reciprocal(stat["co"][:, 0:2], stat["sm"][:, c:c + 2]))
                    r0 = stat["r0"][:, 4 * (i % 2) + h:4 * (i % 2) + h + 1]
                    vec.tensor_copy(r0, stat["co"][:, 0:1])
                    link(vec.scalar_tensor_tensor(stat["co"][:, 2:3], stat["co"][:, 1:2], neglam, stat["sm"][:, c:c + 1], ALU.mult, ALU.mult))
                    if n >= 2:
                        dve.wait_ge(*full[f"T{n % 2}"].at("aT", n - 2))
                    vec.scalar_tensor_tensor(a_sb[:, n % 2, 0:(i + 1) * P], e_sb[:, n % 2, 1, 0:(i + 1) * P], stat["co"][:, 2:3],
                                             e_sb[:, n % 2, 0, 0:(i + 1) * P], ALU.mult, ALU.add).then_inc(*dve_s.inc("a", n))

                def head_norm(t):
                    dve.wait_ge(*full["O"].at("o", t))
                    o = o_sb[:, t % 2, :]
                    if t < TP:
                        dve.wait_ge(dve_c.sem, dve_c.now())
                        ins = vec.tensor_tensor(groups(o, H, DV), groups(bank("O"), H, DV), wide(stat["r0"][:, 4 * (t % 2):4 * (t % 2) + 4], H, DV), ALU.mult)
                    else:
                        ins = vec.tensor_copy(o, bank("O"))
                    ins.then_inc(*read["O"].inc("o", t))
                    dve.wait_ge(*read["O"].at("o", t))
                    link(vec.tensor_tensor(tmp[:, :], o, o, ALU.mult))
                    vec.tensor_reduce(stat["sso"][:, 4 * t:4 * t + 4], groups(tmp[:, :], H, DV), AX.X, ALU.add).then_inc(*dve_s.inc("sso", t))

                def head_scale(t):
                    o = groups(o_sb[:, t % 2, :], H, DV)
                    dve.wait_ge(*pool_c.at("rso", t))
                    vec.tensor_tensor(o, o, wide(stat["rso"][:, 4 * t:4 * t + 4], H, DV), ALU.mult).then_inc(*dve_s.inc("o", t))

                def head_turned(t):
                    u = f"T{t % 2}"
                    dve.wait_ge(*full[u].at("oT", t))
                    vec.tensor_scalar(catT[:, 4:8, t * P:(t + 1) * P], groups(bank(u), H, P), par[:, PAR["on"]], par[:, PAR["keep"]],
                                      ALU.mult, ALU.mult).then_inc(*read[u].inc("oT", t))

                for n in range(len(ATT) + 1):
                    if n < len(ATT):
                        biggest(n)
                    if n >= 1:
                        combine(n - 1)
                    if n >= 6 and n % 4 == 2:
                        head_norm(n // 4 - 1)
                    if n >= 7 and n % 4 == 3:
                        head_scale(n // 4 - 1)
                    if n >= 9 and n % 4 == 1:
                        head_turned(n // 4 - 2)
                head_turned(2)
                for g in range(4):
                    u = f"S{g % 2}"
                    dve.wait_ge(*full[u].at("ss", g))
                    link(vec.tensor_reduce(stat["mxs"][:, g:g + 1], bank(u)[:, 0:320], AX.X, ALU.max))
                    vec.tensor_scalar(stat["nbs"][:, g:g + 1], stat["mxs"][:, g:g + 1], -SCALE, None, ALU.mult).then_inc(*dve_s.inc("nbs", g))
                    if g == 0:
                        head_norm(3)
                        head_scale(3)
                    dve.wait_ge(*read[u].at("ss", g))
                    link(vec.reciprocal(stat["mxs"][:, g:g + 1], stat["sms"][:, g:g + 1]))
                    vec.tensor_scalar(es[:, g % 2, :], es[:, g % 2, :], stat["mxs"][:, g:g + 1], stat["rowf"], ALU.mult, ALU.mult).then_inc(*dve_s.inc("ps", g))
                    u = f"T{g % 2}"
                    dve.wait_ge(*full[u].at("pT", g))
                    for rows, a, b in ((P, 0, PAGES), (64, PAGES, PAGES + 1)):
                        pt = bank(u)[0:rows, a * P:b * P].rearrange("p (j r m t) -> p j r m t", j=b - a, m=2, t=NS)
                        for j in range(b - a):
                            ins = vec.tensor_reduce(aTs[0:rows, g % 2, a + j, :].rearrange("p (r t) -> p r t", t=NS),
                                                    pt[:, j, :, :, :].rearrange("p r m t -> p r t m"), AX.X, ALU.add)
                            if j == b - a - 1 and a == PAGES:
                                ins.then_inc(*read[u].inc("pT", g))
                            else:
                                link(ins)
                    if g == 0:
                        head_turned(3)
                head_norm(TP)
                head_scale(TP)
                head_turned(TP)

                for n in range(2):
                    for t in range(NT):
                        u = f"S{(n * NT + t) % 2}"
                        dve.wait_ge(*full[u].at("y", n, t))
                        cols = x[:, t, n * W:(n + 1) * W]
                        vec.tensor_tensor(cols, cols, bank(u), ALU.add).then_inc(*read[u].inc("y", n, t))
                norm_rows("h2", "rs2", "g2")

                dve.wait_ge(*full["O"].at("logits"))
                vec.tensor_copy(lg[:, :, :], bank("O")[:, 0:NT * 20].rearrange("p (t n) -> p t n", t=NT)).then_inc(*read["O"].inc("logits"))
                dve.wait_ge(*read["O"].at("logits"))
                lgg, lge = lg[:, :, 0:G], lg[:, :, G:20].rearrange("p t (g j) -> p t g j", g=G)

                def rank(out, cols, n):
                    A, B = cmpA[:, 0:n * EG, :], cmpB[:, 0:n * EG, :]
                    A4, B4 = (a.rearrange("p (n j) i -> p n j i", j=EG) for a in (A, B))
                    vi = cols.unsqueeze(2).to_broadcast([P, n, EG, EG])
                    vj = cols.unsqueeze(3).to_broadcast([P, n, EG, EG])
                    vec.tensor_tensor(A4, vi, vj, ALU.is_gt)
                    link(vec.tensor_tensor(B4, vi, vj, ALU.is_equal))
                    first = c32[:, C_FIRST][:, 0:EG * EG].rearrange("p (j i) -> p j i", j=EG).unsqueeze(1).to_broadcast([P, n, EG, EG])
                    link(vec.tensor_tensor(B4, B4, first, ALU.mult))
                    link(vec.tensor_tensor(A, A, B, ALU.add))
                    link(vec.tensor_reduce(out, A, AX.X, ALU.add))

                link(vec.tensor_copy(stat["goh"].rearrange("p (t g) -> p t g", t=NT), lgg))
                rank(stat["rank"], stat["goh"].rearrange("p (t g) -> p t g", t=NT), NT)
                link(vec.tensor_scalar(stat["goh"], stat["rank"], 0.5, None, ALU.is_lt))
                link(vec.tensor_copy(stat["ex"].rearrange("p (t n) -> p t n", t=NT), lg[:, :, G:20]))
                ex = stat["ex"].rearrange("p (n j) -> p n j", j=EG)
                rank(stat["sel"], ex, NT * G)
                flat = placed[:, :, :]
                selA, selB, R, win, work = (flat[:, i, :] for i in range(5))
                goh4 = wide(stat["goh"], NT * G, EG)
                for sel, op, c in ((selA, ALU.is_lt, 0.5), (selB, ALU.is_equal, 1.0)):
                    link(vec.scalar_tensor_tensor(groups(sel, NT * G, EG), groups(stat["sel"], NT * G, EG), c, goh4, op, ALU.mult))
                link(vec.memset(placed[NROW:P, 0:2, TP * E:NT * E], 0.0))
                vec.tensor_tensor(M[:, :], selA, selB, ALU.add).then_inc(*dve_s.inc("M"))
                vec.tensor_copy(rows_of[:, :, :, 3], selB.rearrange("p (t e) -> p t e", t=NT))
                dve.wait_ge(*full["I"].at("ranks"))
                vec.tensor_copy(stat["cnt"], bank("I")[:, NT * E:(NT + 1) * E])
                vec.scalar_tensor_tensor(R, bank("I")[:, 0:NT * E], 1.0, M[:, :], ALU.add, ALU.mult).then_inc(*read["I"].inc("ranks"))
                dve.wait_ge(*read["I"].at("ranks"))
                iota = c32[:, C_IOTA]

                def one_hot(s, places, label=None):
                    ins = vec.tensor_tensor(onehot[:, s % 4, :, :], places.unsqueeze(2).to_broadcast([P, NT, P]), across(iota, NT, P), ALU.is_equal)
                    if label is not None:
                        ins.then_inc(*dve_s.inc("onehot", label))

                def index(g):
                    dve.wait_ge(*full["I"].at("idx", g))
                    n = len(GROUPS[g])
                    cols = bank("I")[:, 0:4 * n].rearrange("p (s c) -> p s c", c=4)
                    s0 = GROUPS[g][0]
                    link(vec.tensor_reduce(work[:, 0:n], cols[:, :, 0:3], AX.X, ALU.add))
                    vec.scalar_tensor_tensor(work[:, 4:4 + n], cols[:, :, 3], float(TOK), work[:, 0:n], ALU.mult, ALU.add).then_inc(*read["I"].inc("idx", g))
                    dve.wait_ge(*read["I"].at("idx", g))
                    vec.tensor_scalar(isca[:, s0:s0 + n], work[:, 4:4 + n], SKIP, None, ALU.add)
                    vec.tensor_scalar(igat[:, s0:s0 + n], work[:, 0:n], SKIP, None, ALU.add).then_inc(*dve_s.inc("idx", g))
                    dve.wait_ge(*dve_s.at("idx", g))

                def main_group(g):
                    for s in GROUPS[g]:
                        one_hot(s, R.rearrange("p (t e) -> p t e", t=NT)[:, :, s], g if s == GROUPS[g][-1] else None)
                    index(g)

                def extra_group(g):
                    for s in GROUPS[g]:
                        link(vec.scalar_tensor_tensor(work, win, 0.5, win, ALU.is_gt, ALU.mult))
                        link(vec.scalar_tensor_tensor(work, work, P + 0.5, work, ALU.is_lt, ALU.mult))
                        link(vec.tensor_reduce(stat["vt"], work.rearrange("p (t e) -> p t e", t=NT), AX.X, ALU.add))
                        link(vec.scalar_tensor_tensor(work, work, 0.5, selB, ALU.is_gt, ALU.mult))
                        link(vec.tensor_reduce(stat["rank"][:, 0:NT], work.rearrange("p (t e) -> p t e", t=NT), AX.X, ALU.add))
                        link(vec.tensor_copy(rows_ofx[:, s - E, :, 3], stat["rank"][:, 0:NT]))
                        link(vec.tensor_scalar(win, win, float(P), None, ALU.subtract))
                        one_hot(s, stat["vt"], g if s == GROUPS[g][-1] else None)
                        if s != GROUPS[g][-1]:
                            link(vec.tensor_copy(stat["gm"][:, 0:1], stat["gs"][:, 0:1]))
                    index(g)

                def logits_down():
                    link(vec.tensor_reduce(stat["gm"], lgg, AX.X, ALU.max))
                    link(vec.tensor_tensor(lgg, lgg, wide(stat["gm"], NT, G), ALU.subtract))
                    link(vec.tensor_reduce(stat["em"], ex, AX.X, ALU.max))
                    link(vec.tensor_tensor(ex, ex, wide(stat["em"], NT * G, EG), ALU.subtract))
                    vec.tensor_copy(lg[:, :, G:20], stat["ex"].rearrange("p (t n) -> p t n", t=NT)).then_inc(*dve_s.inc("lgsub"))

                def gate_values():
                    dve.wait_ge(*act_s.at("lgexp"))
                    link(vec.tensor_reduce(stat["gs"], lgg, AX.X, ALU.add))
                    link(vec.reciprocal(stat["gw"], stat["gs"]))
                    link(vec.tensor_copy(stat["ex"].rearrange("p (t n) -> p t n", t=NT), lg[:, :, G:20]))
                    link(vec.tensor_tensor(stat["ex"], stat["ex"], M[:, :], ALU.mult))
                    link(vec.tensor_reduce(stat["es"], ex, AX.X, ALU.add))
                    link(vec.scalar_tensor_tensor(stat["es"], stat["goh"], -1.0, stat["es"], ALU.mult, ALU.add))
                    link(vec.tensor_scalar(stat["es"], stat["es"], 1.0, 1e-30, ALU.add, ALU.max))
                    link(vec.reciprocal(stat["em"], stat["es"]))
                    em = stat["em"].rearrange("p (t g) -> p t g", t=NT)
                    link(vec.tensor_tensor(em, em, wide(stat["gw"], NT, G), ALU.mult))
                    g80 = gates[:, :, :].rearrange("p t e -> p (t e)")
                    link(vec.tensor_tensor(groups(g80, NT * G, EG), ex, wide(stat["em"], NT * G, EG), ALU.mult))
                    for a, sel in enumerate((selA, selB)):
                        link(vec.tensor_tensor(work, g80, sel, ALU.mult))
                        link(vec.tensor_reduce(stat["gAB"][:, a * NT:(a + 1) * NT], work.rearrange("p (t e) -> p t e", t=NT), AX.X, ALU.add))

                def extra_plan():
                    cnt, nov, ovb = stat["cnt"], stat["nov"], stat["ovb"]
                    link(vec.tensor_scalar(nov, cnt, P + 0.5, None, ALU.is_gt))
                    for c in range(2, NT):
                        link(vec.scalar_tensor_tensor(nov, cnt, c * P + 0.5, nov, ALU.is_gt, ALU.add))
                    pairs = cmpA.rearrange("p n j -> p (n j)")[:, 0:E * E].rearrange("p (a b) -> p a b", a=E)
                    link(vec.tensor_tensor(pairs, nov.unsqueeze(1).to_broadcast([P, E, E]), groups(c32[:, C_TRI], E, E), ALU.mult))
                    link(vec.tensor_reduce(ovb, pairs, AX.X, ALU.add))
                    link(vec.tensor_reduce(stat["vt"][:, 0:1], nov, AX.X, ALU.add))
                    vec.tensor_copy(flags[:, 0:1], stat["vt"][:, 0:1])
                    own = cmpA.rearrange("p n j -> p (n j)")[:, 0:EXTRA * E].rearrange("p (s e) -> p s e", s=EXTRA)
                    end = cmpB.rearrange("p n j -> p (n j)")[:, 0:EXTRA * E].rearrange("p (s e) -> p s e", s=EXTRA)
                    slots = c32[:, C_SLOTS][:, 0:EXTRA].unsqueeze(2).to_broadcast([P, EXTRA, E])
                    names = c32[:, C_SLOTS][:, 8:8 + E].unsqueeze(1).to_broadcast([P, EXTRA, E])
                    link(vec.tensor_tensor(own, ovb.unsqueeze(1).to_broadcast([P, EXTRA, E]), slots, ALU.is_le))
                    link(vec.tensor_tensor(nov, nov, ovb, ALU.add))
                    link(vec.tensor_tensor(end, nov.unsqueeze(1).to_broadcast([P, EXTRA, E]), slots, ALU.is_gt))
                    link(vec.tensor_tensor(own, own, end, ALU.mult))
                    link(vec.tensor_tensor(own, own, names, ALU.mult))
                    link(vec.tensor_reduce(work[:, 0:EXTRA], own, AX.X, ALU.add))
                    vec.tensor_copy(flags[:, 1:1 + EXTRA], work[:, 0:EXTRA]).then_inc(*dve_s.inc("flags"))
                    dve.wait_ge(*dve_s.at("flags"))
                    link(vec.tensor_scalar(ovb, ovb, float(P), float(P), ALU.mult, ALU.subtract))
                    w3, r3 = (a.rearrange("p (t e) -> p t e", t=NT) for a in (win, R))
                    link(vec.tensor_tensor(w3, r3, across(ovb, NT, E), ALU.add))
                    link(vec.scalar_tensor_tensor(win, R, P + 0.5, win, ALU.is_gt, ALU.mult))

                def in_turned(b, key):
                    for hf in range(2):
                        dve.wait_ge(*full[f"T{hf}"].at("tr", *key, hf))
                        g = par[:, PAR["g2"]][:, hf * HALF:(hf + 1) * HALF].unsqueeze(2).to_broadcast([P, HALF, P])
                        vec.tensor_tensor(hsT[:, b, hf * HALF:(hf + 1) * HALF, :], bank(f"T{hf}").rearrange("p (j t) -> p j t", j=HALF),
                                          g, ALU.mult).then_inc(*read[f"T{hf}"].inc("tr", *key, hf))

                def gated(b, key):
                    dve.wait_ge(*act_s.at("sil", *key))
                    vec.tensor_tensor(act_sb[:, b, :], sil[:, b, :], bank(f"S{b}")[:, DE:2 * DE], ALU.mult).then_inc(*read[f"S{b}"].inc("gu", *key))

                for g in range(3):
                    main_group(g)
                    if g == 0:
                        logits_down()
                in_turned(0, ("m", 0))
                for n in range(E):
                    if n < 2:
                        main_group(n + 3)
                    if n in (4, 6):
                        extra_group(n // 2 + 3)
                    if n == 2:
                        gate_values()
                    if n == 3:
                        extra_plan()
                    if n + 1 < E:
                        in_turned((n + 1) % 2, ("m", n + 1))
                    gated(n % 2, ("m", n))
                n_extra = extra_slots(dve, "dve")
                with turns(dve, "extra") as q:
                    for b in range(2):
                        def slot():
                            in_turned(b, ("x", b))
                            gated(b, ("x", b))
                        only_if(dve, n_extra > q * 2 + b, slot)
                for t in range(NT):
                    n = NROW if t == TP else P
                    dve.wait_ge(*y_in[t % 2].at("y", t))
                    for a in range(2):
                        ins = vec.scalar_tensor_tensor(x[0:n, t, :], both[0:n, t % 2, a, :], stat["gAB"][0:n, a * NT + t:a * NT + t + 1],
                                                       x[0:n, t, :], ALU.mult, ALU.add)
                        if a:
                            ins.then_inc(*x_ready.inc())
                        else:
                            link(ins)

        return totals


_SHAPES = [("yp", (4 * P, D)), ("ys", (NROW, D)), ("kp", (L, TP, P, W)), ("vp", (L, TP, P, W)), ("ks", (L, NROW, W)),
           ("vs", (L, NROW, W)), ("cvs", (L, NROW, W))]


def layout(a):
    f = np.float32

    def blocks(w):
        k, n = w.shape
        return w.reshape(k // (HALF * P), HALF, P, n // W, W).transpose(3, 0, 2, 1, 4).reshape(-1, P, PIECE)

    w_in, w_out = a["w_in"], a["w_out"]
    w = np.empty((L * W_LAYER, P, PIECE), f)
    for l in range(L):
        parts = w[l * W_LAYER:(l + 1) * W_LAYER]
        cols = blocks(w_in[l])
        for i, c in enumerate((3, 4, 2, 1, 0)):
            parts[2 * i:2 * i + 2] = cols[2 * c:2 * c + 2]
        parts[N_IN:N_DENSE] = blocks(w_out[l])
        for e in range(E):
            at = N_DENSE + PER_EXPERT * e
            parts[at:at + 2] = blocks(np.concatenate([a["w_gate"][l, e], a["w_up"][l, e]], axis=1))
            parts[at + 2] = a["w_down"][l, e].reshape(2, P, D).transpose(1, 0, 2).reshape(P, 2 * D)
    par = np.zeros((L, P, NPAR), f)

    def put(name, value):
        par[:, :, PAR[name]] = value
    put("g1", a["norm1_g"].reshape(L, KD, P).transpose(0, 2, 1))
    put("g2", a["norm2_g"].reshape(L, KD, P).transpose(0, 2, 1))
    put("qn", np.concatenate([a["qn_g"], a["qn_g"]], axis=1)[:, :, None])
    put("on", a["b_onorm_g"][:, :, None])
    for l in range(L):
        init = 0.8 - 0.6 * math.exp(-0.3 * l)
        par[l, :, PAR["init"]] = init
        par[l, :, PAR["keep"]] = 1.0 - init
    put("kn", a["kn_g"][:, None, :])
    put("av", a["a_vnorm_g"][:, None, :])
    put("lam", np.concatenate([a["lam_q1"], a["lam_k1"], a["lam_q2"], a["lam_k2"]], axis=1)[:, None, :])
    bs = a["a_bs"].reshape(L, 4, 2, P).transpose(0, 2, 1, 3).reshape(L, 2, 4 * P)
    put("bs", np.repeat(bs, DHA, axis=1))
    router = np.concatenate([a["router_g"], a["router_e"]], axis=2)
    put("router", router.reshape(L, KD, P, 20).transpose(0, 2, 1, 3).reshape(L, P, KD * 20))
    c32 = np.zeros((P, NC32), f)
    r = np.arange(P)
    c32[:, C_ID] = np.eye(P)
    c32[:, C_CAUSAL] = r[:, None] <= r[None, :]
    c32[:, C_BATCH] = r[:, None] // NS == r[None, :] // NS
    c32[0:NS, C_SPREAD] = r[0:NS, None] == r[None, :] % NS
    j, i = np.divmod(np.arange(EG * EG), EG)
    c32[:, C_FIRST.start:C_FIRST.start + EG * EG] = i < j
    a16 = np.arange(E)
    c32[:, C_TRI] = (a16[None, :] < a16[:, None]).reshape(1, -1)
    c32[:, C_IOTA] = r[None, :] + 1
    rows = np.zeros((P, NT, 4))
    rows[:, :, 0], rows[:, :, 1], rows[:, :, 2] = r[:, None], P * np.arange(NT)[None, :], -SKIP
    c32[:, C_ROWS] = rows.reshape(P, -1)
    c32[:, C_SLOTS.start:C_SLOTS.start + EXTRA] = np.arange(EXTRA)
    c32[:, C_SLOTS.start + 8:C_SLOTS.start + 8 + E] = a16
    c32[:, C_MAP0] = (r[:, None] // NS) % 2 == 0
    c32[:, C_MAP1] = (r[:, None] // NS) % 2 == 1
    c16 = np.zeros((P, NC16), f)
    c16[:, B_ID] = np.eye(P)
    c16[:, B_CAUSAL] = np.where(r[None, :] <= r[:, None], 0.0, -1e30)
    c16[:, B_ONES] = 1.0
    c16[:, B_BEFORE] = r[:, None] < r[None, :]
    row, key = np.arange(64), np.arange(64)
    for b in range(NB):
        ok = (key[None, :] // NS == b) & (key[None, :] % NS <= row[:, None] % NS)
        c16[0:64, B_SAMPLE.start + b * 64:B_SAMPLE.start + (b + 1) * 64] = np.where(ok, 0.0, -1e30)
    return {
        "xp": a["x_prompt"].reshape(4 * P, D), "xs": a["x_sample"].reshape(NROW, D),
        "w": w, "par": par, "ws": a["a_ws"].transpose(0, 3, 1, 2),
        "ck": a["cache_k"].transpose(0, 1, 4, 3, 2).reshape(L * NPOOL, P, H, P),
        "cv": a["cache_v"].reshape(L * NPOOL, P, W),
        "pages": a["page_table"].reshape(1, -1).astype(np.int32), "c32": c32, "c16": c16,
    }


def build(nc, arrays, totals):
    d = {n: nc.dram_tensor(f"in_{n}", v.shape, mybir.dt.from_np(v.dtype), kind="ExternalInput").ap() for n, v in arrays.items()}
    for n, shape in _SHAPES:
        d[n] = nc.dram_tensor(f"out_{n}", shape, F32, kind="ExternalOutput").ap()
    program(nc, totals, d)


def kernel(**inputs):
    import concourse.bacc as bacc
    from concourse.bass_utils import run_bass_kernel_spmd
    arrays = {n: np.ascontiguousarray(v) for n, v in layout({n: np.asarray(v) for n, v in inputs.items()}).items()}
    totals = {}
    for _ in range(2):
        nc = bacc.Bacc("TRN2", target_bir_lowering=False, num_devices=1)
        build(nc, arrays, totals)
    r = run_bass_kernel_spmd(nc, [{f"in_{n}": v for n, v in arrays.items()}], core_ids=[0]).results[0]
    o = {n: r[f"out_{n}"] for n, _ in _SHAPES}
    return (o["yp"].reshape(1, 4 * P, D), o["ys"].reshape(NB, NS, D), o["kp"].reshape(L, 1, 4 * P, H, 2 * DK),
            o["vp"].reshape(L, 1, 4 * P, H, DV), o["ks"].reshape(L, NB, NS, H, 2 * DK), o["vs"].reshape(L, NB, NS, H, DV),
            o["cvs"].reshape(L, NB, NS, HA * DHA))
```

```python
import math
from contextlib import ExitStack, contextmanager

import numpy as np
import concourse.bass as bass
from concourse import mybir

ALU = mybir.AluOpType
ACT = mybir.ActivationFunctionType
AX = mybir.AxisListType
F32 = mybir.dt.float32
BF16 = mybir.dt.bfloat16

P = 128
L = 2
D = 1024
KD = D // P
NT = 5
TP = 4
TOK = NT * P
NB, NS = 8, 8
NROW = NB * NS
H = 4
DK, DV = 64, 128
HA, DHA = 8, 64
PAGES = 2
NPOOL = 20
E, G, EG = 16, 4, 4
DE = 256
NR = G + E
EPS = 1e-6
SCALE = DK ** -0.5
W = 512
HALF = KD // 2
PIECE = HALF * W
RING = 6
N_IN = 10
N_OUT = 4
N_DENSE = N_IN + N_OUT
PER_EXPERT = 3
W_LAYER = N_DENSE + E * PER_EXPERT
EXTRA = 2 * (TP * P + NROW) // P - 1
EXTRA += EXTRA % 2
PER_LAYER = W_LAYER + EXTRA * PER_EXPERT
SKIP = 65536.0
CREDIT = 8

_PAR = [("g1", KD), ("g2", KD), ("qn", 1), ("on", 1), ("keep", 1), ("init", 1), ("kn", DK), ("av", W),
        ("lam", 4 * DK), ("bs", 4 * P), ("router", KD * 20)]
PAR = {}
_at = 0
for _n, _w in _PAR:
    PAR[_n] = slice(_at, _at + _w)
    _at += _w
NPAR = _at
C_ID, C_CAUSAL, C_BATCH, C_SPREAD, C_FIRST = (slice(i * P, (i + 1) * P) for i in range(5))
NC32 = 8 * P + NT * 4 + 24
C_TRI = slice(5 * P, 7 * P)
C_IOTA = slice(7 * P, 8 * P)
C_ROWS = slice(8 * P, 8 * P + NT * 4)
C_SLOTS = slice(8 * P + NT * 4, 8 * P + NT * 4 + 24)
C_MAP0, C_MAP1 = slice(4 * P + 16, 4 * P + 17), slice(4 * P + 17, 4 * P + 18)
B_ID, B_CAUSAL = slice(0, P), slice(P, 2 * P)
B_SAMPLE = slice(2 * P, 2 * P + NB * NROW)
B_ONES, B_BEFORE = (slice(2 * P + NB * NROW + i * P, 2 * P + NB * NROW + (i + 1) * P) for i in range(2))
NC16 = 4 * P + NB * NROW


class Count:

    loops = []
    every = []

    def __init__(self, sem, name, totals, start=0, answers=None):
        self.sem, self.name, self.totals = sem, name, totals
        self.local, self.where = start, totals.setdefault(("where", name), {})
        self.answers, self.begin = answers, start
        Count.every.append(self)

    def step(self, loop):
        if self.answers:
            return self.answers.step(loop)
        return self.totals.get((self.name, loop), 0)

    def inc(self, *label, by=1):
        self.local += by
        self.where[label] = (self.local, tuple(n for n, _, _ in Count.loops))
        return self.sem, by

    def value(self, local, names):
        active = {n: i for n, i, _ in Count.loops}
        out = local
        for n in names:
            if self.step(n):
                out = (active[n] if n in active else TURNS[n] - 1) * self.step(n) + out
        return out

    def at(self, *label, less=0):
        local, names = (self.answers or self).where.get(label, (1 + less, ()))
        return self.sem, self.value(local - less + (self.begin if self.answers else 0), names)

    def now(self, more=0):
        return self.value(self.local + more, [n for n, _, _ in Count.loops])


TURNS = {"layer": L, "extra": EXTRA // 2 - 1}


def only_if(eng, cond, body, arrivals=(), uncounted=()):
    before = {c: c.local for c in Count.every}
    with eng.If(cond):
        body()
    after = {c: c.local for c in Count.every}
    with eng.Else():
        for c in before:
            c.local = before[c]
        if not arrivals:
            eng.drain()
        for c in before:
            if after[c] != before[c] and c not in uncounted:
                if c in arrivals:
                    eng.wait_ge(c.sem, c.now())
                eng.sem_inc(c.sem, after[c] - before[c])
                c.local = after[c]
    eng.nop()


def extras(eng, n_extra, slot, **moved):
    def pair(key, number, q):
        slot(key, 0, number, q)
        only_if(eng, n_extra > number + 1, lambda: slot(key, 1, number + 1, q), **moved)

    def others():
        with turns(eng, "extra") as q:
            only_if(eng, n_extra > q * 2 + 2, lambda: pair("x", q * 2 + 2, q), **moved)

    def first():
        pair("e", 0, 0)
        only_if(eng, n_extra > 2, others, **moved)

    only_if(eng, n_extra > 0, first, **moved)


@contextmanager
def turns(eng, name):
    before = {c: c.local for c in Count.every}
    with eng.Fori(0, TURNS[name]) as i:
        Count.loops.append((name, i, TURNS[name]))
        yield i
        Count.loops.pop()
    for c in Count.every:
        if c in before and c.local != before[c]:
            c.totals[(c.name, name)] = c.local - before[c]
            c.local = before[c] + TURNS[name] * (c.local - before[c])


def program(nc, totals, d):
    Count.loops, Count.every = [], []
    with ExitStack() as ctx:
        def sb(name, shape, dt=F32):
            return ctx.enter_context(nc.sbuf_tensor(name, shape, dt))

        def count(name, start=0, answers=None):
            return Count(ctx.enter_context(nc.semaphore(name)), name, totals, start, answers)

        h_rows = nc.dram_tensor("h_rows", [TOK, D], F32).ap()
        y_rows = nc.dram_tensor("y_rows", [2 * TOK, D], F32).ap()
        x = sb("x", [P, NT, D])
        ring = sb("ring", [P, RING, PIECE])
        hT_cols = sb("hT", [P, KD * TOK])
        hT = hT_cols[:, :].rearrange("p (k t) -> p k t", k=KD)
        spare = ring[:, RING - 2:RING, :].rearrange("p a n -> p (a n)")
        e_sb = spare[:, 0:2048].rearrange("p (b m k) -> p b m k", b=2, m=2)
        aT = spare[:, 2048:3072].rearrange("p (b j k) -> p b j k", b=2, j=4)
        es = spare[:, 3072:3072 + 640].rearrange("p (b k) -> p b k", b=2)
        aTs = spare[:, 3712:3712 + 384].rearrange("p (b j k) -> p b j k", b=2, j=3)
        cat_cols = sb("cat", [P, KD * TOK])
        catT = cat_cols[:, :].rearrange("p (k t) -> p k t", k=KD)
        qz = cat_cols[:, 4 * TOK:8 * TOK].rearrange("p (t n) -> p t n", t=NT)
        hn = sb("hn", [P, 2, D])
        qS = hn[:, :, :].rearrange("p a (b h r) -> p (a b) h r", b=4, h=H)
        kva = sb("kva", [P, NT, W])
        v = sb("v", [P, NT, W])
        qk = sb("qk", [P, 2 * H * TOK])
        qT, kT = (qk[:, i * H * TOK:(i + 1) * H * TOK].rearrange("p (h t) -> p h t", h=H) for i in range(2))
        hn2 = qk[:, :].rearrange("p (t n) -> p t n", t=NT)
        par = sb("par", [P, NPAR])
        ws = sb("ws", [P, HA, P])
        kc = sb("kc", [P, 2, H, PAGES * P])
        vc = sb("vc", [P, 2, PAGES, W])
        sqj = sb("sqj", [P, 2, W])
        tmp = sb("tmp", [P, W])
        o_sb = sb("o_sb", [P, 2, W])
        oT = sb("oT", [P, H, P])
        c32 = sb("c32", [P, NC32])
        c16 = sb("c16", [P, NC16], BF16)
        st = sb("st", [P, 640])
        lg = sb("lg", [P, NT, 20])
        cmpA = cat_cols[:, 0:NT * NR * EG].rearrange("p (n j) -> p n j", j=EG)
        cmpB = cat_cols[:, 512:512 + NT * NR * EG].rearrange("p (n j) -> p n j", j=EG)
        sil = cat_cols[:, 1024:1536].rearrange("p (b f) -> p b f", b=2)
        act_sb = cat_cols[:, 1536:2048].rearrange("p (b f) -> p b f", b=2)
        actT = cat_cols[:, 2048:2560].rearrange("p (b f t) -> p b f t", b=2, f=2)
        onehot = cat_cols[:, 2560:3840].bitcast(BF16).rearrange("p (b t s) -> p b t s", b=4, t=NT)
        hs = hT_cols[:, 0:2 * D].rearrange("p (b n) -> p b n", b=2)
        hsT = hT_cols[:, 2 * D:4 * D].rearrange("p (b k t) -> p b k t", b=2, k=KD)
        both = [cols[:, b * 2 * D:(b + 1) * 2 * D].rearrange("p (a n) -> p a n", a=2) for cols in (hT_cols, qk) for b in range(2)]
        y_sb = hn
        rows_of = sb("rows_of", [P, NT, E, 4], BF16)
        rows_ofx = sb("rows_ofx", [P, EXTRA, NT, 4], BF16)
        M = sb("M", [P, NT * E], BF16)
        placed = cat_cols[:, 3840:4240].rearrange("p (i n) -> p i n", i=5)
        gates = cat_cols[:, 4240:4320].rearrange("p (t e) -> p t e", t=NT)
        igat = sb("igat", [P, E + EXTRA + 2], mybir.dt.uint32)
        isca = sb("isca", [P, E + EXTRA], mybir.dt.uint32)
        icur = sb("icur", [P, 2, 2], mybir.dt.uint32)
        flags = sb("flags", [P, 16], mybir.dt.int32)
        half = sb("half", [P, 64])
        pages = sb("pages", [1, NB * PAGES], mybir.dt.int32)
        ps = ctx.enter_context(nc.psum_tensor("ps", [P, 8, 512], F32))

        stat = {}
        used = 0
        for name, w in [("ss", NT), ("rs", NT), ("ssk", 8 * NT), ("rsk", 8 * NT), ("ssa", NT), ("rsa", NT),
                        ("sso", 4 * NT), ("rso", 4 * NT), ("mx", 8), ("nb", 8), ("sm", 16), ("co", 8), ("r0", 8),
                        ("mxs", 4), ("nbs", 4), ("sms", 4), ("lam", 4), ("gm", 5), ("gs", 5), ("gw", 5),
                        ("rank", 100), ("goh", 20), ("em", 20), ("es", 20), ("ex", 80), ("ms", 8), ("rowf", 1), ("gAB", 10), ("cnt", 16), ("nov", 16), ("ovb", 16), ("vt", 5)]:
            stat[name] = st[:, used:used + w]
            used += w
        assert used <= 640

        ident, identb = c32[:, C_ID], c16[:, B_ID]

        FIRST = {"S0": 0, "J": 1, "T0": 2, "T1": 3, "S1": 4, "I": 5, "O": 6, "F": 7}
        full = {u: count(f"full_{u}") for u in FIRST}
        read = {u: count(f"read_{u}", 1, full[u]) for u in FIRST}

        def bank(u, k=0):
            return ps[:, FIRST[u] + k, :]

        landed = [count(f"landed_{s}") for s in range(RING)]
        piece_used = count("piece_used", CREDIT)
        x_in = [count(f"x_in{t}") for t in range(NT)]
        c32_in, c16_in = count("c32_in"), count("c16_in")
        par_in, ws_in = count("par_in"), count("ws_in")
        kc_in, vc_in = ([count(f"{n}_in{b}") for b in range(2)] for n in ("kc", "vc"))
        kc_used, vc_used = count("kc_used", 2), count("vc_used", 2)
        pages_in = count("pages_in")
        k_stored, va_stored, v_stored, stored = count("k_stored"), count("va_stored"), count("v_stored"), count("stored")
        act_s, dve_s, pool_s = count("act_s"), count("dve_s"), count("pool_s")
        dve_c, pool_c = count("dve_c"), count("pool_c")
        pool_passed = ctx.enter_context(nc.semaphore("pool_passed"))
        x_ready = count("x_ready", NT)
        h_stored = count("h_stored")
        hs_in = [count(f"hs_in{b}") for b in range(2)]
        hs_used = [count(f"hs_used{b}", 1) for b in range(2)]
        y_out = [count(f"y_out{b}") for b in range(2)]
        hs_inx = [count(f"hs_inx{b}") for b in range(2)]
        y_outx = [count(f"y_outx{b}") for b in range(2)]
        y_in = [count(f"y_in{b}") for b in range(4)]
        passed = {e: ctx.enter_context(nc.semaphore(f"passed_{e}")) for e in ("sp", "act", "dve", "pe")}

        block = ctx.enter_context(nc.Block())

        GROUPS = [range(0, 2), range(2, 4), range(4, 8), range(8, 12), range(12, 16)]
        GROUPS += [range(E + 4 * i, E + 4 * i + 4) for i in range(EXTRA // 4)]

        EXTRA_AT = {"e": W_LAYER, "x": W_LAYER + 2 * PER_EXPERT}
        INDEX_AT = {0: 2, 1: 3, 2: 4, 5: 5, 7: 6}

        UP_AT = [N_DENSE + max(3 * n - 1, 0) for n in range(E)]
        DOWN_AT = [min(N_DENSE + 3 * n + 4, W_LAYER - 1) for n in range(E)]
        PIECE_AT = list(range(W_LAYER))
        for n in range(E):
            PIECE_AT[UP_AT[n]], PIECE_AT[UP_AT[n] + 1], PIECE_AT[DOWN_AT[n]] = (N_DENSE + PER_EXPERT * n + j for j in range(3))
        assert sorted(PIECE_AT) == list(range(W_LAYER))

        SLOT = [(i if i < N_IN else i + 2) % RING for i in range(PER_LAYER)]
        assert (N_IN + 2) % RING == 0 and SLOT[N_DENSE] == RING - 2 and PER_EXPERT * 2 == RING

        def before_it(i):
            return max([j for j in range(i) if SLOT[j] == SLOT[i]], default=None) if SLOT[i] in SLOT[:i] else \
                max(j for j in range(PER_LAYER) if SLOT[j] == SLOT[i]) - PER_LAYER

        LARGE = {0: [("va", 2)], 1: [("va", 3)], 2: [("va", 4)], 3: [("u", 0)], 4: [("u", 1)], 5: [("u", 2)], 6: [("u", 3)], 7: [("us", 0)]}
        SMALL = {1: [("ss", 0)], 2: [("pT", 0)], 3: [("so", 0)], 5: [("ss", 1)], 6: [("pT", 1)], 7: [("so", 1)],
                 8: [("mix", 0)], 9: [("mix", 1), ("ss", 2)], 10: [("mix", 2), ("pT", 2)], 11: [("mix", 3), ("so", 2)],
                 12: [("wsS", 0)], 13: [("mix", 4), ("ss", 3)], 14: [("pT", 3)], 15: [("so", 3)]}
        def spare_turn(n):
            return f"T{(n + 1) % 2}"

        OT = {t: spare_turn(4 * t + 9) if t < TP - 1 else f"T{t % 2}" for t in range(NT)}
        SO_AT = {g: spare_turn(n) for n, works in SMALL.items() for name, g in works if name == "so"}
        PT_AT = {g: spare_turn(n) for n, works in SMALL.items() for name, g in works if name == "pT"}

        def extra_slots(eng, name):
            eng.wait_ge(*dve_s.at("flags"))
            eng.sem_inc(passed[name], 1)
            return eng.value_load(flags[0:1, 0:1], min_val=0, max_val=EXTRA)

        @block.sync
        def _(sp):
            for c in [*read.values(), piece_used, kc_used, vc_used, x_ready, *hs_used]:
                sp.sem_inc(c.sem, c.begin)
            for t in range(NT):
                n = NROW if t == TP else P
                sp.dma_start(x[0:n, t, :], d["xs"] if t == TP else d["xp"][t * P:(t + 1) * P, :]).then_inc(*x_in[t].inc(by=16))
                if t == 0:
                    sp.dma_start(c32[:, :], d["c32"]).then_inc(*c32_in.inc(by=16))
                    sp.dma_start(cat_cols[:, 0:NC16], d["c16"]).then_inc(*c16_in.inc(by=16))
            with turns(sp, "layer") as l:
                for i in range(W_LAYER):
                    sp.wait_ge(piece_used.sem, l * PER_LAYER + (before_it(i) + 1 + CREDIT))
                    if i == 0:
                        sp.wait_ge(x_ready.sem, l * NT + 2)
                    if i == N_DENSE:
                        sp.wait_ge(*full["O"].at("o", TP - 1))
                        sp.wait_ge(*full[SO_AT[3]].at("so", 3))
                    sp.dma_start(ring[:, SLOT[i], :], d["w"][bass.DynSlice(l * W_LAYER + PIECE_AT[i], 1), :, :].rearrange("a p n -> (a p) n")
                                 ).then_inc(*landed[SLOT[i]].inc("w", i, by=16))
                n_extra = extra_slots(sp, "sp")

                def load(key, b, number, q):
                    e = sp.value_load(flags[0:1, bass.DynSlice(number + 1, 1)] if key == "x" else flags[0:1, number + 1:number + 2], min_val=0, max_val=E - 1)
                    for j in range(PER_EXPERT):
                        i = EXTRA_AT[key] + b * PER_EXPERT + j
                        sp.wait_ge(piece_used.sem, l * PER_LAYER + q * (2 * PER_EXPERT) + (i - RING + 1 + CREDIT))
                        sp.dma_start(ring[:, SLOT[i], :],
                                     d["w"][bass.DynSlice(l * W_LAYER + e * PER_EXPERT + (N_DENSE + j), 1), :, :].rearrange("a p n -> (a p) n")
                                     ).then_inc(*landed[SLOT[i]].inc("w", i, by=16))

                extras(sp, n_extra, load, arrivals=landed)
            for t in range(NT):
                n = NROW if t == TP else P
                sp.wait_ge(x_ready.sem, L * NT + t + 1)
                sp.dma_start(d["ys"] if t == TP else d["yp"][t * P:(t + 1) * P, :], x[0:n, t, :]).then_inc(*stored.inc(by=16))
            sp.wait_ge(stored.sem, stored.now())
            sp.wait_ge(*v_stored.at("v"))
            sp.wait_ge(*va_stored.at("va"))
            sp.wait_ge(*k_stored.at("k"))

        @block.gpsimd
        def _(pool):
            nc.gpsimd.memset(half[:, :], -0.5).then_inc(*pool_c.inc())
            pool.dma_start(pages[:, :], d["pages"]).then_inc(*pages_in.inc(by=16))

            def wait(sem, value):
                pool.wait_ge(sem, value)
                pool.sem_inc(pool_passed, 1)

            def rsqrt(dst, src, n, size, label):
                if Count.loops:
                    wait(pool_c.sem, pool_c.now())
                nc.gpsimd.tensor_scalar(stat["ms"][:, 0:n], src, 1.0 / size, EPS, ALU.mult, ALU.add).then_inc(*pool_c.inc())
                wait(pool_c.sem, pool_c.now())
                nc.gpsimd.tensor_tensor(dst, stat["ms"][:, 0:n], half[:, 0:n], ALU.pow).then_inc(*pool_c.inc(*label))

            def cache_load(b, l, buffer, table, arrived, used, view):
                wait(used.sem, l * NB + (b + 1))
                for g in range(PAGES):
                    page = pool.value_load(pages[0:1, b * PAGES + g:b * PAGES + g + 1], min_val=0, max_val=NPOOL - 1)
                    pool.dma_start(buffer(b % 2, g), view(d[table][bass.DynSlice(l * NPOOL + page, 1)])).then_inc(*arrived[b % 2].inc("kv", b, by=16))

            def keys_load(b, l):
                cache_load(b, l, lambda c, g: kc[:, c, :, g * P:(g + 1) * P], "ck", kc_in, kc_used, lambda a: a.rearrange("a p h t -> (a p) h t"))

            def values_load(b, l):
                cache_load(b, l, lambda c, g: vc[:, c, g, :], "cv", vc_in, vc_used, lambda a: a.rearrange("a p n -> (a p) n"))

            with turns(pool, "layer") as l:
                wait(read["J"].sem, l * full["J"].step("layer") + 1)
                pool.dma_start(par[:, :], d["par"][bass.DynSlice(l, 1), :, :].rearrange("a p n -> (a p) n")).then_inc(*par_in.inc("par", by=16))
                for t in range(NT):
                    wait(*act_s.at("ss1", t))
                    rsqrt(stat["rs"][:, t:t + 1], stat["ss"][:, t:t + 1], 1, D, ("rs1", t))
                    if t == 2:
                        pool.dma_start(ws[:, :, :], d["ws"][bass.DynSlice(l, 1), :, :, :].rearrange("a p h t -> (a p) h t")).then_inc(*ws_in.inc("ws", by=16))
                wait(pages_in.sem, 16)
                for b in range(2):
                    keys_load(b, l)
                    values_load(b, l)
                for t in range(NT):
                    wait(*dve_s.at("ssk", t))
                    rsqrt(stat["rsk"][:, 8 * t:8 * t + 8], stat["ssk"][:, 8 * t:8 * t + 8], 8, DK, ("rsk", t))
                wait(*dve_s.at("k", NT - 1))
                pool.dma_start(d["kp"][bass.DynSlice(l, 1), :, :, :].rearrange("a t p n -> (a p) t n"), kva[:, 0:TP, :]).then_inc(*k_stored.inc(by=16))
                pool.dma_start(d["ks"][bass.DynSlice(l, 1), :, :].rearrange("a p n -> (a p) n"), kva[0:NROW, TP, :]).then_inc(*k_stored.inc("k", by=16))
                for t in (TP - 1, TP):
                    wait(*read[f"S{t % 2}"].at("z", "v", t))
                pool.dma_start(d["vp"][bass.DynSlice(l, 1), :, :, :].rearrange("a t p n -> (a p) t n"), v[:, 0:TP, :]).then_inc(*v_stored.inc(by=16))
                pool.dma_start(d["vs"][bass.DynSlice(l, 1), :, :].rearrange("a p n -> (a p) n"), v[0:NROW, TP, :]).then_inc(*v_stored.inc("v", by=16))
                for t in range(NT):
                    wait(*dve_s.at("ssq", t))
                    rsqrt(stat["rsk"][:, 8 * t:8 * t + 8], stat["ssk"][:, 8 * t:8 * t + 8], 8, DK, ("rsq", t))
                def pair_load(load, g):
                    for b in (2 * g, 2 * g + 1):
                        load(b, l)

                def head_root(t):
                    wait(*dve_s.at("sso", t))
                    rsqrt(stat["rso"][:, 4 * t:4 * t + 4], stat["sso"][:, 4 * t:4 * t + 4], 4, DV, ("rso", t))

                for t in range(NT):
                    wait(*act_s.at("ssa", t))
                    rsqrt(stat["rsa"][:, t:t + 1], stat["ssa"][:, t:t + 1], 1, W, ("rsa", t))
                    if t == TP - 1:
                        pair_load(keys_load, 1)
                wait(*dve_s.at("va", NT - 1))
                pool.dma_start(d["cvs"][bass.DynSlice(l, 1), :, :].rearrange("a p n -> (a p) n"), kva[0:NROW, TP, :]).then_inc(*va_stored.inc("va", by=16))
                pair_load(values_load, 1)
                for g in (2, 3):
                    pair_load(keys_load, g)
                    head_root(g - 2)
                    pair_load(values_load, g)
                head_root(2)
                head_root(3)
                for t in range(NT):
                    if t == 2:
                        head_root(TP)
                    wait(*act_s.at("ss2", t))
                    rsqrt(stat["rs"][:, t:t + 1], stat["ss"][:, t:t + 1], 1, D, ("rs2", t))

                def gather(b, index, key, landed):
                    if key[0] in "ex":
                        wait(*hs_used[b].at("tr", *key))
                    else:
                        wait(*hs_used[b].at("tr", *(key if key[0] == "m" else ("m", E - 2 + b)), less=int(key[0] == "m")))
                    pool.indirect_dma_start(hs[:, b, :], None, h_rows, bass.IndirectOffsetOnAxis(index, 0),
                                            bounds_check=TOK - 1, oob_is_err=False).then_inc(*landed.inc("hs", *key, by=16))

                def scatter(b, index, key, landed):
                    wait(*read["O"].at("down", *key))
                    pool.indirect_dma_start(y_rows, bass.IndirectOffsetOnAxis(index, 0), y_sb[:, b, :], None,
                                            bounds_check=2 * TOK - 1, oob_is_err=False).then_inc(*landed.inc("y", *key, by=16))

                wait(*h_stored.at("h", NT - 1))
                def gather_main(m):
                    wait(*dve_s.at("idx", min(g for g, es in enumerate(GROUPS) if m in es)))
                    gather(m % 2, igat[:, m:m + 1], ("m", m), hs_in[m % 2])

                for m in range(3):
                    gather_main(m)
                for n in range(E):
                    if n + 3 < E:
                        gather_main(n + 3)
                    if n == E - 2:
                        wait(*dve_s.at("flags"))
                        wait(*dve_s.at("idx", len(GROUPS) - 1))
                        n_extra = pool.value_load(flags[0:1, 0:1], min_val=0, max_val=EXTRA)
                    if n >= E - 2:
                        def first_extra():
                            gather(b, igat[:, E + b:E + b + 1], ("x0", b), hs_inx[b])
                        b = n - (E - 2)
                        only_if(pool, n_extra > b, first_extra, uncounted=hs_inx)
                    scatter(n % 2, isca[:, n:n + 1], ("m", n), y_out[n % 2])

                def move(key, b, number, q):
                    def rows_at(table, more, c):
                        if key == "e":
                            return table[:, number + E + more:number + E + more + 1]
                        nc.gpsimd.tensor_copy(icur[:, b, c:c + 1], table[:, bass.DynSlice(number + (E + more), 1)]).then_inc(*pool_c.inc())
                        wait(pool_c.sem, pool_c.now())
                        return icur[:, b, c:c + 1]

                    def next_in():
                        gather(b, rows_at(igat, 2, 0), (key, b), hs_inx[b])

                    wait(*read["O"].at("down", key, b))
                    scatter(b, rows_at(isca, 0, 1), (key, b), y_outx[b])
                    only_if(pool, n_extra > number + 2, next_in, uncounted=hs_inx)

                extras(pool, n_extra, move, uncounted=[*hs_inx, *y_outx])

        ATT = [(i, h) for i in range(TP) for h in range(H)]

        @block.tensor
        def _(pe):
            pending = []

            def mm(out, lhsT, rhs, start=True, stop=True, inc=None, tr=False, loose=False):
                if tr:
                    ins = pe.transpose(out, lhsT, rhs)
                else:
                    ins = pe.matmul(out, lhsT, rhs, start=start, stop=stop, skip_group_check=loose)
                if inc:
                    ins.then_inc(*inc)
                elif pending:
                    c, label = pending.pop(0)
                    ins.then_inc(*c.inc(*label))

            def claim(u):
                pe.wait_ge(read[u].sem, full[u].now(1))

            def turn_rows(stage, t, ready):
                rows = hn2[:, t, :] if stage == "h2" else hn[:, t % 2, :]
                pe.wait_ge(*ready)
                for hf in range(2):
                    u = f"T{hf}"
                    claim(u)
                    for j in range(HALF):
                        k = hf * HALF + j
                        mm(bank(u)[:, j * P:(j + 1) * P], rows[:, k * P:(k + 1) * P], ident, tr=True,
                           inc=full[u].inc(stage, t, hf) if j == HALF - 1 else None)

            gathered = [pe.alloc_register(f"gathered{b}") for b in range(2)]
            for reg in gathered:
                pe.reg_mov(reg, 0)
            pe.wait_ge(c32_in.sem, 16)
            with turns(pe, "layer"):
                def arrived(i):
                    pe.wait_ge(*landed[SLOT[i]].at("w", i))

                def rows(name, c):
                    for t in range(NT):
                        u = f"S{t % 2}"
                        if c > 0:
                            claim(u)
                        else:
                            for j in [0, 1] if t == 0 else [t + 1] if t + 1 < NT else []:
                                turn_rows("h1", j, dve_s.at("hn1", j))
                            claim(u)
                            for hf in range(2):
                                pe.wait_ge(*read[f"T{hf}"].at("h1", t, hf))
                        for k in range(KD):
                            if t == 0 and k % HALF == 0:
                                arrived(2 * c + k // HALF)
                            mm(bank(u), hT[:, k, t * P:(t + 1) * P], ring[:, SLOT[2 * c + k // HALF], (k % HALF) * W:(k % HALF + 1) * W],
                               start=(k == 0), stop=(k == KD - 1),
                               inc=full[u].inc("z", name, t) if k == KD - 1 else None)
                            if t == NT - 1 and k % HALF == HALF - 1:
                                pending.append((piece_used, ()))

                def turn_heads(name, src, ready):
                    for t in range(NT):
                        pe.wait_ge(*ready(t))
                        u = f"T{t % 2}"
                        claim(u)
                        for h in range(H):
                            mm(bank(u)[:, h * P:(h + 1) * P], src[:, t, h * P:(h + 1) * P], ident, tr=True,
                               inc=full[u].inc(name, t) if h == H - 1 else None)

                rows("k", 0)
                rows("v", 1)
                rows("q", 2)
                turn_heads("kT", kva, lambda t: dve_s.at("k", t))

                def large(name, j):
                    claim("F")
                    c = 3 if name == "va" else 4
                    for m in range(4) if name == "us" else [j]:
                        for k in range(KD):
                            i = 2 * c + k // HALF
                            if j == 0 and m == 0 and k % HALF == 0:
                                arrived(i)
                            w = ring[:, SLOT[i], (k % HALF) * W:(k % HALF + 1) * W]
                            if name == "va":
                                args = bank("F"), hT[:, k, j * P:(j + 1) * P], w
                            elif name == "u":
                                args = bank("F"), w[:, m * P:(m + 1) * P], hT[:, k, 0:TP * P]
                            else:
                                args = bank("F")[:, m * P:(m + 1) * P], w[:, m * P:(m + 1) * P], hT[:, k, TP * P:TOK]
                            last = k == KD - 1 and (name != "us" or m == 3)
                            mm(*args, start=(k == 0), stop=(k == KD - 1), inc=full["F"].inc(name, j) if last else None)
                            if (name == "us" and m == 3 or (name, j) == ("va", NT - 1)) and k % HALF == HALF - 1:
                                pending.append((piece_used, ()))

                def mix(t):
                    claim("F")
                    pe.wait_ge(*dve_s.at("va", t))
                    if t == TP:
                        pe.wait_ge(*read["F"].at("wsS", 0))
                    for h in range(HA):
                        r = (h % 2) * DHA
                        mm(bank("F")[r:r + DHA, (h // 2) * P:(h // 2 + 1) * P], kva[:, t, h * DHA:(h + 1) * DHA],
                           ws[:, h, :], inc=full["F"].inc("mix", t) if h == HA - 1 else None)

                def sample_mix():
                    claim("F")
                    mm(bank("F")[:, 0:HA * NS].rearrange("p (h t) -> p h t", h=HA), c32[0:NS, C_SPREAD], ws[0:NS, :, 0:NS], inc=full["F"].inc("wsS", 0))

                large("va", 0)
                pe.wait_ge(*dve_s.at("ws"))
                large("va", 1)
                turn_heads("qT", qz, lambda t: dve_s.at("q", t))

                def scores(n):
                    i, h = ATT[n]
                    u = f"S{n % 2}"
                    claim(u)
                    if n == 0:
                        for t in (TP - 1, TP):
                            pe.wait_ge(*read[f"T{t % 2}"].at("qT", t))
                    for m in range(2):
                        mm(bank(u, m)[:, 0:(i + 1) * P], qT[m * DK:(m + 1) * DK, h, i * P:(i + 1) * P],
                           kT[m * DK:(m + 1) * DK, h, 0:(i + 1) * P])
                        mm(bank(u, m)[:, i * P:(i + 1) * P], identb, c16[:, B_CAUSAL], start=False, loose=True,
                           inc=full[u].inc("s", n) if m == 1 else None)

                def turn_probs(n):
                    i, h = ATT[n]
                    pe.wait_ge(*dve_s.at("a", n))
                    u = f"T{n % 2}"
                    claim(u)
                    for j in range(i + 1):
                        mm(bank(u)[:, j * P:(j + 1) * P], e_sb[:, n % 2, 0, j * P:(j + 1) * P], ident, tr=True,
                           inc=full[u].inc("aT", n) if j == i else None)

                def weigh(n):
                    i, h = ATT[n]
                    if h == 0:
                        claim("O")
                    pe.wait_ge(*read[f"T{n % 2}"].at("aT", n))
                    for j in range(i + 1):
                        mm(bank("O")[:, h * DV:(h + 1) * DV], aT[:, n % 2, j, :], v[:, j, h * DV:(h + 1) * DV],
                           start=(j == 0), stop=(j == i), inc=full["O"].inc("o", i) if (h == H - 1 and j == i) else None)

                def turn_out(t):
                    pe.wait_ge(*dve_s.at("o", t))
                    u = OT[t]
                    claim(u)
                    for h in range(H):
                        mm(bank(u)[:, h * P:(h + 1) * P], o_sb[:, t % 2, h * P:(h + 1) * P], ident, tr=True,
                           inc=full[u].inc("oT", t) if h == H - 1 else None)

                def sample_scores(g):
                    claim("F")
                    if g == 0:
                        pe.wait_ge(*dve_s.at("qS"))
                    for b in (2 * g, 2 * g + 1):
                        r = (b % 2) * 64
                        pe.wait_ge(*kc_in[b % 2].at("kv", b))
                        for h in range(H):
                            mm(bank("F")[r:r + 64, 0:PAGES * P], qS[:, b, h, :], kc[:, b % 2, h, :], start=(h == 0), stop=(h == H - 1),
                               inc=kc_used.inc() if h == H - 1 else None)
                        for h in range(H):
                            mm(bank("F")[r:r + 64, PAGES * P:PAGES * P + 64], qS[:, b, h, :], kT[:, h, TP * P:TP * P + 64], start=(h == 0), stop=False)
                        mm(bank("F")[r:r + 64, PAGES * P:PAGES * P + 64], identb[0:64, 0:64],
                           c16[0:64, B_SAMPLE][:, b * 64:(b + 1) * 64], start=False, inc=full["F"].inc("ss", g) if b % 2 else None)

                def sample_turn(g, u):
                    pe.wait_ge(*dve_s.at("ps", g))
                    claim(u)
                    for j in range(PAGES):
                        mm(bank(u)[:, j * P:(j + 1) * P], es[:, g % 2, j * P:(j + 1) * P], ident, tr=True)
                    mm(bank(u)[0:64, PAGES * P:(PAGES + 1) * P], es[:, g % 2, PAGES * P:PAGES * P + 64], ident, tr=True, inc=full[u].inc("pT", g))

                def sample_weigh(g, u):
                    claim(u)
                    pe.wait_ge(*read[PT_AT[g]].at("pT", g))
                    for b in (2 * g, 2 * g + 1):
                        pe.wait_ge(*vc_in[b % 2].at("kv", b))
                        for h in range(H):
                            c = (b % 2) * 32 + h * NS
                            out = bank(u)[:, (2 * h + b % 2) * NS:(2 * h + b % 2 + 1) * NS]
                            for j in range(PAGES):
                                mm(out, vc[:, b % 2, j, h * DV:(h + 1) * DV], aTs[:, g % 2, j, c:c + NS], start=(j == 0), stop=False)
                            mm(out, v[0:64, TP, h * DV:(h + 1) * DV], aTs[0:64, g % 2, PAGES, c:c + NS], start=False,
                               inc=None if h < H - 1 else full[u].inc("so", g) if b % 2 else vc_used.inc())
                    pending.append((vc_used, ()))

                for n in range(len(ATT) + 3):
                    if n < len(ATT):
                        scores(n)
                    if 2 <= n < len(ATT) + 2:
                        turn_probs(n - 2)
                    for name, j in LARGE.get(n, []):
                        large(name, j)
                    for name, j in SMALL.get(n, []):
                        if name == "mix":
                            mix(j)
                        elif name == "wsS":
                            sample_mix()
                        elif name == "ss":
                            sample_scores(j)
                        elif name == "pT":
                            sample_turn(j, spare_turn(n))
                        else:
                            sample_weigh(j, spare_turn(n))
                    if n >= 3:
                        weigh(n - 3)
                    if n >= 9 and n % 4 == 1:
                        turn_out((n - 9) // 4)

                def sample_out():
                    claim("O")
                    pe.wait_ge(*read[SO_AT[3]].at("so", 3))
                    for h in range(H):
                        mm(bank("O")[:, h * P:(h + 1) * P], oT[:, h, :], ident, tr=True, inc=full["O"].inc("o", TP) if h == H - 1 else None)

                for t in range(NT):
                    if t == TP - 1:
                        turn_out(t)
                        sample_out()
                    if t == TP:
                        turn_out(t)
                    pe.wait_ge(*dve_s.at("mix", t))
                    pe.wait_ge(*read[OT[t]].at("oT", t))
                    for n in range(2):
                        u = f"S{n}"
                        claim(u)
                        for k in range(KD):
                            i = N_IN + 2 * n + k // HALF
                            if t == 0 and k % HALF == 0:
                                arrived(i)
                            mm(bank(u), catT[:, k, t * P:(t + 1) * P], ring[:, SLOT[i], (k % HALF) * W:(k % HALF + 1) * W],
                               start=(k == 0), stop=(k == KD - 1), inc=full[u].inc("y", n, t) if k == KD - 1 else None)
                            if t == NT - 1 and k % HALF == HALF - 1:
                                pending.append((piece_used, ()))
                    if t >= 1:
                        turn_rows("h2", t - 1, dve_s.at("hn2", t - 1))

                def router(k):
                    return par[:, PAR["router"]][:, k * NR:(k + 1) * NR]

                claim("F")
                for t in range(TP):
                    for hf in range(2):
                        pe.wait_ge(*read[f"T{hf}"].at("h2", t, hf))
                for k in range(KD):
                    mm(bank("F")[0:NR, :], router(k), hT[:, k, 0:TP * P], start=(k == 0), stop=(k == KD - 1),
                       inc=full["F"].inc("logitsT") if k == KD - 1 else None)
                turn_rows("h2", NT - 1, dve_s.at("hn2", NT - 1))
                claim("O")
                pe.wait_ge(*read["F"].at("logitsT"))
                for hf in range(2):
                    pe.wait_ge(*read[f"T{hf}"].at("h2", TP, hf))
                for k in range(KD):
                    mm(bank("O")[:, TP * NR:NT * NR], hT[:, k, TP * P:TOK], router(k), start=(k == 0), stop=(k == KD - 1))
                for t in range(TP):
                    mm(bank("O")[:, t * NR:(t + 1) * NR], o_sb[0:NR, 0, t * P:(t + 1) * P], ident[0:NR, 0:NR], tr=True,
                       inc=full["O"].inc("logits") if t == TP - 1 else None)

                pe.wait_ge(*dve_s.at("M"))
                claim("I")
                for t in range(NT + 1):
                    for j in range(min(t + 1, NT)):
                        mm(bank("I")[:, t * E:(t + 1) * E], c16[:, B_BEFORE if j == t else B_ONES], M[:, j * E:(j + 1) * E],
                           start=(j == 0), stop=(j == min(t, NT - 1)), inc=full["I"].inc("ranks") if (t == NT and j == NT - 1) else None)

                def index_rows(g):
                    pe.wait_ge(*dve_s.at("onehot", g))
                    claim("I")
                    for n, s in enumerate(GROUPS[g]):
                        for t in range(NT):
                            mm(bank("I")[:, n * 4:n * 4 + 4], onehot[:, s % 4, t, :], rows_of[:, t, s, :] if s < E else rows_ofx[:, s - E, t, :],
                               start=(t == 0), stop=(t == NT - 1), inc=full["I"].inc("idx", g) if (n == len(GROUPS[g]) - 1 and t == NT - 1) else None)

                def turn_in(b, key, arrival):
                    pe.wait_ge(*arrival)
                    for hf in range(2):
                        u = f"T{hf}"
                        claim(u)
                        for j in range(HALF):
                            k = hf * HALF + j
                            mm(bank(u)[:, j * P:(j + 1) * P], hs[:, b, k * P:(k + 1) * P], ident, tr=True,
                               inc=full[u].inc("tr", *key, hf) if j == HALF - 1 else None)
                    pending.append((hs_used[b], ("tr", *key)))

                def up(b, key, hf, i):
                    u = f"S{b}"
                    if hf == 0:
                        claim(u)
                    pe.wait_ge(*read[f"T{hf}"].at("tr", *key, hf))
                    arrived(i + hf)
                    for j in range(HALF):
                        k = hf * HALF + j
                        mm(bank(u), hsT[:, b, k, :], ring[:, SLOT[i + hf], j * W:(j + 1) * W], start=(k == 0), stop=(k == KD - 1),
                           inc=full[u].inc("gu", *key) if k == KD - 1 else None)
                    pending.append((piece_used, ()))

                def turn_act(b, key):
                    pe.wait_ge(*read[f"S{b}"].at("gu", *key))
                    claim("J")
                    for f in range(2):
                        mm(bank("J")[:, f * P:(f + 1) * P], act_sb[:, b, f * P:(f + 1) * P], ident, tr=True,
                           inc=full["J"].inc("actT", *key) if f else None)

                def down(b, key, i):
                    claim("O")
                    pe.wait_ge(*read["J"].at("actT", *key))
                    arrived(i)
                    for c in range(2):
                        for f in range(2):
                            mm(bank("O", c), actT[:, b, f, :], ring[:, SLOT[i], f * D + c * W:f * D + (c + 1) * W], start=(f == 0), stop=(f == 1),
                               inc=full["O"].inc("down", *key) if (c and f) else None)
                    pending.append((piece_used, ()))

                def flush():
                    claim("T0")
                    while pending:
                        mm(bank("T0")[:, 0:P], ident, ident, tr=True)

                index_rows(0)
                index_rows(1)
                turn_in(0, ("m", 0), hs_in[0].at("hs", "m", 0))
                for n in range(E + 1):
                    b = n % 2
                    if n < E:
                        up(b, ("m", n), 0, UP_AT[n])
                    if n >= 1:
                        turn_act(1 - b, ("m", n - 1))
                    if n < E:
                        up(b, ("m", n), 1, UP_AT[n])
                    if n in INDEX_AT:
                        index_rows(INDEX_AT[n])
                    if n + 1 < E:
                        turn_in(1 - b, ("m", n + 1), hs_in[1 - b].at("hs", "m", n + 1))
                    if n >= 1:
                        down(1 - b, ("m", n - 1), DOWN_AT[n - 1])
                flush()
                n_extra = extra_slots(pe, "pe")

                def slot(key, b, number, q):
                    i = EXTRA_AT[key] + b * PER_EXPERT
                    pe.reg_add(gathered[b], gathered[b], 16)
                    turn_in(b, (key, b), (hs_inx[b].sem, pe.snap(gathered[b])))
                    up(b, (key, b), 0, i)
                    up(b, (key, b), 1, i)
                    turn_act(b, (key, b))
                    down(b, (key, b), i + 2)
                    flush()

                extras(pe, n_extra, slot)

        @block.scalar
        def _(act):
            def store_rows(t):
                act.wait_ge(*dve_s.at("hn2", t))
                act.dma_start(h_rows[t * P:(t + 1) * P, :], hn2[:, t, :]).then_inc(*h_stored.inc("h", t, by=16))

            scratch = {"ss1": o_sb[:, :, :].rearrange("p a n -> p (a n)"), "ss2": sqj[:, :, :].rearrange("p a n -> p (a n)")}

            scattered = [act.alloc_register(f"scattered{b}") for b in range(2)]
            for reg in scattered:
                act.reg_mov(reg, 0)
            with turns(act, "layer") as l:
                def square(stage, t):
                    if t:
                        act.wait_ge(*act_s.at(stage, t - 1))
                    nc.scalar.activation(scratch[stage], x[:, t, :], ACT.Square, accum_out=stat["ss"][:, t:t + 1]).then_inc(*act_s.inc(stage, t))

                def square_first(t):
                    act.wait_ge(x_in[t].sem, 16)
                    act.wait_ge(x_ready.sem, l * NT + (t + 1))
                    square("ss1", t)

                for t in range(3):
                    square_first(t)

                def evacuate(name, dst):
                    for t in range(NT):
                        u = f"S{t % 2}"
                        act.wait_ge(*full[u].at("z", name, t))
                        if name in "kq":
                            if t >= 2:
                                act.wait_ge(*dve_s.at("ss" + name, t - 2))
                            elif name == "q":
                                act.wait_ge(*dve_s.at("ssk", NT - 1))
                            nc.scalar.activation(sqj[:, t % 2, :], bank(u), ACT.Square).then_inc(*act_s.inc("sq", name, t))
                            nc.scalar.copy(dst[:, t, :], bank(u)).then_inc(*read[u].inc("z", name, t))
                            if name == "k" and t + 3 < NT:
                                square_first(t + 3)
                        else:
                            nc.scalar.copy(dst[:, t, :], bank(u)).then_inc(*read[u].inc("z", name, t))

                evacuate("k", kva)
                evacuate("v", v)
                evacuate("q", qz)
                for t in range(NT):
                    act.wait_ge(*full[f"T{t % 2}"].at("kT", t))
                    nc.scalar.copy(kT[:, :, t * P:(t + 1) * P], bank(f"T{t % 2}").rearrange("p (h t) -> p h t", h=H)).then_inc(*read[f"T{t % 2}"].inc("kT", t))
                act.wait_ge(*dve_s.at("ssq", NT - 1))

                def large(name, j):
                    act.wait_ge(*full["F"].at(name, j))
                    if name == "u":
                        nc.scalar.activation(catT[:, j, 0:TP * P], bank("F"), ACT.Gelu_apprx_tanh).then_inc(*read["F"].inc(name, j))
                        return
                    if name == "us":
                        nc.scalar.activation(catT[:, 0:4, TP * P:TOK], bank("F").rearrange("p (m t) -> p m t", m=4), ACT.Gelu_apprx_tanh
                                             ).then_inc(*read["F"].inc(name, j))
                        return
                    if j == 0:
                        act.wait_ge(*k_stored.at("k"))
                    nc.scalar.activation(kva[:, j, :], bank("F"), ACT.Gelu_apprx_tanh).then_inc(*read["F"].inc(name, j))
                    act.wait_ge(*read["F"].at(name, j))
                    if j >= 2:
                        act.wait_ge(*act_s.at("ssa", j - 2))
                    nc.scalar.activation(sqj[:, j % 2, :], kva[:, j, :], ACT.Square, accum_out=stat["ssa"][:, j:j + 1]).then_inc(*act_s.inc("ssa", j))

                large("va", 0)
                large("va", 1)
                act.wait_ge(*par_in.at("par"))
                for t in range(NT):
                    act.wait_ge(*full[f"T{t % 2}"].at("qT", t))
                    nc.scalar.mul(qT[:, :, t * P:(t + 1) * P], bank(f"T{t % 2}").rearrange("p (h t) -> p h t", h=H), par[:, PAR["qn"]]).then_inc(*read[f"T{t % 2}"].inc("qT", t))
                act.wait_ge(*dve_s.at("lamdot"))
                nc.scalar.activation(stat["lam"][:, 0:2], stat["lam"][:, 0:2], ACT.Exp).then_inc(*act_s.inc("lamexp"))

                def probs(n):
                    i, h = ATT[n]
                    act.wait_ge(*dve_s.at("nb", n))
                    if n >= 2:
                        act.wait_ge(*full[f"T{n % 2}"].at("aT", n - 2))
                    for m in range(2):
                        c = 2 * (n % 4) + m
                        ins = nc.scalar.activation(e_sb[:, n % 2, m, 0:(i + 1) * P], bank(f"S{n % 2}", m)[:, 0:(i + 1) * P], ACT.Exp,
                                                   bias=stat["nb"][:, c:c + 1], scale=SCALE,
                                                   accum_out=stat["sm"][:, c:c + 1])
                    ins.then_inc(*read[f"S{n % 2}"].inc("s", n))

                def probs_turned(n):
                    i, h = ATT[n]
                    u = f"T{n % 2}"
                    act.wait_ge(*full[u].at("aT", n))
                    nc.scalar.copy(aT[:, n % 2, 0:i + 1, :], bank(u)[:, 0:(i + 1) * P].rearrange("p (j q) -> p j q", q=P)).then_inc(*read[u].inc("aT", n))

                def sample_probs(g):
                    act.wait_ge(*dve_s.at("nbs", g))
                    nc.scalar.activation(es[:, g % 2, :], bank("F")[:, 0:320], ACT.Exp, bias=stat["nbs"][:, g:g + 1], scale=SCALE,
                                         accum_out=stat["sms"][:, g:g + 1]).then_inc(*read["F"].inc("ss", g))

                def sample_values(g, u):
                    act.wait_ge(*full[u].at("so", g))
                    nc.scalar.copy(oT[:, :, 2 * NS * g:2 * NS * (g + 1)], bank(u)[:, 0:H * 2 * NS].rearrange("p (h t) -> p h t", h=H)).then_inc(*read[u].inc("so", g))

                for n in range(len(ATT) + 2):
                    if n < len(ATT):
                        probs(n)
                    if n >= 2:
                        probs_turned(n - 2)
                    for name, j in LARGE.get(n, []):
                        large(name, j)
                    for name, j in SMALL.get(n, []):
                        if name == "ss":
                            sample_probs(j)
                        if name == "so":
                            sample_values(j, spare_turn(n))

                for t in range(NT):
                    for n in range(2):
                        act.wait_ge(*read[f"S{n}"].at("y", n, t))
                    square("ss2", t)
                    if t:
                        store_rows(t - 1)
                store_rows(NT - 1)
                act.wait_ge(*full["F"].at("logitsT"))
                nc.scalar.copy(o_sb[0:NR, 0, :], bank("F")[0:NR, :]).then_inc(*read["F"].inc("logitsT"))
                act.wait_ge(*dve_s.at("lgsub"))
                nc.scalar.activation(lg[:, :, :], lg[:, :, :], ACT.Exp).then_inc(*act_s.inc("lgexp"))
                def silu(b, key):
                    act.wait_ge(*full[f"S{b}"].at("gu", *key))
                    nc.scalar.activation(sil[:, b, :], bank(f"S{b}")[:, 0:DE], ACT.Silu).then_inc(*act_s.inc("sil", *key))

                def act_turned(b, key):
                    act.wait_ge(*full["J"].at("actT", *key))
                    nc.scalar.copy(actT[:, b, :, :], bank("J")[:, 0:2 * P].rearrange("p (f t) -> p f t", f=2)).then_inc(*read["J"].inc("actT", *key))

                def result(b, key, reused):
                    act.wait_ge(*full["O"].at("down", *key))
                    if reused:
                        act.wait_ge(*y_out[b].at("y", "m", E - 2 + b if key[0] in "ex" else key[1] - 2))
                    nc.scalar.copy(y_sb[:, b, :], ps[:, 6:8, :].rearrange("p a n -> p (a n)")).then_inc(*read["O"].inc("down", *key))

                for n in range(E + 1):
                    if n >= 1:
                        act_turned((n - 1) % 2, ("m", n - 1))
                    if n < E:
                        silu(n % 2, ("m", n))
                    if n >= 1:
                        result((n - 1) % 2, ("m", n - 1), n >= 3)
                n_extra = extra_slots(act, "act")

                def slot(key, b, number, q):
                    silu(b, (key, b))
                    act_turned(b, (key, b))
                    result(b, (key, b), True)
                    act.reg_add(scattered[b], scattered[b], 16)
                    act.wait_ge(y_outx[b].sem, act.snap(scattered[b]))
                    act.sem_inc(passed["act"], 1)

                extras(act, n_extra, slot)
                for t in range(NT):
                    n = NROW if t == TP else P
                    if t == 0:
                        act.wait_ge(*full["O"].at("down", "x", 1))
                        for b in range(2):
                            act.wait_ge(*y_out[b].at("y", "m", E - 2 + b))
                    if t == TP:
                        act.wait_ge(x_ready.sem, l * NT + (NT + t - 3))
                    for a in range(2):
                        act.dma_start(both[t % 4][0:n, a, :], y_rows[a * TOK + t * P:a * TOK + t * P + n, :]).then_inc(*y_in[t % 4].inc("y", t, by=16))

        @block.vector
        def _(dve):
            vec = nc.vector

            def link(ins):
                ins.then_inc(*dve_c.inc())
                dve.wait_ge(dve_c.sem, dve_c.now())

            vec.memset(x[NROW:P, TP, :], 0.0)
            vec.memset(oT[:, :, :], 0.0)
            dve.wait_ge(c32_in.sem, 16)
            dve.wait_ge(c16_in.sem, 16)
            vec.tensor_copy(c16[:, :], cat_cols[:, 0:NC16]).then_inc(*dve_s.inc("init"))
            rows = c32[:, C_ROWS].rearrange("p (t c) -> p t c", c=4)
            vec.tensor_copy(rows_of[:, :, :, :], rows.unsqueeze(2).to_broadcast([P, NT, E, 4]))
            vec.tensor_copy(rows_ofx[:, :, :, :], rows.unsqueeze(1).to_broadcast([P, EXTRA, NT, 4]))

            def norm_tile(stage, stage_r, gain):
                def scaled(t):
                    if stage == "h1":
                        dve.wait_ge(x_in[t].sem, 16)
                    dve.wait_ge(*pool_c.at(stage_r, t))
                    vec.tensor_scalar(hn2[:, t, :] if stage == "h2" else hn[:, t % 2, :], x[:, t, :], stat["rs"][:, t:t + 1], None, ALU.mult).then_inc(*dve_s.inc("hn" + stage[1], t))

                def turned(t):
                    for hf in range(2):
                        dve.wait_ge(*full[f"T{hf}"].at(stage, t, hf))
                        g = par[:, PAR[gain]][:, hf * HALF:(hf + 1) * HALF].unsqueeze(2).to_broadcast([P, HALF, P])
                        vec.tensor_tensor(hT[:, hf * HALF:(hf + 1) * HALF, t * P:(t + 1) * P],
                                          bank(f"T{hf}").rearrange("p (j t) -> p j t", j=HALF), g, ALU.mult).then_inc(*read[f"T{hf}"].inc(stage, t, hf))

                return scaled, turned

            def norm_rows(stage, stage_r, gain):
                scaled, turned = norm_tile(stage, stage_r, gain)
                for t in range(NT + 1):
                    if t < NT:
                        scaled(t)
                    if t >= 1:
                        turned(t - 1)

            def groups(ap, n, w):
                return ap.rearrange("p (n w) -> p n w", n=n)

            def wide(ap, n, w):
                return ap.unsqueeze(2).to_broadcast([P, n, w])

            def across(ap, n, w):
                return ap.unsqueeze(1).to_broadcast([P, n, w])

            with turns(dve, "layer"):
                dve.wait_ge(*par_in.at("par"))
                norm_rows("h1", "rs1", "g1")
                dve.wait_ge(*ws_in.at("ws"))
                vec.tensor_tensor(ws[:, :, :], ws[:, :, :], across(c32[:, C_CAUSAL], HA, P), ALU.mult).then_inc(*dve_s.inc("ws"))
                lam = par[:, PAR["lam"]]
                for i in range(2):
                    link(vec.tensor_tensor(tmp[:, i * DK:(i + 1) * DK], lam[:, 2 * i * DK:(2 * i + 1) * DK], lam[:, (2 * i + 1) * DK:(2 * i + 2) * DK], ALU.mult))
                vec.tensor_reduce(stat["lam"][:, 0:2], groups(tmp[:, 0:2 * DK], 2, DK), AX.X, ALU.add).then_inc(*dve_s.inc("lamdot"))
                link(vec.memset(qS[:, :, :, :], 0.0))

                def sums(name, t):
                    dve.wait_ge(*act_s.at("sq", name, t))
                    if name == "q":
                        dve.wait_ge(dve_c.sem, dve_c.now())
                    vec.tensor_reduce(stat["ssk"][:, 8 * t:8 * t + 8], groups(sqj[:, t % 2, :], 8, DK), AX.X, ALU.add).then_inc(*dve_s.inc("ss" + name, t))

                for t in range(NT):
                    sums("k", t)
                for t in range(NT):
                    dve.wait_ge(*pool_c.at("rsk", t))
                    dve.wait_ge(*read[f"S{t % 2}"].at("z", "k", t))
                    z = groups(kva[:, t, :], 8, DK)
                    link(vec.tensor_tensor(z, z, wide(stat["rsk"][:, 8 * t:8 * t + 8], 8, DK), ALU.mult))
                    vec.tensor_tensor(z, z, across(par[:, PAR["kn"]], 8, DK), ALU.mult).then_inc(*dve_s.inc("k", t))
                for t in range(NT):
                    sums("q", t)
                for t in range(NT):
                    dve.wait_ge(*pool_c.at("rsq", t))
                    dve.wait_ge(*read[f"S{t % 2}"].at("z", "q", t))
                    z = groups(qz[:, t, :], 8, DK)
                    vec.tensor_tensor(z, z, wide(stat["rsk"][:, 8 * t:8 * t + 8], 8, DK), ALU.mult).then_inc(*dve_s.inc("q", t))
                dve.wait_ge(*read["T0"].at("qT", TP))
                for h in range(H):
                    for m in range(2):
                        r = slice(m * DK, (m + 1) * DK)
                        c = h * 16 + m * NS
                        ins = vec.tensor_copy(qS[r, :, h, c:c + NS], qT[r, h, TP * P:TP * P + NROW].rearrange("p (b t) -> p b t", b=NB))
                ins.then_inc(*dve_s.inc("qS"))
                dve.wait_ge(*act_s.at("lamexp"))
                link(vec.tensor_tensor(stat["lam"][:, 2:3], stat["lam"][:, 1:2], stat["lam"][:, 0:1], ALU.subtract))
                link(vec.tensor_tensor(stat["lam"][:, 3:4], stat["lam"][:, 2:3], par[:, PAR["init"]], ALU.subtract))
                neglam = stat["lam"][:, 3:4]
                link(vec.scalar_tensor_tensor(stat["rowf"], c32[:, C_MAP1], neglam, c32[:, C_MAP0], ALU.mult, ALU.add))

                def scale_va(t):
                    dve.wait_ge(*pool_c.at("rsa", t))
                    vec.scalar_tensor_tensor(kva[:, t, :], kva[:, t, :], stat["rsa"][:, t:t + 1], par[:, PAR["av"]],
                                             ALU.mult, ALU.mult).then_inc(*dve_s.inc("va", t))

                def sample_mix():
                    dve.wait_ge(*full["F"].at("wsS", 0))
                    vec.tensor_tensor(ws[:, :, :].rearrange("p h (b t) -> p h b t", t=NS),
                                      bank("F")[:, 0:HA * NS].rearrange("p (h t) -> p h t", h=HA).unsqueeze(2).to_broadcast([P, HA, 16, NS]),
                                      c32[:, C_BATCH].rearrange("p (b t) -> p b t", t=NS).unsqueeze(1).to_broadcast([P, HA, 16, NS]),
                                      ALU.mult).then_inc(*read["F"].inc("wsS", 0))

                def mix(t):
                    dve.wait_ge(*full["F"].at("mix", t))
                    bs = par[:, PAR["bs"]].rearrange("p (c t) -> p c t", c=4)
                    s, o = bank("F"), tmp[:, :]
                    if t < TP:
                        s, o = (a.rearrange("p (c t) -> p c t", c=4) for a in (s, o))
                    else:
                        s, o = (a.rearrange("p (c b t) -> p c b t", c=4, t=NS) for a in (s, o))
                        bs = bs[:, :, 0:NS].unsqueeze(2).to_broadcast([P, 4, 16, NS])
                    dve.wait_ge(dve_c.sem, dve_c.now())
                    if t:
                        dve.wait_ge(*dve_s.at("mix", t - 1))
                    vec.tensor_tensor(o, s, bs, ALU.add).then_inc(*read["F"].inc("mix", t))
                    dve.wait_ge(*read["F"].at("mix", t))
                    vec.tensor_tensor(catT[:, 0:4, t * P:(t + 1) * P], tmp[:, :].rearrange("p (c t) -> p c t", c=4),
                                      catT[:, 0:4, t * P:(t + 1) * P], ALU.mult).then_inc(*dve_s.inc("mix", t))

                def biggest(n):
                    i, h = ATT[n]
                    c = 2 * (n % 4)
                    dve.wait_ge(*full[f"S{n % 2}"].at("s", n))
                    b0 = FIRST[f"S{n % 2}"]
                    link(vec.tensor_reduce(stat["mx"][:, c:c + 2], ps[:, b0:b0 + 2, 0:(i + 1) * P], AX.X, ALU.max))
                    vec.tensor_scalar(stat["nb"][:, c:c + 2], stat["mx"][:, c:c + 2], -SCALE, None, ALU.mult).then_inc(*dve_s.inc("nb", n))

                def combine(n):
                    i, h = ATT[n]
                    c = 2 * (n % 4)
                    dve.wait_ge(*read[f"S{n % 2}"].at("s", n))
                    link(vec.reciprocal(stat["co"][:, 0:2], stat["sm"][:, c:c + 2]))
                    r0 = stat["r0"][:, 4 * (i % 2) + h:4 * (i % 2) + h + 1]
                    vec.tensor_copy(r0, stat["co"][:, 0:1])
                    link(vec.scalar_tensor_tensor(stat["co"][:, 2:3], stat["co"][:, 1:2], neglam, stat["sm"][:, c:c + 1], ALU.mult, ALU.mult))
                    vec.scalar_tensor_tensor(e_sb[:, n % 2, 0, 0:(i + 1) * P], e_sb[:, n % 2, 1, 0:(i + 1) * P], stat["co"][:, 2:3],
                                             e_sb[:, n % 2, 0, 0:(i + 1) * P], ALU.mult, ALU.add).then_inc(*dve_s.inc("a", n))

                def head_norm(t):
                    dve.wait_ge(*full["O"].at("o", t))
                    o = o_sb[:, t % 2, :]
                    if t < TP:
                        dve.wait_ge(dve_c.sem, dve_c.now())
                        ins = vec.tensor_tensor(groups(o, H, DV), groups(bank("O"), H, DV), wide(stat["r0"][:, 4 * (t % 2):4 * (t % 2) + 4], H, DV), ALU.mult)
                    else:
                        ins = vec.tensor_copy(o, bank("O"))
                    ins.then_inc(*read["O"].inc("o", t))
                    dve.wait_ge(*read["O"].at("o", t))
                    last_mix = [j for m, works in SMALL.items() for name, j in works if name == "mix" and m <= 4 * t + 6]
                    if last_mix:
                        dve.wait_ge(*dve_s.at("mix", last_mix[-1]))
                    link(vec.tensor_tensor(tmp[:, :], o, o, ALU.mult))
                    vec.tensor_reduce(stat["sso"][:, 4 * t:4 * t + 4], groups(tmp[:, :], H, DV), AX.X, ALU.add).then_inc(*dve_s.inc("sso", t))

                def head_scale(t):
                    o = groups(o_sb[:, t % 2, :], H, DV)
                    dve.wait_ge(*pool_c.at("rso", t))
                    vec.tensor_tensor(o, o, wide(stat["rso"][:, 4 * t:4 * t + 4], H, DV), ALU.mult).then_inc(*dve_s.inc("o", t))

                def head_turned(t):
                    u = OT[t]
                    dve.wait_ge(*full[u].at("oT", t))
                    vec.tensor_scalar(catT[:, 4:8, t * P:(t + 1) * P], groups(bank(u), H, P), par[:, PAR["on"]], par[:, PAR["keep"]],
                                      ALU.mult, ALU.mult).then_inc(*read[u].inc("oT", t))

                def sample_biggest(g):
                    dve.wait_ge(*full["F"].at("ss", g))
                    link(vec.tensor_reduce(stat["mxs"][:, g:g + 1], bank("F")[:, 0:320], AX.X, ALU.max))
                    vec.tensor_scalar(stat["nbs"][:, g:g + 1], stat["mxs"][:, g:g + 1], -SCALE, None, ALU.mult).then_inc(*dve_s.inc("nbs", g))

                def sample_combine(g, u):
                    dve.wait_ge(*read["F"].at("ss", g))
                    link(vec.reciprocal(stat["mxs"][:, g:g + 1], stat["sms"][:, g:g + 1]))
                    vec.tensor_scalar(es[:, g % 2, :], es[:, g % 2, :], stat["mxs"][:, g:g + 1], stat["rowf"], ALU.mult, ALU.mult).then_inc(*dve_s.inc("ps", g))
                    dve.wait_ge(*full[u].at("pT", g))
                    for rows, a, b in ((P, 0, PAGES), (64, PAGES, PAGES + 1)):
                        pt = bank(u)[0:rows, a * P:b * P].rearrange("p (j r m t) -> p j r m t", j=b - a, m=2, t=NS)
                        for j in range(b - a):
                            ins = vec.tensor_reduce(aTs[0:rows, g % 2, a + j, :].rearrange("p (r t) -> p r t", t=NS),
                                                    pt[:, j, :, :, :].rearrange("p r m t -> p r t m"), AX.X, ALU.add)
                            if j == b - a - 1 and a == PAGES:
                                ins.then_inc(*read[u].inc("pT", g))
                            else:
                                link(ins)

                def add_out(n, t):
                    u = f"S{n}"
                    dve.wait_ge(*full[u].at("y", n, t))
                    cols = x[:, t, n * W:(n + 1) * W]
                    vec.tensor_tensor(cols, cols, bank(u), ALU.add).then_inc(*read[u].inc("y", n, t))

                VA_AT = {0: [0, 1], 1: [2], 2: [3], 3: [4]}
                for n in range(len(ATT) + 1):
                    if n < len(ATT):
                        biggest(n)
                    if n >= 10 and n % 4 == 2:
                        head_turned((n - 10) // 4)
                    if n >= 7 and n % 4 == 3:
                        head_norm((n - 7) // 4)
                    if n >= 1:
                        combine(n - 1)
                    if n >= 8 and n % 4 == 0:
                        head_scale((n - 8) // 4)
                    for t in VA_AT.get(n, []):
                        scale_va(t)
                    for name, j in SMALL.get(n, []):
                        if name == "mix":
                            mix(j)
                        elif name == "wsS":
                            sample_mix()
                        elif name == "ss":
                            sample_biggest(j)
                        elif name == "pT":
                            sample_combine(j, spare_turn(n))
                head_turned(2)
                head_norm(3)
                head_scale(3)
                scaled, turned = norm_tile("h2", "rs2", "g2")
                for t in range(NT + 1):
                    if t < NT:
                        add_out(0, t)
                    if t >= 1:
                        scaled(t - 1)
                    if t < NT:
                        add_out(1, t)
                    if t >= 1:
                        turned(t - 1)
                    if t == TP - 2:
                        head_turned(TP - 1)
                        head_norm(TP)
                        head_scale(TP)
                    if t == TP - 1:
                        head_turned(TP)

                dve.wait_ge(*full["O"].at("logits"))
                vec.tensor_copy(lg[:, :, :], bank("O")[:, 0:NT * 20].rearrange("p (t n) -> p t n", t=NT)).then_inc(*read["O"].inc("logits"))
                dve.wait_ge(*read["O"].at("logits"))
                lgg, lge = lg[:, :, 0:G], lg[:, :, G:20].rearrange("p t (g j) -> p t g j", g=G)

                sets = NT * (1 + G)
                A, B = cmpA[:, 0:sets * EG, :], cmpB[:, 0:sets * EG, :]
                A4, B4 = (a.rearrange("p (n j) i -> p n j i", j=EG) for a in (A, B))
                cols = lg[:, :, :].rearrange("p t (s j) -> p (t s) j", j=EG)
                vi = cols.unsqueeze(2).to_broadcast([P, sets, EG, EG])
                vj = cols.unsqueeze(3).to_broadcast([P, sets, EG, EG])
                vec.tensor_tensor(A4, vi, vj, ALU.is_gt)
                link(vec.tensor_tensor(B4, vi, vj, ALU.is_equal))
                first = c32[:, C_FIRST][:, 0:EG * EG].rearrange("p (j i) -> p j i", j=EG).unsqueeze(1).to_broadcast([P, sets, EG, EG])
                link(vec.tensor_tensor(B4, B4, first, ALU.mult))
                link(vec.tensor_tensor(A, A, B, ALU.add))
                link(vec.tensor_reduce(stat["rank"], A, AX.X, ALU.add))
                ranks = stat["rank"].rearrange("p (t s j) -> p t s j", t=NT, j=EG)
                link(vec.tensor_scalar(stat["goh"].rearrange("p (t g) -> p t g", t=NT), ranks[:, :, 0, :], 0.5, None, ALU.is_lt))
                ex = stat["ex"].rearrange("p (n j) -> p n j", j=EG)
                flat = placed[:, :, :]
                selA, selB, R, win, work = (flat[:, i, :] for i in range(5))
                goh4 = wide(stat["goh"], NT * G, EG)
                for sel, op, c in ((selA, ALU.is_lt, 0.5), (selB, ALU.is_equal, 1.0)):
                    link(vec.scalar_tensor_tensor(sel.rearrange("p (t g j) -> p t g j", t=NT, j=EG), ranks[:, :, 1:1 + G, :], c,
                                                  goh4.rearrange("p (t g) j -> p t g j", t=NT), op, ALU.mult))
                link(vec.memset(placed[NROW:P, 0:2, TP * E:NT * E], 0.0))
                vec.tensor_tensor(M[:, :], selA, selB, ALU.add).then_inc(*dve_s.inc("M"))
                vec.tensor_copy(rows_of[:, :, :, 3], selB.rearrange("p (t e) -> p t e", t=NT))
                dve.wait_ge(*full["I"].at("ranks"))
                vec.tensor_copy(stat["cnt"], bank("I")[:, NT * E:(NT + 1) * E])
                vec.scalar_tensor_tensor(R, bank("I")[:, 0:NT * E], 1.0, M[:, :], ALU.add, ALU.mult).then_inc(*read["I"].inc("ranks"))
                dve.wait_ge(*read["I"].at("ranks"))
                iota = c32[:, C_IOTA]

                def one_hot(s, places, label=None):
                    ins = vec.tensor_tensor(onehot[:, s % 4, :, :], places.unsqueeze(2).to_broadcast([P, NT, P]), across(iota, NT, P), ALU.is_equal)
                    if label is not None:
                        ins.then_inc(*dve_s.inc("onehot", label))
                    return ins

                def index(g):
                    dve.wait_ge(*full["I"].at("idx", g))
                    n = len(GROUPS[g])
                    cols = bank("I")[:, 0:4 * n].rearrange("p (s c) -> p s c", c=4)
                    s0 = GROUPS[g][0]
                    link(vec.tensor_reduce(work[:, 0:n], cols[:, :, 0:3], AX.X, ALU.add))
                    vec.scalar_tensor_tensor(work[:, 4:4 + n], cols[:, :, 3], float(TOK), work[:, 0:n], ALU.mult, ALU.add).then_inc(*read["I"].inc("idx", g))
                    dve.wait_ge(*read["I"].at("idx", g))
                    vec.tensor_scalar(igat[:, s0:s0 + n], work[:, 0:n], SKIP, None, ALU.add)
                    vec.tensor_scalar(isca[:, s0:s0 + n], work[:, 4:4 + n], SKIP, None, ALU.add).then_inc(*dve_s.inc("idx", g))
                    dve.wait_ge(*dve_s.at("idx", g))

                def main_group(g):
                    for s in GROUPS[g]:
                        one_hot(s, R.rearrange("p (t e) -> p t e", t=NT)[:, :, s], g if s == GROUPS[g][-1] else None)
                    index(g)

                def extra_group(g):
                    for s in GROUPS[g]:
                        link(vec.scalar_tensor_tensor(work, win, 0.5, win, ALU.is_gt, ALU.mult))
                        link(vec.scalar_tensor_tensor(work, work, P + 0.5, work, ALU.is_lt, ALU.mult))
                        link(vec.tensor_reduce(stat["vt"], work.rearrange("p (t e) -> p t e", t=NT), AX.X, ALU.add))
                        link(vec.scalar_tensor_tensor(work, work, 0.5, selB, ALU.is_gt, ALU.mult))
                        link(vec.tensor_reduce(stat["rank"][:, 0:NT], work.rearrange("p (t e) -> p t e", t=NT), AX.X, ALU.add))
                        link(vec.tensor_copy(rows_ofx[:, s - E, :, 3], stat["rank"][:, 0:NT]))
                        link(vec.tensor_scalar(win, win, float(P), None, ALU.subtract))
                        if s != GROUPS[g][-1]:
                            link(one_hot(s, stat["vt"]))
                        else:
                            one_hot(s, stat["vt"], g)
                    index(g)

                def logits_down():
                    link(vec.tensor_copy(stat["ex"].rearrange("p (t n) -> p t n", t=NT), lg[:, :, G:NR]))
                    link(vec.tensor_reduce(stat["gm"], lgg, AX.X, ALU.max))
                    link(vec.tensor_tensor(lgg, lgg, wide(stat["gm"], NT, G), ALU.subtract))
                    link(vec.tensor_reduce(stat["em"], ex, AX.X, ALU.max))
                    link(vec.tensor_tensor(ex, ex, wide(stat["em"], NT * G, EG), ALU.subtract))
                    vec.tensor_copy(lg[:, :, G:20], stat["ex"].rearrange("p (t n) -> p t n", t=NT)).then_inc(*dve_s.inc("lgsub"))

                def gate_values():
                    dve.wait_ge(*act_s.at("lgexp"))
                    link(vec.tensor_reduce(stat["gs"], lgg, AX.X, ALU.add))
                    link(vec.reciprocal(stat["gw"], stat["gs"]))
                    link(vec.tensor_copy(stat["ex"].rearrange("p (t n) -> p t n", t=NT), lg[:, :, G:20]))
                    link(vec.tensor_tensor(stat["ex"], stat["ex"], M[:, :], ALU.mult))
                    link(vec.tensor_reduce(stat["es"], ex, AX.X, ALU.add))
                    link(vec.scalar_tensor_tensor(stat["es"], stat["goh"], -1.0, stat["es"], ALU.mult, ALU.add))
                    link(vec.tensor_scalar(stat["es"], stat["es"], 1.0, 1e-30, ALU.add, ALU.max))
                    link(vec.reciprocal(stat["em"], stat["es"]))
                    em = stat["em"].rearrange("p (t g) -> p t g", t=NT)
                    link(vec.tensor_tensor(em, em, wide(stat["gw"], NT, G), ALU.mult))
                    g80 = gates[:, :, :].rearrange("p t e -> p (t e)")
                    link(vec.tensor_tensor(groups(g80, NT * G, EG), ex, wide(stat["em"], NT * G, EG), ALU.mult))
                    for a, sel in enumerate((selA, selB)):
                        link(vec.tensor_tensor(work, g80, sel, ALU.mult))
                        link(vec.tensor_reduce(stat["gAB"][:, a * NT:(a + 1) * NT], work.rearrange("p (t e) -> p t e", t=NT), AX.X, ALU.add))

                def extra_plan():
                    cnt, nov, ovb = stat["cnt"], stat["nov"], stat["ovb"]
                    link(vec.tensor_scalar(nov, cnt, P + 0.5, None, ALU.is_gt))
                    for c in range(2, NT):
                        link(vec.scalar_tensor_tensor(nov, cnt, c * P + 0.5, nov, ALU.is_gt, ALU.add))
                    pairs = cmpA.rearrange("p n j -> p (n j)")[:, 0:E * E].rearrange("p (a b) -> p a b", a=E)
                    link(vec.tensor_tensor(pairs, nov.unsqueeze(1).to_broadcast([P, E, E]), groups(c32[:, C_TRI], E, E), ALU.mult))
                    link(vec.tensor_reduce(ovb, pairs, AX.X, ALU.add))
                    link(vec.tensor_reduce(stat["vt"][:, 0:1], nov, AX.X, ALU.add))
                    vec.tensor_copy(flags[:, 0:1], stat["vt"][:, 0:1])
                    own = cmpA.rearrange("p n j -> p (n j)")[:, 0:EXTRA * E].rearrange("p (s e) -> p s e", s=EXTRA)
                    end = cmpB.rearrange("p n j -> p (n j)")[:, 0:EXTRA * E].rearrange("p (s e) -> p s e", s=EXTRA)
                    slots = c32[:, C_SLOTS][:, 0:EXTRA].unsqueeze(2).to_broadcast([P, EXTRA, E])
                    names = c32[:, C_SLOTS][:, 8:8 + E].unsqueeze(1).to_broadcast([P, EXTRA, E])
                    link(vec.tensor_tensor(own, ovb.unsqueeze(1).to_broadcast([P, EXTRA, E]), slots, ALU.is_le))
                    link(vec.tensor_tensor(nov, nov, ovb, ALU.add))
                    link(vec.tensor_tensor(end, nov.unsqueeze(1).to_broadcast([P, EXTRA, E]), slots, ALU.is_gt))
                    link(vec.tensor_tensor(own, own, end, ALU.mult))
                    link(vec.tensor_tensor(own, own, names, ALU.mult))
                    link(vec.tensor_reduce(work[:, 0:EXTRA], own, AX.X, ALU.add))
                    vec.tensor_copy(flags[:, 1:1 + EXTRA], work[:, 0:EXTRA]).then_inc(*dve_s.inc("flags"))
                    dve.wait_ge(*dve_s.at("flags"))
                    link(vec.tensor_scalar(ovb, ovb, float(P), float(P), ALU.mult, ALU.subtract))
                    w3, r3 = (a.rearrange("p (t e) -> p t e", t=NT) for a in (win, R))
                    link(vec.tensor_tensor(w3, r3, across(ovb, NT, E), ALU.add))
                    link(vec.scalar_tensor_tensor(win, R, P + 0.5, win, ALU.is_gt, ALU.mult))

                def in_turned(b, key):
                    for hf in range(2):
                        dve.wait_ge(*full[f"T{hf}"].at("tr", *key, hf))
                        g = par[:, PAR["g2"]][:, hf * HALF:(hf + 1) * HALF].unsqueeze(2).to_broadcast([P, HALF, P])
                        vec.tensor_tensor(hsT[:, b, hf * HALF:(hf + 1) * HALF, :], bank(f"T{hf}").rearrange("p (j t) -> p j t", j=HALF),
                                          g, ALU.mult).then_inc(*read[f"T{hf}"].inc("tr", *key, hf))

                def gated(b, key):
                    dve.wait_ge(*act_s.at("sil", *key))
                    vec.tensor_tensor(act_sb[:, b, :], sil[:, b, :], bank(f"S{b}")[:, DE:2 * DE], ALU.mult).then_inc(*read[f"S{b}"].inc("gu", *key))

                main_group(0)
                logits_down()
                main_group(1)
                in_turned(0, ("m", 0))
                for n in range(E):
                    if n in INDEX_AT:
                        g = INDEX_AT[n]
                        (main_group if g < 5 else extra_group)(g)
                    if n == 3:
                        gate_values()
                    if n == 4:
                        extra_plan()
                    if n + 1 < E:
                        in_turned((n + 1) % 2, ("m", n + 1))
                    gated(n % 2, ("m", n))
                n_extra = extra_slots(dve, "dve")

                def slot(key, b, number, q):
                    in_turned(b, (key, b))
                    gated(b, (key, b))

                extras(dve, n_extra, slot)
                for t in range(NT):
                    n = NROW if t == TP else P
                    dve.wait_ge(*y_in[t % 4].at("y", t))
                    for a in range(2):
                        ins = vec.scalar_tensor_tensor(x[0:n, t, :], both[t % 4][0:n, a, :], stat["gAB"][0:n, a * NT + t:a * NT + t + 1],
                                                       x[0:n, t, :], ALU.mult, ALU.add)
                        if a:
                            ins.then_inc(*x_ready.inc())
                        else:
                            link(ins)

        return totals


_SHAPES = [("yp", (4 * P, D)), ("ys", (NROW, D)), ("kp", (L, TP, P, W)), ("vp", (L, TP, P, W)), ("ks", (L, NROW, W)),
           ("vs", (L, NROW, W)), ("cvs", (L, NROW, W))]


def layout(a):
    f = np.float32

    def blocks(w):
        k, n = w.shape
        return w.reshape(k // (HALF * P), HALF, P, n // W, W).transpose(3, 0, 2, 1, 4).reshape(-1, P, PIECE)

    w_in, w_out = a["w_in"], a["w_out"]
    w = np.empty((L * W_LAYER, P, PIECE), f)
    for l in range(L):
        parts = w[l * W_LAYER:(l + 1) * W_LAYER]
        cols = blocks(w_in[l])
        for i, c in enumerate((3, 4, 2, 1, 0)):
            parts[2 * i:2 * i + 2] = cols[2 * c:2 * c + 2]
        parts[N_IN:N_DENSE] = blocks(w_out[l])
        for e in range(E):
            at = N_DENSE + PER_EXPERT * e
            parts[at:at + 2] = blocks(np.concatenate([a["w_gate"][l, e], a["w_up"][l, e]], axis=1))
            parts[at + 2] = a["w_down"][l, e].reshape(2, P, D).transpose(1, 0, 2).reshape(P, 2 * D)
    par = np.zeros((L, P, NPAR), f)

    def put(name, value):
        par[:, :, PAR[name]] = value
    put("g1", a["norm1_g"].reshape(L, KD, P).transpose(0, 2, 1))
    put("g2", a["norm2_g"].reshape(L, KD, P).transpose(0, 2, 1))
    put("qn", np.concatenate([a["qn_g"], a["qn_g"]], axis=1)[:, :, None])
    put("on", a["b_onorm_g"][:, :, None])
    for l in range(L):
        init = 0.8 - 0.6 * math.exp(-0.3 * l)
        par[l, :, PAR["init"]] = init
        par[l, :, PAR["keep"]] = 1.0 - init
    put("kn", a["kn_g"][:, None, :])
    put("av", a["a_vnorm_g"][:, None, :])
    put("lam", np.concatenate([a["lam_q1"], a["lam_k1"], a["lam_q2"], a["lam_k2"]], axis=1)[:, None, :])
    bs = a["a_bs"].reshape(L, 4, 2, P).transpose(0, 2, 1, 3).reshape(L, 2, 4 * P)
    put("bs", np.repeat(bs, DHA, axis=1))
    router = np.concatenate([a["router_g"], a["router_e"]], axis=2)
    put("router", router.reshape(L, KD, P, 20).transpose(0, 2, 1, 3).reshape(L, P, KD * 20))
    c32 = np.zeros((P, NC32), f)
    r = np.arange(P)
    c32[:, C_ID] = np.eye(P)
    c32[:, C_CAUSAL] = r[:, None] <= r[None, :]
    c32[:, C_BATCH] = r[:, None] // NS == r[None, :] // NS
    c32[0:NS, C_SPREAD] = r[0:NS, None] == r[None, :] % NS
    j, i = np.divmod(np.arange(EG * EG), EG)
    c32[:, C_FIRST.start:C_FIRST.start + EG * EG] = i < j
    a16 = np.arange(E)
    c32[:, C_TRI] = (a16[None, :] < a16[:, None]).reshape(1, -1)
    c32[:, C_IOTA] = r[None, :] + 1
    rows = np.zeros((P, NT, 4))
    rows[:, :, 0], rows[:, :, 1], rows[:, :, 2] = r[:, None], P * np.arange(NT)[None, :], -SKIP
    c32[:, C_ROWS] = rows.reshape(P, -1)
    c32[:, C_SLOTS.start:C_SLOTS.start + EXTRA] = np.arange(EXTRA)
    c32[:, C_SLOTS.start + 8:C_SLOTS.start + 8 + E] = a16
    c32[:, C_MAP0] = (r[:, None] // NS) % 2 == 0
    c32[:, C_MAP1] = (r[:, None] // NS) % 2 == 1
    c16 = np.zeros((P, NC16), f)
    c16[:, B_ID] = np.eye(P)
    c16[:, B_CAUSAL] = np.where(r[None, :] <= r[:, None], 0.0, -1e30)
    c16[:, B_ONES] = 1.0
    c16[:, B_BEFORE] = r[:, None] < r[None, :]
    row, key = np.arange(64), np.arange(64)
    for b in range(NB):
        ok = (key[None, :] // NS == b) & (key[None, :] % NS <= row[:, None] % NS)
        c16[0:64, B_SAMPLE.start + b * 64:B_SAMPLE.start + (b + 1) * 64] = np.where(ok, 0.0, -1e30)
    return {
        "xp": a["x_prompt"].reshape(4 * P, D), "xs": a["x_sample"].reshape(NROW, D),
        "w": w, "par": par, "ws": a["a_ws"].transpose(0, 3, 1, 2),
        "ck": a["cache_k"].transpose(0, 1, 4, 3, 2).reshape(L * NPOOL, P, H, P),
        "cv": a["cache_v"].reshape(L * NPOOL, P, W),
        "pages": a["page_table"].reshape(1, -1).astype(np.int32), "c32": c32, "c16": c16,
    }


def build(nc, arrays, totals):
    d = {n: nc.dram_tensor(f"in_{n}", v.shape, mybir.dt.from_np(v.dtype), kind="ExternalInput").ap() for n, v in arrays.items()}
    for n, shape in _SHAPES:
        d[n] = nc.dram_tensor(f"out_{n}", shape, F32, kind="ExternalOutput").ap()
    program(nc, totals, d)


def kernel(**inputs):
    import concourse.bacc as bacc
    from concourse.bass_utils import run_bass_kernel_spmd
    arrays = {n: np.ascontiguousarray(v) for n, v in layout({n: np.asarray(v) for n, v in inputs.items()}).items()}
    totals = {}
    for _ in range(2):
        nc = bacc.Bacc("TRN2", target_bir_lowering=False, num_devices=1)
        build(nc, arrays, totals)
    r = run_bass_kernel_spmd(nc, [{f"in_{n}": v for n, v in arrays.items()}], core_ids=[0]).results[0]
    o = {n: r[f"out_{n}"] for n, _ in _SHAPES}
    return (o["yp"].reshape(1, 4 * P, D), o["ys"].reshape(NB, NS, D), o["kp"].reshape(L, 1, 4 * P, H, 2 * DK),
            o["vp"].reshape(L, 1, 4 * P, H, DV), o["ks"].reshape(L, NB, NS, H, 2 * DK), o["vs"].reshape(L, NB, NS, H, DV),
            o["cvs"].reshape(L, NB, NS, HA * DHA))
```
